# Optimizing a Trainium2 kernel written in Bass

```python
import math
import jax, jax.numpy as jnp
from jax import lax
import numpy as np

D_MODEL = 2048
BATCH = 1
SEQ = 256
DEPTH = 2

N_A = DEPTH // 2
N_B = DEPTH - N_A
SSM_WIDTH = D_MODEL
SSM_GROUP = 16
SSM_GROUPS = SSM_WIDTH // SSM_GROUP
SSM_STATE = 64
N_HEADS = 16
N_KV = 4
HPG = N_HEADS // N_KV
HEAD_DIM = D_MODEL // N_HEADS
ATT_WIDTH = N_HEADS * HEAD_DIM
N_BRANCH = 3
CMP_LEN = 32
CMP_STRIDE = 16
SEL_LEN = 64
SEL_TOPK = 16
WINDOW = 512
WIN_QBLOCK = 128
SEL_QCHUNK = 32
SEL_BONUS = 1e3
NEG = -1e30
EPS = 1e-6


def rmsnorm(x, g):
    xf = x.astype(jnp.float32)
    y = xf * lax.rsqrt(jnp.mean(xf * xf, axis=-1, keepdims=True) + EPS)
    return (y * g.astype(jnp.float32)).astype(x.dtype)

def modulate(h, shift, scale):
    return h * (1.0 + scale[:, None, :]) + shift[:, None, :]

def masked_softmax(s, mask):
    s = jnp.where(mask, s.astype(jnp.float32), NEG)
    p = jax.nn.softmax(s, axis=-1)
    return jnp.where(mask, p, 0.0)

def s5_discretize(lam_re, lam_im, log_step, b_re, b_im):
    dt = jnp.exp(log_step.astype(jnp.float32))[:, None]
    lr, li = lam_re.astype(jnp.float32), lam_im.astype(jnp.float32)
    mag = jnp.exp(lr * dt)
    a_re, a_im = mag * jnp.cos(li * dt), mag * jnp.sin(li * dt)
    den = lr * lr + li * li
    coef_re = ((a_re - 1.0) * lr + a_im * li) / den
    coef_im = (a_im * lr - (a_re - 1.0) * li) / den
    br, bi = b_re.astype(jnp.float32), b_im.astype(jnp.float32)
    bb_re = coef_re[..., None] * br - coef_im[..., None] * bi
    bb_im = coef_re[..., None] * bi + coef_im[..., None] * br
    return a_re, a_im, bb_re, bb_im

def _ssm_combine(left, right):
    ar_i, ai_i, br_i, bi_i = left
    ar_j, ai_j, br_j, bi_j = right
    return (ar_j * ar_i - ai_j * ai_i,
            ar_j * ai_i + ai_j * ar_i,
            ar_j * br_i - ai_j * bi_i + br_j,
            ar_j * bi_i + ai_j * br_i + bi_j)

def _scan_one(a_re, a_im, bu_re, bu_im):
    out = lax.associative_scan(_ssm_combine, (a_re, a_im, bu_re, bu_im), axis=0)
    return out[2], out[3]

def s5_mixer(h, w_in, lam_re, lam_im, log_step, b_re, b_im, c_re, c_im, d_skip, w_glu, b_glu, w_out):
    B_, L, _ = h.shape
    u, z = jnp.split(h @ w_in, 2, axis=-1)
    ug = u.reshape(B_, L, SSM_GROUPS, SSM_GROUP).astype(jnp.float32)
    a_re, a_im, bb_re, bb_im = s5_discretize(lam_re, lam_im, log_step, b_re, b_im)
    bu_re = jnp.einsum('blgc,gnc->blgn', ug, bb_re)
    bu_im = jnp.einsum('blgc,gnc->blgn', ug, bb_im)
    shp = (L, SSM_GROUPS, SSM_STATE)
    x_re, x_im = jax.vmap(_scan_one, in_axes=(None, None, 0, 0))(
        jnp.broadcast_to(a_re, shp), jnp.broadcast_to(a_im, shp), bu_re, bu_im)
    y = (jnp.einsum('blgn,gcn->blgc', x_re, c_re.astype(jnp.float32))
         - jnp.einsum('blgn,gcn->blgc', x_im, c_im.astype(jnp.float32)))
    y = y + d_skip.astype(jnp.float32).reshape(SSM_GROUPS, SSM_GROUP) * ug
    y = jax.nn.gelu(y.reshape(B_, L, SSM_WIDTH).astype(h.dtype))
    y = y * jax.nn.sigmoid(y @ w_glu + b_glu)
    return (y * jax.nn.silu(z)) @ w_out

def compress_blocks(t, blk_idx, pe, w1, b1, w2, b2):
    blocks = t[:, blk_idx] + pe[None, None, :, None, :]
    B_, n = blocks.shape[:2]
    flat = jnp.moveaxis(blocks, 3, 2).reshape(B_, n, N_KV, CMP_LEN * HEAD_DIM)
    return jax.nn.gelu(flat @ w1 + b1) @ w2 + b2

def nsa_shared_kv(h_kv, w_kv, cmp_pe, cmp_w1, cmp_b1, cmp_w2, cmp_b2):
    B_, L, _ = h_kv.shape
    kv = (h_kv @ w_kv).reshape(B_, L, 2 * N_BRANCH, N_KV, HEAD_DIM)
    n_cmp = (L - CMP_LEN) // CMP_STRIDE + 1
    blk_idx = np.arange(n_cmp)[:, None] * CMP_STRIDE + np.arange(CMP_LEN)[None, :]
    kc = compress_blocks(kv[:, :, 0], blk_idx, cmp_pe[0], cmp_w1[0], cmp_b1[0], cmp_w2[0], cmp_b2[0])
    vc = compress_blocks(kv[:, :, 1], blk_idx, cmp_pe[1], cmp_w1[1], cmp_b1[1], cmp_w2[1], cmp_b2[1])
    return kc, vc, kv[:, :, 2], kv[:, :, 3], kv[:, :, 4], kv[:, :, 5]

def cmp_attention(q, kc, vc, pos):
    n_cmp = kc.shape[1]
    s = jnp.einsum('blghd,bngd->bghln', q, kc)
    blk_end = jnp.arange(n_cmp) * CMP_STRIDE + CMP_LEN - 1
    mask = blk_end[None, :] <= pos[:, None]
    p = masked_softmax(s, mask)
    o = jnp.einsum('bghln,bngd->blghd', p.astype(vc.dtype), vc)
    return o, p.sum(axis=2)

def selection_overlap(n_cmp, n_slc):
    c0 = np.arange(n_cmp)[:, None] * CMP_STRIDE
    s0 = np.arange(n_slc)[None, :] * SEL_LEN
    ov = np.clip(np.minimum(c0 + CMP_LEN, s0 + SEL_LEN) - np.maximum(c0, s0), 0, None)
    return (ov / CMP_STRIDE).astype(np.float32)

def select_blocks(p_cmp, pos):
    n_cmp = p_cmp.shape[-1]
    n_slc = pos.shape[0] // SEL_LEN
    p_slc = jnp.einsum('bgln,ns->bgls', p_cmp, jnp.asarray(selection_overlap(n_cmp, n_slc)))
    blk = jnp.arange(n_slc)[None, :]
    cur = (pos // SEL_LEN)[:, None]
    valid = blk <= cur
    forced = ((blk == 0) | (blk == cur) | (blk == cur - 1)).astype(jnp.float32)
    score = jnp.where(valid, p_slc + SEL_BONUS * forced, -SEL_BONUS)
    top, idx = lax.top_k(score, min(SEL_TOPK, n_slc))
    return idx, top > -0.5 * SEL_BONUS

def selected_attention(q, ks, vs, idx, ok):
    B_, L = q.shape[:2]
    n_slc = L // SEL_LEN
    n_ch = L // SEL_QCHUNK
    kb = jnp.moveaxis(ks.reshape(B_, n_slc, SEL_LEN, N_KV, HEAD_DIM), 3, 1)
    vb = jnp.moveaxis(vs.reshape(B_, n_slc, SEL_LEN, N_KV, HEAD_DIM), 3, 1)
    q_ch = jnp.moveaxis(q.reshape(B_, n_ch, SEL_QCHUNK, N_KV, HPG, HEAD_DIM), 1, 0)
    idx_ch = jnp.moveaxis(idx.reshape(B_, N_KV, n_ch, SEL_QCHUNK, -1), 2, 0)
    ok_ch = jnp.moveaxis(ok.reshape(B_, N_KV, n_ch, SEL_QCHUNK, -1), 2, 0)
    gather = jax.vmap(jax.vmap(lambda blocks, ix: blocks[ix]))
    offs = jnp.arange(SEL_LEN)

    def chunk(args):
        ci, qc, ic, oc = args
        t = ci * SEL_QCHUNK + jnp.arange(SEL_QCHUNK)
        kg = gather(kb, ic)
        vg = gather(vb, ic)
        s = jnp.einsum('bqghd,bgqksd->bgqhks', qc, kg)
        kpos = ic[..., None] * SEL_LEN + offs
        mask = (oc[..., None] & (kpos <= t[None, None, :, None, None]))[:, :, :, None]
        p = masked_softmax(s.reshape(*s.shape[:4], -1), mask.reshape(*mask.shape[:4], -1))
        p = p.reshape(s.shape).astype(vg.dtype)
        return jnp.einsum('bgqhks,bgqksd->bqghd', p, vg)

    o = lax.map(chunk, (jnp.arange(n_ch), q_ch, idx_ch, ok_ch))
    return jnp.moveaxis(o, 0, 1).reshape(B_, L, N_KV, HPG, HEAD_DIM)

def window_attention(q, kw, vw):
    B_, L = q.shape[:2]
    nb = L // WIN_QBLOCK
    span = WIN_QBLOCK + WINDOW
    pad = ((0, 0), (WINDOW, 0), (0, 0), (0, 0))
    kp, vp = jnp.pad(kw, pad), jnp.pad(vw, pad)
    q_blk = jnp.moveaxis(q.reshape(B_, nb, WIN_QBLOCK, N_KV, HPG, HEAD_DIM), 1, 0)
    koff = np.arange(span) - WINDOW
    rel = np.arange(WIN_QBLOCK)[:, None] - koff[None, :]
    band = (rel >= 0) & (rel < WINDOW)

    def block(args):
        bi, qb = args
        start = bi * WIN_QBLOCK
        kb = lax.dynamic_slice_in_dim(kp, start, span, axis=1)
        vb = lax.dynamic_slice_in_dim(vp, start, span, axis=1)
        mask = band & ((start + koff) >= 0)[None, :]
        s = jnp.einsum('bqghd,bkgd->bghqk', qb, kb)
        p = masked_softmax(s, mask).astype(vb.dtype)
        return jnp.einsum('bghqk,bkgd->bqghd', p, vb)

    o = lax.map(block, (jnp.arange(nb), q_blk))
    return jnp.moveaxis(o, 0, 1).reshape(B_, L, N_KV, HPG, HEAD_DIM)

def nsa_mixer(h, w_qg, w_o, kc, vc, ks, vs, kw, vw):
    B_, L, _ = h.shape
    proj = h @ w_qg
    q = proj[..., :ATT_WIDTH].reshape(B_, L, N_KV, HPG, HEAD_DIM) * (HEAD_DIM ** -0.5)
    g_end = ATT_WIDTH + N_BRANCH * N_HEADS
    gates = jax.nn.sigmoid(proj[..., ATT_WIDTH:g_end].astype(jnp.float32)).astype(h.dtype)
    gates = gates.reshape(B_, L, N_BRANCH, N_KV, HPG, 1)
    z = proj[..., g_end:].reshape(B_, L, N_BRANCH, N_KV, HPG, HEAD_DIM)
    pos = jnp.arange(L)
    o_cmp, p_cmp = cmp_attention(q, kc, vc, pos)
    idx, ok = select_blocks(p_cmp, pos)
    o_sel = selected_attention(q, ks, vs, idx, ok)
    o_win = window_attention(q, kw, vw)
    o_br = jnp.stack([o_cmp, o_sel, o_win], axis=2)
    o = jnp.sum(gates * jax.nn.silu(z) * o_br, axis=2)
    return o.reshape(B_, L, ATT_WIDTH) @ w_o

def first_inputs(seed: int = 0) -> dict:
    key = jax.random.key(seed)
    keys = list(jax.random.split(key, 40))

    def nrm(shape, s):
        return s * jax.random.normal(keys.pop(), shape, jnp.float32)

    D, E, G, N = D_MODEL, SSM_WIDTH, SSM_GROUPS, SSM_STATE
    qg_cols = ATT_WIDTH + N_BRANCH * N_HEADS + N_BRANCH * ATT_WIDTH
    lam_im0 = jnp.pi * jnp.arange(N, dtype=jnp.float32)
    return {
        "x": nrm((BATCH, SEQ, D), 1.0),
        "c": nrm((BATCH, D), 1.0),
        "norm_g": 1.0 + nrm((DEPTH, D), 0.02),
        "mod_w": nrm((DEPTH, D, 3 * D), 0.5 * D ** -0.5),
        "mod_b": nrm((DEPTH, 3 * D), 0.01),
        "ssm_w_in": nrm((N_A, D, 2 * E), D ** -0.5),
        "ssm_lam_re": -0.5 + nrm((N_A, G, N), 0.01),
        "ssm_lam_im": lam_im0 + nrm((N_A, G, N), 0.01),
        "ssm_log_step": jax.random.uniform(keys.pop(), (N_A, G), jnp.float32, math.log(1e-3), math.log(1e-1)),
        "ssm_b_re": nrm((N_A, G, N, SSM_GROUP), (2 * SSM_GROUP) ** -0.5),
        "ssm_b_im": nrm((N_A, G, N, SSM_GROUP), (2 * SSM_GROUP) ** -0.5),
        "ssm_c_re": nrm((N_A, G, SSM_GROUP, N), 0.5),
        "ssm_c_im": nrm((N_A, G, SSM_GROUP, N), 0.5),
        "ssm_d": nrm((N_A, E), 1.0),
        "ssm_w_glu": nrm((N_A, E, E), E ** -0.5),
        "ssm_b_glu": nrm((N_A, E), 0.01),
        "ssm_w_out": nrm((N_A, E, D), E ** -0.5),
        "kv_norm_g": 1.0 + nrm((D,), 0.02),
        "kv_mod_w": nrm((D, 2 * D), 0.5 * D ** -0.5),
        "kv_mod_b": nrm((2 * D,), 0.01),
        "w_kv": nrm((D, 2 * N_BRANCH * N_KV * HEAD_DIM), D ** -0.5),
        "cmp_pe": nrm((2, CMP_LEN, HEAD_DIM), 0.02),
        "cmp_w1": nrm((2, CMP_LEN * HEAD_DIM, HEAD_DIM), (CMP_LEN * HEAD_DIM) ** -0.5),
        "cmp_b1": nrm((2, HEAD_DIM), 0.01),
        "cmp_w2": nrm((2, HEAD_DIM, HEAD_DIM), HEAD_DIM ** -0.5),
        "cmp_b2": nrm((2, HEAD_DIM), 0.01),
        "nsa_w_qg": nrm((N_B, D, qg_cols), D ** -0.5),
        "nsa_w_o": nrm((N_B, ATT_WIDTH, D), ATT_WIDTH ** -0.5),
        "final_norm_g": 1.0 + nrm((D,), 0.02),
    }

def first_block(x, c, norm_g, mod_w, mod_b, ssm_w_in, ssm_lam_re, ssm_lam_im, ssm_log_step,
              ssm_b_re, ssm_b_im, ssm_c_re, ssm_c_im, ssm_d, ssm_w_glu, ssm_b_glu, ssm_w_out,
              kv_norm_g, kv_mod_w, kv_mod_b, w_kv, cmp_pe, cmp_w1, cmp_b1, cmp_w2, cmp_b2,
              nsa_w_qg, nsa_w_o, final_norm_g):
    c_act = jax.nn.silu(c)
    shared = None
    for layer in range(DEPTH):
        if layer == N_A:
            kv_shift, kv_scale = jnp.split(c_act @ kv_mod_w + kv_mod_b, 2, axis=-1)
            h_kv = modulate(rmsnorm(x, kv_norm_g), kv_shift, kv_scale)
            shared = nsa_shared_kv(h_kv, w_kv, cmp_pe, cmp_w1, cmp_b1, cmp_w2, cmp_b2)
        shift, scale, gate = jnp.split(c_act @ mod_w[layer] + mod_b[layer], 3, axis=-1)
        h = modulate(rmsnorm(x, norm_g[layer]), shift, scale)
        if layer < N_A:
            out = s5_mixer(h, ssm_w_in[layer], ssm_lam_re[layer], ssm_lam_im[layer],
                           ssm_log_step[layer], ssm_b_re[layer], ssm_b_im[layer],
                           ssm_c_re[layer], ssm_c_im[layer], ssm_d[layer],
                           ssm_w_glu[layer], ssm_b_glu[layer], ssm_w_out[layer])
        else:
            j = layer - N_A
            out = nsa_mixer(h, nsa_w_qg[j], nsa_w_o[j], *shared)
        x = x + gate[:, None, :] * out
    return rmsnorm(x, final_norm_g)


DEPTH_2 = 1

GDN_HEADS = 8
GDN_HEAD_DIM = 128
GDN_WIDTH = GDN_HEADS * GDN_HEAD_DIM
GDN_CONV = 4
GDN_CHUNK = 64
MOBA_HEADS = 8
MOBA_HEAD_DIM = 128
MOBA_WIDTH = MOBA_HEADS * MOBA_HEAD_DIM
MOBA_BLOCK = 256
MOBA_TOPK = 3
MOBA_Q_CHUNK = 16
REL_BUCKETS = 32
REL_MAX_DIST = 2048
D_FF = ((8 * D_MODEL // 3 + 255) // 256) * 256
PROJ_SPLITS = (GDN_WIDTH,) * 4 + (GDN_HEADS,) * 2 + (MOBA_WIDTH,) * 3 + (D_MODEL,) * 2
D_PROJ = sum(PROJ_SPLITS)
RMS_EPS = 1e-6
NEG_INF = -1e30


def _rmsnorm(x, w):
    x32 = x.astype(jnp.float32)
    y = x32 * lax.rsqrt(jnp.mean(x32 * x32, axis=-1, keepdims=True) + RMS_EPS)
    return (y * w.astype(jnp.float32)).astype(x.dtype)

def _l2norm(x):
    return x * lax.rsqrt(jnp.sum(x * x, axis=-1, keepdims=True) + RMS_EPS)

def _causal_short_conv(u, w):
    K = w.shape[0]
    T = u.shape[1]
    up = jnp.pad(u, ((0, 0), (K - 1, 0), (0, 0)))
    y = up[:, 0:T] * w[0]
    for j in range(1, K):
        y = y + up[:, j:j + T] * w[j]
    return jax.nn.silu(y)

def _chunk_gated_delta_rule(q, k, v, g, beta):
    B, H, T, Dk = q.shape
    Dv = v.shape[-1]
    C = GDN_CHUNK
    N = T // C
    q = q * (Dk ** -0.5)
    q, k, v = (t.reshape(B, H, N, C, t.shape[-1]) for t in (q, k, v))
    g = jnp.cumsum(g.reshape(B, H, N, C), axis=-1)
    beta = beta.reshape(B, H, N, C)
    incl = jnp.tril(jnp.ones((C, C), dtype=bool))
    strict = jnp.tril(jnp.ones((C, C), dtype=bool), k=-1)
    diff = g[..., :, None] - g[..., None, :]
    decay = jnp.where(incl, jnp.exp(jnp.where(incl, diff, 0.0)), 0.0)
    k_beta = k * beta[..., None]
    L = jnp.where(strict, jnp.einsum('bhnik,bhnjk->bhnij', k_beta, k) * decay, 0.0)
    eye = jnp.eye(C, dtype=q.dtype)
    rhs = jnp.concatenate([k_beta * jnp.exp(g)[..., None], v * beta[..., None]], axis=-1)
    wu = lax.linalg.triangular_solve(eye + L, rhs, left_side=True, lower=True)
    w, u = wu[..., :Dk], wu[..., Dk:]
    A = jnp.where(incl, jnp.einsum('bhnik,bhnjk->bhnij', q, k) * decay, 0.0)
    g_last = g[..., -1]
    q_dec = q * jnp.exp(g)[..., None]
    k_dec = k * jnp.exp(g_last[..., None] - g)[..., None]
    xs = tuple(jnp.moveaxis(t, 2, 0) for t in (q_dec, k_dec, w, u, A, g_last))

    def step(S, inp):
        q_n, k_n, w_n, u_n, A_n, gl_n = inp
        v_new = u_n - jnp.einsum('bhck,bhkv->bhcv', w_n, S)
        o_n = jnp.einsum('bhck,bhkv->bhcv', q_n, S) + jnp.einsum('bhcs,bhsv->bhcv', A_n, v_new)
        S = S * jnp.exp(gl_n)[..., None, None] + jnp.einsum('bhck,bhcv->bhkv', k_n, v_new)
        return S, o_n

    S0 = jnp.zeros((B, H, Dk, Dv), q.dtype)
    _, o = lax.scan(step, S0, xs)
    return jnp.moveaxis(o, 0, 2).reshape(B, H, T, Dv)

def _gated_deltanet(q, k, v, z, beta_logit, a_logit, conv_w, a_log, dt_bias, o_norm_w):
    B, T, _ = q.shape
    H, Dh = GDN_HEADS, GDN_HEAD_DIM
    f32 = jnp.float32
    qkv = _causal_short_conv(jnp.concatenate([q, k, v], axis=-1), conv_w).astype(f32)
    q, k, v = (t.reshape(B, T, H, Dh).transpose(0, 2, 1, 3) for t in jnp.split(qkv, 3, axis=-1))
    q = _l2norm(q)
    k = _l2norm(k)
    beta = jax.nn.sigmoid(beta_logit.astype(f32)).transpose(0, 2, 1)
    g = -jnp.exp(a_log.astype(f32)) * jax.nn.softplus(a_logit.astype(f32) + dt_bias.astype(f32))
    g = g.transpose(0, 2, 1)
    o = _chunk_gated_delta_rule(q, k, v, g, beta).transpose(0, 2, 1, 3)
    o = _rmsnorm(o, o_norm_w) * jax.nn.silu(z.astype(f32).reshape(B, T, H, Dh))
    return o.reshape(B, T, H * Dh).astype(z.dtype)

def _t5_bucket(dist):
    max_exact = REL_BUCKETS // 2
    d = dist.astype(jnp.float32)
    log_ratio = jnp.log(jnp.maximum(d, float(max_exact)) / max_exact) / math.log(REL_MAX_DIST / max_exact)
    large = max_exact + (log_ratio * (REL_BUCKETS - max_exact)).astype(jnp.int32)
    large = jnp.minimum(large, REL_BUCKETS - 1)
    return jnp.where(dist < max_exact, dist, large)

def _moba_attention(q, k, v, q_norm_w, k_norm_w, rel_bias):
    B, T, _ = q.shape
    H, Dh, BS, QC = MOBA_HEADS, MOBA_HEAD_DIM, MOBA_BLOCK, MOBA_Q_CHUNK
    out_dtype = q.dtype

    def heads(t):
        return t.astype(jnp.float32).reshape(B, T, H, Dh).transpose(0, 2, 1, 3)

    q = _rmsnorm(heads(q), q_norm_w)
    k = _rmsnorm(heads(k), k_norm_w)
    v = heads(v)
    Tp = -(-T // BS) * BS
    pad = ((0, 0), (0, 0), (0, Tp - T), (0, 0))
    q, k, v = (jnp.pad(t, pad) for t in (q, k, v))
    NB = Tp // BS
    topk = min(MOBA_TOPK, NB)
    k_blocks = k.reshape(B, H, NB, BS, Dh)
    v_blocks = v.reshape(B, H, NB, BS, Dh)
    k_mean = jnp.mean(k_blocks, axis=3)
    route = jnp.einsum('bhtd,bhnd->bhtn', q, k_mean)
    q_block = jnp.arange(Tp) // BS
    fully_past = jnp.arange(NB)[None, :] < q_block[:, None]
    route = jnp.where(fully_past, route, NEG_INF)
    _, sel = lax.top_k(route, topk)
    n_qc = Tp // QC
    q_c = jnp.moveaxis(q.reshape(B, H, n_qc, QC, Dh), 2, 0)
    sel_c = jnp.moveaxis(sel.reshape(B, H, n_qc, QC, topk), 2, 0)
    rel_t = rel_bias.astype(jnp.float32).T
    b_idx = jnp.arange(B)[:, None, None, None]
    h_idx = jnp.arange(H)[None, :, None, None]
    scale = Dh ** -0.5
    offs = jnp.arange(BS)

    def attend(args):
        c, q_n, sel_n = args
        q_pos = c * QC + jnp.arange(QC)
        blk = (c * QC) // BS
        k_own = lax.dynamic_index_in_dim(k_blocks, blk, axis=2, keepdims=False)
        v_own = lax.dynamic_index_in_dim(v_blocks, blk, axis=2, keepdims=False)
        dist_own = q_pos[:, None] - (blk * BS + offs)[None, :]
        s_own = jnp.einsum('bhqd,bhkd->bhqk', q_n, k_own) * scale + rel_t[:, _t5_bucket(jnp.maximum(dist_own, 0))][None]
        s_own = jnp.where(dist_own >= 0, s_own, NEG_INF)
        k_sel = k_blocks[b_idx, h_idx, sel_n]
        v_sel = v_blocks[b_idx, h_idx, sel_n]
        dist_sel = q_pos[None, None, :, None, None] - (sel_n[..., None] * BS + offs)
        s_sel = jnp.einsum('bhqd,bhqnkd->bhqnk', q_n, k_sel) * scale + rel_t[h_idx[..., None], _t5_bucket(jnp.maximum(dist_sel, 0))]
        s_sel = jnp.where((sel_n < blk)[..., None], s_sel, NEG_INF)
        logits = jnp.concatenate([s_own, s_sel.reshape(B, H, QC, topk * BS)], axis=-1)
        p = jax.nn.softmax(logits, axis=-1)
        p_own = p[..., :BS]
        p_sel = p[..., BS:].reshape(B, H, QC, topk, BS)
        return jnp.einsum('bhqk,bhkd->bhqd', p_own, v_own) + jnp.einsum('bhqnk,bhqnkd->bhqd', p_sel, v_sel)

    o = lax.map(attend, (jnp.arange(n_qc), q_c, sel_c))
    o = jnp.moveaxis(o, 0, 2).reshape(B, H, Tp, Dh)[:, :, :T]
    return o.transpose(0, 2, 1, 3).reshape(B, T, H * Dh).astype(out_dtype)

def second_inputs(seed: int = 0) -> dict:
    key = jax.random.key(seed)
    ks = jax.random.split(key, 17)
    f32 = jnp.float32

    def normal(k, shape, fan_in):
        return jax.random.normal(k, shape, f32) * fan_in ** -0.5

    def gain(k, shape):
        return 1.0 + 0.1 * jax.random.normal(k, shape, f32)

    x = jax.random.normal(ks[0], (BATCH, SEQ, D_MODEL), f32)
    norm_mix_w = gain(ks[1], (DEPTH_2, D_MODEL))
    w_in = normal(ks[2], (DEPTH_2, D_MODEL, D_PROJ), D_MODEL)
    conv_w = normal(ks[3], (DEPTH_2, GDN_CONV, 3 * GDN_WIDTH), GDN_CONV)
    a_log = jnp.log(jax.random.uniform(ks[4], (DEPTH_2, GDN_HEADS), f32, 1.0, 16.0))
    dt = jnp.exp(jax.random.uniform(ks[5], (DEPTH_2, GDN_HEADS), f32, math.log(1e-3), math.log(1e-1)))
    dt_bias = dt + jnp.log(-jnp.expm1(-dt))
    gdn_o_norm_w = gain(ks[6], (DEPTH_2, GDN_HEAD_DIM))
    q_norm_w = gain(ks[7], (DEPTH_2, MOBA_HEAD_DIM))
    k_norm_w = gain(ks[8], (DEPTH_2, MOBA_HEAD_DIM))
    rel_bias = 0.5 * jax.random.normal(ks[9], (REL_BUCKETS, MOBA_HEADS), f32)
    w_branch_gdn = normal(ks[10], (DEPTH_2, GDN_WIDTH, D_MODEL), GDN_WIDTH)
    w_branch_moba = normal(ks[11], (DEPTH_2, MOBA_WIDTH, D_MODEL), MOBA_WIDTH)
    w_out = normal(ks[12], (DEPTH_2, D_MODEL, D_MODEL), D_MODEL)
    norm_ffn_w = gain(ks[13], (DEPTH_2, D_MODEL))
    w_ffn_gate = normal(ks[14], (DEPTH_2, D_MODEL, D_FF), D_MODEL)
    w_ffn_up = normal(ks[15], (DEPTH_2, D_MODEL, D_FF), D_MODEL)
    w_ffn_down = normal(ks[16], (DEPTH_2, D_FF, D_MODEL), D_FF)
    return {'x': x, 'norm_mix_w': norm_mix_w, 'w_in': w_in, 'conv_w': conv_w, 'a_log': a_log,
            'dt_bias': dt_bias, 'gdn_o_norm_w': gdn_o_norm_w, 'q_norm_w': q_norm_w, 'k_norm_w': k_norm_w,
            'rel_bias': rel_bias, 'w_branch_gdn': w_branch_gdn, 'w_branch_moba': w_branch_moba,
            'w_out': w_out, 'norm_ffn_w': norm_ffn_w, 'w_ffn_gate': w_ffn_gate, 'w_ffn_up': w_ffn_up,
            'w_ffn_down': w_ffn_down}

def second_block(x, norm_mix_w, w_in, conv_w, a_log, dt_bias, gdn_o_norm_w, q_norm_w, k_norm_w,
              rel_bias, w_branch_gdn, w_branch_moba, w_out, norm_ffn_w, w_ffn_gate, w_ffn_up, w_ffn_down):
    split_at = np.cumsum(PROJ_SPLITS)[:-1].tolist()
    h = x
    for l in range(DEPTH_2):
        u = _rmsnorm(h, norm_mix_w[l])
        proj = jnp.einsum('btd,de->bte', u, w_in[l])
        (q_a, k_a, v_a, z_a, beta_a, dec_a, q_b, k_b, v_b, gate_a, gate_b) = jnp.split(proj, split_at, axis=-1)
        y_a = _gated_deltanet(q_a, k_a, v_a, z_a, beta_a, dec_a, conv_w[l], a_log[l], dt_bias[l], gdn_o_norm_w[l])
        y_b = _moba_attention(q_b, k_b, v_b, q_norm_w[l], k_norm_w[l], rel_bias)
        mix = (jax.nn.sigmoid(gate_a) * jnp.einsum('btc,cd->btd', y_a, w_branch_gdn[l])
               + jax.nn.sigmoid(gate_b) * jnp.einsum('btc,cd->btd', y_b, w_branch_moba[l]))
        h = h + jnp.einsum('btd,de->bte', mix, w_out[l])
        u = _rmsnorm(h, norm_ffn_w[l])
        hid = jax.nn.silu(jnp.einsum('btd,df->btf', u, w_ffn_gate[l])) * jnp.einsum('btd,df->btf', u, w_ffn_up[l])
        h = h + jnp.einsum('btf,fd->btd', hid, w_ffn_down[l])
    return h


def setup_inputs(seed=0):
    out = dict(first_inputs(seed))
    for name, value in second_inputs(seed + 1).items():
        if name != "x":
            out[name + "_2"] = value
    return out


def reference(
    x, c, norm_g, mod_w, mod_b, ssm_w_in, ssm_lam_re, ssm_lam_im, ssm_log_step, ssm_b_re,
    ssm_b_im, ssm_c_re, ssm_c_im, ssm_d, ssm_w_glu, ssm_b_glu, ssm_w_out, kv_norm_g, kv_mod_w,
    kv_mod_b, w_kv, cmp_pe, cmp_w1, cmp_b1, cmp_w2, cmp_b2, nsa_w_qg, nsa_w_o, final_norm_g,
    norm_mix_w_2, w_in_2, conv_w_2, a_log_2, dt_bias_2, gdn_o_norm_w_2, q_norm_w_2, k_norm_w_2,
    rel_bias_2, w_branch_gdn_2, w_branch_moba_2, w_out_2, norm_ffn_w_2, w_ffn_gate_2,
    w_ffn_up_2, w_ffn_down_2,
):
    x = first_block(
        x, c, norm_g, mod_w, mod_b, ssm_w_in, ssm_lam_re, ssm_lam_im, ssm_log_step, ssm_b_re,
        ssm_b_im, ssm_c_re, ssm_c_im, ssm_d, ssm_w_glu, ssm_b_glu, ssm_w_out, kv_norm_g,
        kv_mod_w, kv_mod_b, w_kv, cmp_pe, cmp_w1, cmp_b1, cmp_w2, cmp_b2, nsa_w_qg, nsa_w_o,
        final_norm_g,
    )
    return second_block(
        x, norm_mix_w_2, w_in_2, conv_w_2, a_log_2, dt_bias_2, gdn_o_norm_w_2, q_norm_w_2,
        k_norm_w_2, rel_bias_2, w_branch_gdn_2, w_branch_moba_2, w_out_2, norm_ffn_w_2,
        w_ffn_gate_2, w_ffn_up_2, w_ffn_down_2,
    )


_drawn_inputs = setup_inputs


def setup_inputs(seed=0):
    import zlib

    import numpy as np

    out = dict(_drawn_inputs(seed))
    spreads = {}
    factors = {'norm_g': 8.0,
     'mod_b': 8.0,
     'ssm_lam_re': 8.0,
     'ssm_b_glu': 8.0,
     'kv_norm_g': 8.0,
     'kv_mod_b': 8.0,
     'cmp_pe': 8.0,
     'cmp_b1': 8.0,
     'cmp_b2': 26.499,
     'q_norm_w_2': 6.084,
     'k_norm_w_2': 5.703}
    for name, (base, spread) in spreads.items():
        noise = np.random.default_rng([zlib.crc32(name.encode()), seed]).standard_normal(out[name].shape)
        drawn = base * np.exp(spread * noise) if base else spread * noise
        out[name] = __import__('jax').numpy.asarray(drawn.astype(out[name].dtype))
    for name, factor in factors.items():
        out[name] = (out[name] * factor).astype(out[name].dtype)
    return out
```

```python
import math
from contextlib import ExitStack

import numpy as np

import concourse.bass as bass
import concourse.mybir as mybir

F32 = mybir.dt.float32
ALU = mybir.AluOpType
ACT = mybir.ActivationFunctionType
AX_X = mybir.AxisListType.X
ds = bass.ds

P = 128
T = 256
TT = T // P
D = 2048
KD = D // P
RING = 4
SLOT_COLS = 256
SLOT = KD * SLOT_COLS
G, N, CG = 128, 64, 16
STILES = G * N // P
SBLOCKS = STILES // 4
HEADS, KV, HPG, DH = 16, 4, 4, 128
NCMP, CMP_LEN, CMP_STRIDE = 15, 32, 16
GH, CH = 8, 64
NCH = T // CH
FF = 5632
KF = FF // P
DMA_SCRATCH = 64
EPS = 1e-6
NEG = -1e30
SCALE = DH ** -0.5
ROUND = 1.5 * 2.0 ** 23
TWO_PI = 2.0 * math.pi
TURN = float(np.nextafter(np.float32(TWO_PI), np.float32(0)))
TWO_PI_HI = 6.28125
TWO_PI_LO = TWO_PI - TWO_PI_HI

COLS = [("c", 16), ("norm_g", 32), ("mod_b", 128), ("kv_norm_g", 16), ("ssm_d", 16), ("b_glu", 16),
        ("final_g", 16), ("mix_g", 16), ("ffn_g", 16), ("conv_w", 96), ("q_norm", 1), ("k_norm", 1),
        ("o_norm", 1), ("cmp_b1", 2), ("cmp_b2", 2), ("pe", 64), ("lam_re", 64), ("lam_im", 64)]
COL = {}
for _name, _n in COLS:
    COL[_name] = (sum(n for _, n in COLS[:len(COL)]), _n)
NCOLS = sum(n for _, n in COLS)

CONSTS = [("ident", 128), ("causal", 256), ("cum", 128), ("same", 128), ("decay_neg", 128),
          ("strict", 64), ("cmp_neg", 30), ("cmp_one", 30), ("iota", 256)]
CON = {}
for _name, _n in CONSTS:
    CON[_name] = (sum(n for _, n in CONSTS[:len(CON)]), _n)
NCON = sum(n for _, n in CONSTS)

ORDER = [("mod0", 16), ("u", 24), ("z", 24), ("glu", 24), ("out", 8), ("kv", 8), ("kvrow", 4),
         ("cmp", 2), ("q", 8), ("zn", 24), ("o", 8), ("gdn", 12), ("za", 4), ("qkb", 8), ("vb", 4),
         ("bra", 8), ("brb", 8), ("ga", 8), ("gb", 8), ("out2", 8), ("gate", 22), ("up", 22), ("down", 32)]
BASE = {}
for _name, _n in ORDER:
    BASE[_name] = sum(n for _, n in ORDER[:len(BASE)])
COUNT = dict(ORDER)
MIXED = ("u", "z", "glu")
DENSE = {n: 0 if n == "mod0" else c // 3 if n in MIXED else c // 2 if n == "down" else c for n, c in ORDER}
PBASE = {n: sum(DENSE[m] for m, _ in ORDER[:k]) for k, (n, _) in enumerate(ORDER)}
PAIRS = {"mod0": 0, "u": 8, "z": 16, "glu": 24}


def build(nc, t, stages=99, dump=None):
    ctx = ExitStack()
    with ctx:
        def sb(name, shape):
            return ctx.enter_context(nc.sbuf_tensor(name, shape, F32))

        def sem(name):
            return ctx.enter_context(nc.semaphore(name))

        ring = sb("ring", [P, RING, SLOT])
        xT = sb("xT", [P, KD, T])
        hT = sb("hT", [P, KD, T])
        arena = sb("arena", [P, 6 * 4096])
        E = sb("E", [P, 2048])
        W = sb("W", [P, 2048])
        cols = sb("cols", [P, NCOLS])
        con = sb("con", [P, NCON])
        ones = sb("ones", [P, P])
        eps = sb("eps", [P, 1])
        w_gate = sb("w_gate", [P, KD, 48])
        w_beta = sb("w_beta", [P, KD, 16])
        cmp_w2 = sb("cmp_w2", [P, 2, P])
        cmp_b2r = sb("cmp_b2r", [NCMP, P])
        gdn_rows = sb("gdn_rows", [P, 16])
        c_act = sb("c_act", [P, KD])
        mod = sb("mod", [P, 128])
        gain = sb("gain", [P, KD])
        rstd = sb("rstd", [P, T])
        small = sb("small", [P, 320])

        bank = [ctx.enter_context(nc.psum_tensor(f"bank{k}", [P, 512], F32)) for k in range(RING)]
        aux = ctx.enter_context(nc.psum_tensor("aux", [P, 2048], F32))

        def B(k, lo=0, n=4096):
            return arena[:, 4096 * k + lo:4096 * k + lo + n]

        def tiles(ap):
            return ap.rearrange("p (j n) -> p j n", n=T)

        def col(name, lo=0, n=None):
            o, m = COL[name]
            return cols[:, o + lo:o + lo + (m - lo if n is None else n)]

        def cst(name, lo=0, n=None):
            o, m = CON[name]
            return con[:, o + lo:o + lo + (m - lo if n is None else n)]

        ident = cst("ident")

        def A(k, lo=0, n=512):
            return aux[:, 512 * k + lo:512 * k + lo + n]

        def bc(ap, n):
            return ap.rearrange("p (a o) -> p a o", o=1).to_broadcast([ap.shape[0], ap.shape[1], n])

        def rep(ap, n):
            return ap.rearrange("p (o a) -> p o a", o=1).to_broadcast([ap.shape[0], n, ap.shape[1]])

        SH0, SC0, GT0, KSH, KSC, SH1, SC1, GT1 = (mod[:, 16 * k:16 * k + 16] for k in range(8))

        params_in = sem("params_in")
        weights_in = [sem(f"weights_in{k}") for k in range(RING)]
        products = sem("products")
        slot_free = [sem(f"slot_free{k}") for k in range(RING)]
        acc_ready = sem("acc_ready")
        acc_used = sem("acc_used")
        c_ready = sem("c_ready")
        ones_ready = sem("ones_ready")
        mod_ready = sem("mod_ready")
        sq_ready = sem("sq_ready")
        ms_ready = sem("ms_ready")
        std_ready = sem("std_ready")
        h_ready = sem("h_ready")
        x_ready = sem("x_ready")
        stored = sem("stored")


        def wait_free(eng, n, r):
            eng.wait_ge(slot_free[n % RING], r + n // RING + 1)

        def wait_landed(eng, n, r):
            eng.wait_ge(weights_in[n % RING], 16 * r + 16 * (n // RING + 1))

        def load(sp, n, r, src):
            dst, from_ = src
            wait_free(sp, n, r)
            sp.dma_start(dst(ring[:, n % RING, :]), from_).then_inc(weights_in[n % RING], 16)

        def stream(sp, name, src):
            steps(sp, name, lambda i, k: load(sp, BASE[name] + k, i, src(i, k)), COUNT[name])

        def stream_mod0(sp, src):
            with sp.Fori(0, COUNT["mod0"] // 8) as i:
                for k in range(8):
                    load(sp, BASE["mod0"] + k, 2 * i, src(2 * i, k))

        def stream_mixed(sp, name, src, mod_src):
            with sp.Fori(0, COUNT[name] // 12) as i:
                for k in range(4):
                    load(sp, BASE[name] + 3 * k, 3 * i, src(i, k))
                    for x in range(2):
                        load(sp, BASE[name] + 3 * k + 1 + x, 3 * i, mod_src(2 * i, 2 * PAIRS[name] + 2 * k + x))

        def cols_of(w, first=0, kd=KD):
            view = w.rearrange("(j p) n -> p j n", p=P)

            def src(i, k):
                at = first + SLOT_COLS * k
                if not isinstance(i, int):
                    at = ds(SLOT_COLS * 4 * i + at, SLOT_COLS)
                else:
                    at = slice(at, at + SLOT_COLS)
                return (lambda slot: slot[:, 0:kd * SLOT_COLS].rearrange("p (j n) -> p j n", j=kd)), view[:, :, at]
            return src

        def steps(eng, name, body, count=None):
            count = DENSE[name] if count is None else count
            if count // 4 > 1:
                with eng.Fori(0, count // 4) as i:
                    for k in range(4):
                        body(i, k)
            else:
                for k in range(count - count % 4):
                    body(0, k)
            for k in range(count - count % 4, count):
                body(0, k)

        def place(name, i, k):
            return (BASE[name] + 3 * k, 3 * i) if name in MIXED else (BASE[name] + k, i)

        def slot_ready(pe, name, i, k):
            n, r = place(name, i, k)
            wait_landed(pe, n, r)
            wait_free(pe, n, r)
            return n % RING

        def dense(pe, name, act, kd=KD):
            def body(i, k):
                s = slot_ready(pe, name, i, k)
                w = ring[:, s, :].rearrange("p (j n) -> p j n", n=SLOT_COLS)
                for f in range(2):
                    for j in range(kd):
                        last = nc.tensor.matmul(bank[s][:, T * f:T * f + T], w[:, j, P * f:P * f + P], act[:, j, :],
                                                start=j == 0, stop=j == kd - 1)
                last.then_inc(products, 1)
                if name in MIXED:
                    mod_columns(pe, name, i, k)
            steps(pe, name, body)

        def dense_rows(pe, name, act):
            def body(i, k):
                s = slot_ready(pe, name, i, k)
                w = ring[:, s, :].rearrange("p (j n) -> p j n", n=SLOT_COLS)
                for f in range(TT):
                    for j in range(KD):
                        last = nc.tensor.matmul(bank[s][:, T * f:T * f + T], act[:, j, P * f:P * f + P], w[:, j, :],
                                                start=j == 0, stop=j == KD - 1)
                last.then_inc(products, 1)
            steps(pe, name, body)

        acc = E[:, 1024:2048].rearrange("p (b x n) -> p b x n", b=2, x=2)
        MOD_BANK = {"mod0": 2, "u": 3, "z": 2, "glu": 3}

        def mod_pair(dve, name, i, k, slots):
            v = nc.vector
            dve.wait_ge(acc_used, 4 * i + PAIRS[name] + k + 1)
            for n, r in slots:
                wait_landed(dve, n, r)
            for j in range(KD):
                for x, (n, r) in enumerate(slots):
                    w = ring[:, n % RING, SLOT_COLS * j:SLOT_COLS * j + SLOT_COLS]
                    a = acc[:, k % 2, x, :]
                    if j == 0:
                        last = v.tensor_scalar(a, w, c_act[:, j:j + 1], None, ALU.mult)
                    else:
                        last = v.scalar_tensor_tensor(a, w, c_act[:, j:j + 1], a, ALU.mult, ALU.add)
                    if j == KD - 1:
                        last.then_inc(slot_free[n % RING], 1)
                if j < KD - 1:
                    dve.drain()
            dve.drain().then_inc(acc_ready, 1)

        def mod_columns(pe, name, i, k):
            pe.wait_ge(acc_ready, 4 * i + PAIRS[name] + k + 1)
            for x in range(2):
                for f in range(2):
                    at = 512 * MOD_BANK[name] + 4 * k + 2 * x + f
                    at = slice(at, at + 1) if isinstance(i, int) else ds(16 * i + at, 1)
                    last = nc.tensor.matmul(aux[:, at], acc[:, k % 2, x, P * f:P * f + P], ones[:, 0:1],
                                            start=True, stop=True)
            last.then_inc(acc_used, 1)

        def dve_mods(dve, name):
            with dve.Fori(0, 2) as i:
                for k in range(4):
                    if name == "mod0":
                        slots = [(BASE[name] + 2 * k + x, 2 * i) for x in range(2)]
                    else:
                        slots = [(BASE[name] + 3 * k + 1 + x, 3 * i) for x in range(2)]
                    mod_pair(dve, name, i, k, slots)
            dve.wait_ge(acc_used, PAIRS[name] + 8 + 2)
            at = 4 * PAIRS[name]
            nc.vector.tensor_tensor(mod[:, at:at + 32], A(MOD_BANK[name], 0, 32), col("mod_b", at, 32), ALU.add)
            dve.drain()

        def product_ready(act, name, i, k):
            act.wait_ge(products, 4 * i + PBASE[name] + k + 1)
            act.wait_ge(params_in, 16 * N_PARAMS)
            n, r = place(name, i, k)
            return n % RING

        def loop_wait(act, sem, value):
            act.wait_ge(sem, value)
            act.wait_ge(params_in, 16 * N_PARAMS)

        def drain_to(act, name, dst, func=ACT.Copy, scale=1.0):
            def body(i, k):
                s = product_ready(act, name, i, k)
                at = slice(2 * k, 2 * k + 2) if isinstance(i, int) else ds(8 * i + 2 * k, 2)
                nc.scalar.activation(dst[:, at, :], bank[s][:].rearrange("p (f n) -> p f n", f=2), func,
                                     scale=scale).then_inc(slot_free[s], 1)
            steps(act, name, body)

        def wait_drained(eng, name):
            n = BASE[name] + COUNT[name] - (3 if name in MIXED else 1)
            eng.wait_ge(slot_free[n % RING], n // RING + 2)


        def act_mean_square(act, k, sq):
            act.wait_ge(x_ready, k + 1)
            nc.scalar.activation(sq, xT[:].rearrange("p j n -> p (j n)"), ACT.Square).then_inc(sq_ready, 1)
            act.wait_ge(ms_ready, k + 1)
            nc.scalar.activation(rstd[:], A(0, 0, T), ACT.Sqrt, scale=1.0 / D, bias=eps[:]).then_inc(std_ready, 1)

        def pe_mean_square(pe, k, sq):
            pe.wait_ge(sq_ready, k + 1)
            for j in range(KD):
                last = nc.tensor.matmul(A(0, 0, T), ones[:], sq[:, T * j:T * j + T], start=j == 0, stop=j == KD - 1)
            last.then_inc(ms_ready, 1)

        def dve_rstd(dve, k):
            dve.wait_ge(std_ready, k + 1)
            nc.vector.reciprocal(rstd[:], rstd[:])
            dve.drain()

        def dve_modulated(dve, dst, g, scale, shift):
            if scale is not None:
                nc.vector.scalar_tensor_tensor(gain[:], scale, 1.0, g, ALU.add, ALU.mult)
            nc.vector.tensor_tensor(dst, xT[:], rep(rstd[:], KD), ALU.mult)
            dve.drain()
            for j in range(KD):
                if scale is not None:
                    last = nc.vector.tensor_scalar(dst[:, j, :], dst[:, j, :], gain[:, j:j + 1], shift[:, j:j + 1],
                                                   ALU.mult, ALU.add)
                else:
                    last = nc.vector.tensor_scalar(dst[:, j, :], dst[:, j, :], g[:, j:j + 1], None, ALU.mult)
            return last

        def dve_residual(dve, name, out, gate):
            wait_drained(dve, name)
            for j in range(KD):
                if gate is None:
                    last = nc.vector.tensor_tensor(xT[:, j, :], xT[:, j, :], out[:, j, :], ALU.add)
                else:
                    last = nc.vector.scalar_tensor_tensor(xT[:, j, :], out[:, j, :], gate[:, j:j + 1], xT[:, j, :],
                                                          ALU.mult, ALU.add)
            dve.drain().then_inc(x_ready, 1)

        N_PARAMS = 10

        def sp_params(sp):
            for dst, src in ((cols[:], t["cols"]), (con[:], t["con"]), (xT[:], t["xT"]),
                             (w_gate[:], t["w_gate"].rearrange("(j p) n -> p j n", p=P)),
                             (w_beta[:], t["w_beta"].rearrange("(j p) n -> p j n", p=P)),
                             (cmp_w2[:], t["cmp_w2"].rearrange("k a b -> a k b")),
                             (cmp_b2r[:], t["cmp_b2v"].to_broadcast([NCMP, P])),
                             (gdn_rows[:], t["gdn_rows"].to_broadcast([P, 16])),
                             (small[0:64, 0:64], t["log_step"][0:1, :].to_broadcast([64, 64])),
                             (small[64:128, 0:64], t["log_step"][1:2, :].to_broadcast([64, 64]))):
                sp.dma_start(dst, src).then_inc(params_in, 16)

        def act_start(act):
            for k in range(RING):
                act.nop().then_inc(slot_free[k], 1)
            act.wait_ge(params_in, 16 * N_PARAMS)
            nc.scalar.activation(c_act[:], col("c"), ACT.Silu).then_inc(c_ready, 1)

        def pe_mod0(pe):
            pe.wait_ge(params_in, 16 * N_PARAMS)
            pe.nop().then_inc(acc_used, 2)
            with pe.Fori(0, 2) as i:
                for k in range(4):
                    mod_columns(pe, "mod0", i, k)

        def dve_start(dve):
            nc.vector.memset(ones[:], 1.0)
            nc.vector.memset(eps[:], EPS)
            dve.wait_ge(params_in, 16 * N_PARAMS)
            dve.drain().then_inc(x_ready, 1)

        def dve_norm0(dve):
            dve_rstd(dve, 0)
            dve_modulated(dve, hT[:], col("norm_g", 0, 16), SC0, SH0).then_inc(h_ready, 1)

        B_RE, B_IM, C_RE, C_IM = (B(3, 1024 * k, 1024) for k in range(4))
        BB_RE, BB_IM, NC_RE, NC_IM = (B(4, 1024 * k, 1024) for k in range(4))
        BT = B(2).rearrange("p (b n) -> p b n", n=256)
        u_all, z_all = tiles(B(0)), tiles(B(1))
        hflat = hT[:].rearrange("p j n -> p (j n)")
        SIN = [hflat[:, 1024 * k:1024 * k + 1024] for k in range(2)]
        COS = [hflat[:, 2048 + 1024 * k:3072 + 1024 * k] for k in range(2)]
        PH, HALF = B(4, 0, 1024), B(4, 1024, 1024)
        ZC = B(3, 0, 2048)
        MC, MS = B(5, 0, 2048), B(5, 2048, 2048)
        V = E[:]
        dt, mag, turns, c_re, c_im = (small[:, 64 * k:64 * k + 64] for k in range(5))
        t0, t1, t2, t3, t4 = (E[:, 64 * k:64 * k + 64] for k in range(5))
        ub = W[:, 0:256]
        bT = W[:, 256:512]
        cpad = W[:, 512:2048].rearrange("p (r k n) -> p r k n", r=3, k=4)
        bst = rstd[:]
        ysum = rstd[:]

        ssm_in = sem("ssm_in")
        dt_ready = sem("dt_ready")
        arg_ready = sem("arg_ready")
        mag_ready = sem("mag_ready")
        angle_ready = sem("angle_ready")
        root_ready = sem("root_ready")
        neg_ready = sem("neg_ready")
        bb_ready = sem("bb_ready")
        spread_ready = sem("spread_ready")
        bT_ready = sem("bT_ready")
        bT_kept = sem("bT_kept")
        staged = sem("staged")
        c_staged = sem("c_staged")
        frac_ready = sem("frac_ready")
        trig_ready = sem("trig_ready")
        bu_ready = sem("bu_ready")
        bu_used = sem("bu_used")
        turned = sem("turned")
        y_ready = sem("y_ready")
        ysum_ready = sem("ysum_ready")
        y_kept = sem("y_kept")
        glu_ready = sem("glu_ready")

        def sp_ssm_loads(sp):
            for dst, name in ((B_RE, "b_re"), (B_IM, "b_im"), (C_RE, "ssm_c_re"), (C_IM, "ssm_c_im")):
                sp.dma_start(dst, t[name]).then_inc(ssm_in, 16)

        def act_ssm_params(act):
            nc.scalar.activation(dt, dt, ACT.Exp).then_inc(dt_ready, 1)
            act.wait_ge(arg_ready, 1)
            nc.scalar.activation(mag, t0, ACT.Exp).then_inc(mag_ready, 1)
            act.wait_ge(angle_ready, 1)
            nc.scalar.activation(t2, t1, ACT.Sin)
            nc.scalar.activation(t3, t1, ACT.Sin, scale=0.5).then_inc(root_ready, 1)
            act.wait_ge(ssm_in, 64)
            nc.scalar.mul(NC_RE, C_RE, -1.0)
            nc.scalar.mul(NC_IM, C_IM, -1.0).then_inc(neg_ready, 1)

        def dve_ssm_params(dve):
            lr, li = col("lam_re"), col("lam_im")
            v = nc.vector
            dve.wait_ge(dt_ready, 1)
            v.tensor_tensor(t0, lr, dt, ALU.mult).then_inc(arg_ready, 1)
            v.tensor_tensor(t1, li, dt, ALU.mult)
            dve.drain()
            v.tensor_scalar(t2, t1, 1.0 / TWO_PI, ROUND, ALU.mult, ALU.add)
            dve.drain()
            v.tensor_scalar(t2, t2, ROUND, None, ALU.subtract)
            dve.drain()
            v.scalar_tensor_tensor(t1, t2, -TWO_PI_HI, t1, ALU.mult, ALU.add)
            dve.drain()
            v.scalar_tensor_tensor(t1, t2, -TWO_PI_LO, t1, ALU.mult, ALU.add)
            dve.drain()
            v.tensor_scalar(t1, t1, 3.1415925, -3.1415925, ALU.min, ALU.max)
            dve.drain()
            v.tensor_scalar(turns, t1, 1.0 / TWO_PI, None, ALU.mult).then_inc(angle_ready, 1)
            dve.wait_ge(root_ready, 1)
            dve.wait_ge(mag_ready, 1)
            v.tensor_tensor(t3, t3, t3, ALU.mult)
            v.tensor_tensor(t2, t2, mag, ALU.mult)
            dve.drain()
            v.tensor_scalar(t3, t3, -2.0, 1.0, ALU.mult, ALU.add)
            dve.drain()
            v.tensor_tensor(t3, t3, mag, ALU.mult)
            dve.drain()
            v.tensor_scalar(t3, t3, 1.0, None, ALU.subtract)
            v.tensor_tensor(t0, lr, lr, ALU.mult)
            v.tensor_tensor(t1, li, li, ALU.mult)
            dve.drain()
            v.tensor_tensor(t0, t0, t1, ALU.add)
            dve.drain()
            v.reciprocal(t0, t0)
            v.tensor_tensor(t1, t3, lr, ALU.mult)
            v.tensor_tensor(t4, t2, li, ALU.mult)
            v.tensor_tensor(c_im, t2, lr, ALU.mult)
            dve.drain()
            v.tensor_tensor(t1, t1, t4, ALU.add)
            dve.drain()
            v.tensor_tensor(c_re, t1, t0, ALU.mult)
            v.tensor_tensor(t4, t3, li, ALU.mult)
            dve.drain()
            v.tensor_tensor(c_im, c_im, t4, ALU.subtract)
            dve.drain()
            v.tensor_tensor(c_im, c_im, t0, ALU.mult)
            dve.drain()
            dve.wait_ge(ssm_in, 64)

            def g(x):
                return x.rearrange("p (a n) -> p a n", n=CG)

            tmp = MC[:, 0:1024]
            v.tensor_tensor(g(BB_RE), g(B_RE), bc(c_re, CG), ALU.mult)
            v.tensor_tensor(g(tmp), g(B_IM), bc(c_im, CG), ALU.mult)
            v.tensor_tensor(g(BB_IM), g(B_IM), bc(c_re, CG), ALU.mult)
            dve.drain()
            v.tensor_tensor(BB_RE, BB_RE, tmp, ALU.subtract)
            dve.drain()
            v.tensor_tensor(g(tmp), g(B_RE), bc(c_im, CG), ALU.mult)
            dve.drain()
            v.tensor_tensor(BB_IM, BB_IM, tmp, ALU.add)
            v.memset(bst, 0.0)
            v.memset(cpad.rearrange("p r k n -> p (r k n)"), 0.0)
            dve.drain().then_inc(bb_ready, 1)
            with dve.Fori(0, SBLOCKS) as b:
                dve.wait_ge(bT_kept, b + 1)
                for r, bb in ((0, BB_RE), (1, BB_IM)):
                    src = bb.rearrange("p (k c) -> p k c", c=CG)
                    dst = bst[:, P * r:P * r + P].rearrange("p (k h c) -> p k h c", h=2, c=CG)
                    v.tensor_copy(dst[0:64, :, 0, :], src[0:64, ds(4 * b, 4), :])
                    last = v.tensor_copy(dst[64:128, :, 1, :], src[64:128, ds(4 * b, 4), :])
                last.then_inc(spread_ready, 1)

        def pe_ssm_params(pe):
            with pe.Fori(0, SBLOCKS) as b:
                pe.wait_ge(spread_ready, b + 1)
                nc.tensor.transpose(A(1, 0, P), bst[:, 0:P], ident)
                nc.tensor.transpose(A(1, P, P), bst[:, P:2 * P], ident).then_inc(bT_ready, 1)

        def act_ssm_transposed(act):
            act.nop().then_inc(bT_kept, 1)
            with act.Fori(0, SBLOCKS) as b:
                loop_wait(act, bT_ready, b + 1)
                nc.scalar.copy(BT[:, ds(b, 1), :], A(1, 0, 256).rearrange("p (o n) -> p o n", o=1)).then_inc(bT_kept, 1)

        def blocks(eng, body):
            body(0, 0, False, True)
            with eng.Fori(0, SBLOCKS // 2 - 1) as i:
                for k in range(2):
                    body(2 * i + 1 + k, 1 - k, True, True)
            body(SBLOCKS - 1, 1, True, False)

        def at_block(x, b):
            return x[:, b:b + 1, :] if isinstance(b, int) else x[:, ds(b, 1), :]

        def act_ssm(act):
            def stage_inputs(b):
                nc.scalar.copy(ub.rearrange("p (o n) -> p o n", o=1), at_block(u_all, b))
                nc.scalar.copy(bT.rearrange("p (o n) -> p o n", o=1), at_block(BT, b)).then_inc(staged, 1)

            def trig(b, parity):
                act.wait_ge(frac_ready, b + 1)
                nc.scalar.activation(SIN[parity], PH, ACT.Sin, scale=TURN)
                nc.scalar.activation(HALF, PH, ACT.Sin, scale=TURN / 2)
                act.drain()
                nc.scalar.activation(HALF, HALF, ACT.Square)
                act.drain()
                nc.scalar.activation(COS[parity], HALF, ACT.Copy, scale=-2.0, bias=1.0).then_inc(trig_ready, 1)

            def finish(b):
                act.wait_ge(ysum_ready, b + 2)
                nc.scalar.activation(ysum, ysum, ACT.Gelu_apprx_tanh)
                act.drain()
                nc.scalar.copy(at_block(u_all, b), ysum.rearrange("p (o n) -> p o n", o=1)).then_inc(y_kept, 1)

            def body(b, parity, prev, following):
                loop_wait(act, y_ready, b + 1)
                for r, src in ((0, C_RE), (1, NC_RE), (2, NC_IM)):
                    x = src.rearrange("p (k c) -> p k c", c=CG)
                    flat = W[:, 512 + 512 * r:1024 + 512 * r]
                    for h in range(2):
                        rows = slice(64 * h, 64 * h + 64)
                        diag = bass.AP(tensor=flat.tensor, offset=flat[rows, 16 * h:16 * h + 1].offset,
                                       ap=[list(flat[rows].ap[0]), [P + 32, 4], [1, CG]])
                        mine = x[rows, 4 * b:4 * b + 4, :] if isinstance(b, int) else x[rows, ds(4 * b, 4), :]
                        last = nc.scalar.copy(diag, mine)
                last.then_inc(c_staged, 1)
                if following:
                    loop_wait(act, bu_ready, b + 1)
                    stage_inputs(b + 1)
                    trig(b + 1, 1 - parity)
                if prev:
                    finish(b - 1)

            act.drain()
            stage_inputs(0)
            trig(0, 0)
            blocks(act, body)
            finish(SBLOCKS - 1)

        def pe_ssm(pe):
            def inputs(b):
                pe.wait_ge(staged, b + 1)
                pe.wait_ge(bu_used, b + 1)
                for k in range(4):
                    rows = slice(32 * k, 32 * k + 32)
                    for r in range(2):
                        last = nc.tensor.matmul(A(k, T * r, T), bT[rows, P * r:P * r + P], ub[rows, :],
                                                start=True, stop=True)
                last.then_inc(bu_ready, 1)

            def outputs(b):
                pe.wait_ge(c_staged, b + 1)
                pe.wait_ge(ysum_ready, b + 1)
                pe.wait_ge(turned, b + 1)
                zc = ZC.rearrange("p (k r n) -> p k r n", k=4, r=2)
                zs = V.rearrange("p (k r n) -> p k r n", k=4, r=2)
                n = 0
                for k in range(4):
                    for sign, x in ((0, zc[:, k, 0]), (1, zs[:, k, 1]), (2, zs[:, k, 0]), (2, zc[:, k, 1])):
                        last = nc.tensor.matmul(bank[0][:, T:2 * T], cpad[:, sign, k, :], x, start=n == 0, stop=n == 15)
                        n += 1
                last.then_inc(y_ready, 1)

            def body(b, parity, prev, following):
                if following:
                    inputs(b + 1)
                outputs(b)

            pe.nop().then_inc(y_ready, 1)
            inputs(0)
            blocks(pe, body)

        def dve_ssm(dve):
            v = nc.vector
            mag_k = mag.rearrange("p (a o) -> p a o", o=1)
            d_k = col("ssm_d").rearrange("p (a o) -> p a o", o=1)

            def turns_of(b):
                ph = PH.rearrange("p (k n) -> p k n", k=4)
                f = turns.rearrange("p (a o) -> p a o", o=1)
                f = f[:, 4 * b:4 * b + 4, :] if isinstance(b, int) else f[:, ds(4 * b, 4), :]
                v.tensor_tensor(ph, f.to_broadcast([P, 4, T]), rep(cst("iota"), 4), ALU.mult)
                dve.drain()
                v.tensor_scalar(HALF, PH, ROUND, ROUND, ALU.add, ALU.subtract)
                dve.drain()
                v.tensor_tensor(PH, PH, HALF, ALU.subtract).then_inc(frac_ready, 1)

            def finish(b):
                dve.wait_ge(y_kept, b + 1)
                v.scalar_tensor_tensor(ysum, at_block(u_all, b).rearrange("p o n -> p (o n)"),
                                       at_block(d_k, b).rearrange("p a o -> p (a o)"), bank[0][:, T:2 * T],
                                       ALU.mult, ALU.add).then_inc(ysum_ready, 1)

            def body(b, parity, prev, following):
                bu = aux[:].rearrange("p (k r n) -> p k r n", k=4, r=2)
                mc = MC.rearrange("p (k r n) -> p k r n", k=4, r=2)
                ms = MS.rearrange("p (k r n) -> p k r n", k=4, r=2)
                z = V.rearrange("p (k r n) -> p k r n", k=4, r=2)
                zc = ZC.rearrange("p (k r n) -> p k r n", k=4, r=2)
                co = COS[parity].rearrange("p (k n) -> p k n", k=4)
                si = SIN[parity].rearrange("p (k n) -> p k n", k=4)
                dve.wait_ge(trig_ready, b + 1)
                dve.wait_ge(bu_ready, b + 1)
                for r in range(2):
                    v.tensor_tensor(mc[:, :, r, :], bu[:, :, r, :], co, ALU.mult)
                for r in range(2):
                    last = v.tensor_tensor(ms[:, :, r, :], bu[:, :, r, :], si, ALU.mult)
                last.then_inc(bu_used, 1)
                if following:
                    turns_of(b + 1)
                dve.drain()
                dve.wait_ge(y_ready, b + 1)
                v.tensor_tensor(z[:, :, 0, :], mc[:, :, 0, :], ms[:, :, 1, :], ALU.add)
                v.tensor_tensor(z[:, :, 1, :], mc[:, :, 1, :], ms[:, :, 0, :], ALU.subtract)
                if prev:
                    finish(b - 1)
                dve.drain()
                for k in range(4):
                    m = mag_k[:, 4 * b + k:4 * b + k + 1, :] if isinstance(b, int) else mag_k[:, ds(4 * b + k, 1), :]
                    m = m.rearrange("p a o -> p (a o)").to_broadcast([P, T])
                    for r in range(2):
                        v.tensor_tensor_scan(z[:, k, r, :], m, z[:, k, r, :], 0.0, ALU.mult, ALU.add)
                dve.drain()
                for r in range(2):
                    v.tensor_tensor(zc[:, :, r, :], z[:, :, r, :], co, ALU.mult)
                dve.drain()
                for r in range(2):
                    last = v.tensor_tensor(z[:, :, r, :], z[:, :, r, :], si, ALU.mult)
                last.then_inc(turned, 1)

            v.nop().then_inc(bu_used, 1)
            v.nop().then_inc(ysum_ready, 1)
            wait_drained(dve, "z")
            dve.wait_ge(bT_kept, SBLOCKS + 1)
            turns_of(0)
            blocks(dve, body)
            dve.wait_ge(y_ready, SBLOCKS + 1)
            finish(SBLOCKS - 1)

        def act_glu(act):
            s_all = tiles(B(2))

            def body(i, k):
                s = product_ready(act, "glu", i, k)
                for f in range(2):
                    at = 2 * k + f
                    o = COL["b_glu"][0] + at
                    last = nc.scalar.activation(s_all[:, ds(8 * i + at, 1), :].rearrange("p a n -> p (a n)"),
                                                bank[s][:, T * f:T * f + T], ACT.Sigmoid,
                                                bias=cols[:, ds(8 * i + o, 1)])
                last.then_inc(slot_free[s], 1)
            steps(act, "glu", body)

        def dve_glu(dve):
            wait_drained(dve, "glu")
            nc.vector.tensor_tensor(B(2), B(2), B(0), ALU.mult)
            dve.drain()
            nc.vector.tensor_tensor(B(2), B(2), B(1), ALU.mult).then_inc(glu_ready, 1)

        KC, VC, KS, KW = (B(4, 1024 * k, 1024) for k in range(4))
        v_row = E[:].rearrange("p (b t n) -> p b t n", b=2, t=TT)
        cmp_in = [[B(5, 2048 * k + 1024 * h, 1024) for h in range(2)] for k in range(2)]
        q_all = tiles(B(0))
        zn = arena[:, 4096:4 * 4096].rearrange("p (j n) -> p j n", n=T)
        hid = W[:, 0:120].rearrange("p (k n) -> p k n", k=2)
        kcT = W[:, 128:188]
        vcr = W[0:NCMP, 256:768]
        gates = small[:, 0:96].rearrange("p (t n) -> p t n", t=TT)
        qg = B(5, 0, 1024).rearrange("p (h n) -> p h n", h=4)
        vg = W[:, 1024:1536].rearrange("p (b t n) -> p b t n", b=2, t=TT)
        vcg = W[0:NCMP, 1536:1664]
        SS, PP, PT = B(5, 1024, 1024), B(5, 2048, 1024), B(5, 3072, 1024)
        mx, rc = small[:, 96:100], small[:, 100:104]
        cmp_ready = sem("cmp_ready")
        hid_ready = sem("hid_ready")
        hid_act = sem("hid_act")
        cmp_out = sem("cmp_out")
        kc_kept = sem("kc_kept")
        vc_kept = sem("vc_kept")
        gates_ready = sem("gates_ready")
        gates_kept = sem("gates_kept")
        group_staged = sem("group_staged")
        s_ready = sem("s_ready")
        s_shifted = sem("s_shifted")
        e_ready = sem("e_ready")
        p_ready = sem("p_ready")
        pT_ready = sem("pT_ready")
        pT_kept = sem("pT_kept")
        o_ready = sem("o_ready")
        o_used = sem("o_used")
        att_ready = sem("att_ready")

        def dve_norm1(dve):
            dve_rstd(dve, 1)
            dve_modulated(dve, tiles(B(0)), col("kv_norm_g"), KSC, KSH).then_inc(h_ready, 1)
            dve.drain()
            dve_modulated(dve, hT[:], col("norm_g", 16, 16), SC1, SH1).then_inc(h_ready, 1)

        def act_kv(act):
            drain_to(act, "kv", tiles(B(4)))

            def body(i, k):
                s = product_ready(act, "kvrow", i, k)
                nc.scalar.copy(v_row[:, k // 2, :, SLOT_COLS * (k % 2):SLOT_COLS * (k % 2) + SLOT_COLS],
                               bank[s][:].rearrange("p (t n) -> p t n", t=TT)).then_inc(slot_free[s], 1)
            steps(act, "kvrow", body)

        def dve_cmp_in(dve):
            wait_drained(dve, "kv")
            for k, src in ((0, KC), (1, VC)):
                for h in range(2):
                    pe_ = col("pe", 32 * k + 16 * h, 16)
                    last = nc.vector.tensor_tensor(cmp_in[k][h].rearrange("p (a l) -> p a l", l=16),
                                                   src.rearrange("p (a l) -> p a l", l=16), rep(pe_, 64), ALU.add)
            last.then_inc(cmp_ready, 1)

        def pe_cmp(pe):
            pe.wait_ge(cmp_ready, 1)
            for k in range(2):
                s = slot_ready(pe, "cmp", 0, k)
                for l in range(CMP_LEN):
                    x = cmp_in[k][l // 16].rearrange("p (h a l) -> p h a l", h=KV, l=16)
                    x = x[:, :, l // 16:l // 16 + NCMP, l % 16]
                    last = nc.tensor.matmul(bank[s][:, 0:60].rearrange("p (h a) -> p h a", h=KV),
                                            ring[:, s, P * l:P * l + P], x, start=l == 0, stop=l == CMP_LEN - 1)
                last.then_inc(products, 1)
            pe.wait_ge(hid_act, 2)
            nc.tensor.matmul(A(1, 0, 60), cmp_w2[:, 0, :], hid[:, 0, :], start=True, stop=True)
            for h in range(KV):
                last = nc.tensor.matmul(A(2)[0:NCMP, P * h:P * h + P], hid[:, 1, NCMP * h:NCMP * h + NCMP],
                                        cmp_w2[:, 1, :], start=True, stop=True)
            last.then_inc(cmp_out, 1)

        def act_cmp(act):
            for k in range(2):
                s = product_ready(act, "cmp", 0, k)
                nc.scalar.activation(hid[:, k, :], bank[s][:, 0:60], ACT.Gelu_apprx_tanh,
                                     bias=col("cmp_b1", k, 1)).then_inc(hid_act, 1)
                act.wait_ge(hid_act, k + 1)
                act.nop().then_inc(slot_free[s], 1)
            act.wait_ge(cmp_out, 1)
            nc.scalar.activation(kcT, A(1, 0, 60), ACT.Identity, bias=col("cmp_b2", 0, 1)).then_inc(kc_kept, 1)

        def dve_cmp(dve):
            dve.wait_ge(cmp_out, 1)
            nc.vector.tensor_tensor(vcr.rearrange("p (h d) -> p h d", h=KV),
                                    A(2)[0:NCMP].rearrange("p (h d) -> p h d", h=KV),
                                    rep(cmp_b2r[:], KV), ALU.add).then_inc(vc_kept, 1)

        def pe_gates(pe):
            for f in range(TT):
                for j in range(KD):
                    last = nc.tensor.matmul(A(3, 48 * f, 48), hT[:, j, P * f:P * f + P], w_gate[:, j, :],
                                            start=j == 0, stop=j == KD - 1)
            last.then_inc(gates_ready, 1)

        def act_gates(act):
            act.wait_ge(gates_ready, 1)
            nc.scalar.activation(small[:, 0:96], A(3, 0, 96), ACT.Sigmoid).then_inc(gates_kept, 1)

        UNITS = [("cmp", 0), ("cmp", 1), (0, 0), (0, 1), (1, 0), (1, 1)]
        ATT = len(UNITS)

        def act_attend(act):
            act.drain()
            act.wait_ge(vc_kept, 1)
            with act.Fori(0, KV) as g:
                loop_wait(act, o_used, ATT * g + 1)
                nc.scalar.copy(qg, q_all[:, ds(4 * g, 4), :])
                for b in range(2):
                    nc.scalar.copy(vg[:, b], v_row[:, b, :, ds(P * g, P)])
                nc.scalar.copy(vcg, vcr[:, ds(P * g, P)]).then_inc(group_staged, 1)
                for u, (b, f) in enumerate(UNITS):
                    nk = NCMP if b == "cmp" else P * (f + 1)
                    act.wait_ge(s_shifted, ATT * g + u + 1)
                    nc.scalar.activation(PP[:, 0:4 * nk], SS[:, 0:4 * nk], ACT.Exp).then_inc(e_ready, 1)
                    act.wait_ge(pT_ready, ATT * g + u + 1)
                    if b == "cmp":
                        last = nc.scalar.copy(PT[0:NCMP, 0:512], A(2)[0:NCMP])
                    else:
                        last = nc.scalar.copy(PT[:, 0:512 * (f + 1)], aux[:, 1024:1024 + 512 * (f + 1)])
                    last.then_inc(pT_kept, 1)

        def pe_attend(pe):
            pe.wait_ge(kc_kept, 1)
            wait_drained(pe, "zn")
            with pe.Fori(0, KV) as g:
                pe.wait_ge(group_staged, g + 1)
                for u, (b, f) in enumerate(UNITS):
                    rows = slice(P * f, P * f + P)
                    if b == "cmp":
                        nk, keys = NCMP, kcT[:, ds(NCMP * g, NCMP)]
                    else:
                        nk, keys = P * (f + 1), (KS, KW)[b][:, ds(T * g, P * (f + 1))]
                    for h in range(HPG):
                        last = nc.tensor.matmul(aux[:, nk * h:nk * h + nk], qg[:, h, rows], keys, start=True, stop=True)
                    last.then_inc(s_ready, 1)
                    pe.wait_ge(p_ready, ATT * g + u + 1)
                    pe.wait_ge(o_used, ATT * g + u + 1)
                    if b == "cmp":
                        for h in range(HPG):
                            last = nc.tensor.transpose(A(2)[0:NCMP, P * h:P * h + P], PP[:, nk * h:nk * h + nk], ident)
                    else:
                        for kt in range(f + 1):
                            for h in range(HPG):
                                at = nk * h + P * kt
                                last = nc.tensor.transpose(A(2 + kt, P * h, P), PP[:, at:at + P], ident)
                    last.then_inc(pT_ready, 1)
                    pe.wait_ge(pT_kept, ATT * g + u + 1)
                    if b == "cmp":
                        last = nc.tensor.matmul(A(2), vcg, PT[0:NCMP, 0:512], start=True, stop=True)
                    else:
                        for kt in range(f + 1):
                            last = nc.tensor.matmul(A(2), vg[:, b, kt, :], PT[:, 512 * kt:512 * kt + 512],
                                                    start=kt == 0, stop=kt == f)
                    last.then_inc(o_ready, 1)

        def dve_softmax(dve, n, nk, mask, weight, keep=None):
            v = nc.vector
            s3 = SS[:, 0:4 * nk].rearrange("p (h n) -> p h n", h=4)
            p3 = PP[:, 0:4 * nk].rearrange("p (h n) -> p h n", h=4)
            dve.wait_ge(s_ready, n + 1)
            v.tensor_tensor(s3, aux[:, 0:4 * nk].rearrange("p (h n) -> p h n", h=4), mask, ALU.add)
            dve.drain()
            v.reduce_max(mx, s3, AX_X)
            dve.drain()
            v.tensor_tensor(s3, s3, bc(mx, nk), ALU.subtract).then_inc(s_shifted, 1)
            dve.wait_ge(e_ready, n + 1)
            v.reduce_sum(rc, p3, AX_X)
            dve.drain()
            v.reciprocal(rc, rc)
            dve.drain()
            if weight is not None:
                v.tensor_tensor(rc, rc, weight, ALU.mult)
                dve.drain()
            last = v.tensor_tensor(p3, p3, bc(rc, nk), ALU.mult)
            if keep is not None:
                dve.drain()
                last = v.tensor_tensor(p3, p3, keep, ALU.mult)
            last.then_inc(p_ready, 1)

        def dve_attend(dve):
            dve.wait_ge(gates_kept, 1)
            wait_drained(dve, "zn")
            nc.vector.nop().then_inc(o_used, 1)
            with dve.Fori(0, KV) as g:
                for u, (b, f) in enumerate(UNITS):
                    if b == "cmp":
                        nk, mask, br = NCMP, rep(cst("cmp_neg", NCMP * f, NCMP), 4), 0
                        keep = rep(cst("cmp_one", NCMP * f, NCMP), 4)
                    else:
                        nk, br, keep = P * (f + 1), b + 1, None
                        mask = rep(cst("causal", P - P * f, nk), 4)
                    dve_softmax(dve, ATT * g + u, nk, mask, gates[:, f, ds(4 * g + HEADS * br, 4)], keep)
                    dve.wait_ge(o_ready, ATT * g + u + 1)
                    z = zn[:, ds(4 * g + HEADS * br, 4), P * f:P * f + P]
                    nc.vector.tensor_tensor(z, z, A(2).rearrange("p (h n) -> p h n", h=4), ALU.mult).then_inc(o_used, 1)
            dve.drain()
            nc.vector.tensor_tensor(B(1), B(1), B(2), ALU.add)
            dve.drain()
            nc.vector.tensor_tensor(B(1), B(1), B(3), ALU.add).then_inc(att_ready, 1)

        raw = arena[:, 0:6144].rearrange("p (j n) -> p j n", n=T)
        conv = arena[:, 2 * 4096:2 * 4096 + 6144].rearrange("p (j n) -> p j n", n=T)
        za = tiles(B(1, 2048, 2048))
        qk = conv[:, 0:16, :]
        lg = small[:, 0:32].rearrange("p (t n) -> p t n", t=TT)
        beta, gdec, gcum, glast, ebeta, edec = (small[:, 32 + 16 * k:48 + 16 * k].rearrange("p (t h) -> p t h", t=TT)
                                                for k in range(6))
        sp_a, sp_b = (small[:, 128 + 16 * k:144 + 16 * k].rearrange("p (t h) -> p t h", t=TT) for k in range(2))
        ea = small[:, 160:168]
        egl = small[:, 168:200]
        Gb, betab = B(0, 0, 2048), B(0, 2048, 2048)
        wide = [B(5, 0, 2048), B(5, 2048, 2048)]
        EGb = B(1, 0, 2048)
        at_all = B(4, 0, 2048).rearrange("p (h t n) -> p h t n", h=GH, t=TT)
        o_all = tiles(B(4, 2048, 2048))
        st = [B(3, 2048 + 256 * k, 256) for k in range(8)]
        qh, kh, vh = st[0], st[1], st[2]
        LT = E[:, 0:1024].rearrange("p (h t n) -> p h t n", h=GH, t=TT)
        Tsol = E[:, 1024:2048].rearrange("p (c n) -> p c n", c=16)
        Lsys = B(5).rearrange("p (j i) -> p j i", i=CH)
        tmp_solve = W[:, 0:1024]
        red = W[:, 1024:1040]

        conv_ready = sem("conv_ready")
        silu_ready = sem("silu_ready")
        hsq_ready = sem("hsq_ready")
        hms_ready = sem("hms_ready")
        hms_kept = sem("hms_kept")
        qk_ready = sem("qk_ready")
        lg_ready = sem("lg_ready")
        lg_kept = sem("lg_kept")
        beta_ready = sem("beta_ready")
        dec_in = sem("dec_in")
        dec_log = sem("dec_log")
        wide_ready = sem("wide_ready")
        cum_ready = sem("cum_ready")
        cum_kept = sem("cum_kept")
        bcast_ready = sem("bcast_ready")
        bcast_kept = sem("bcast_kept")
        edec_in = sem("edec_in")
        edec_ready = sem("edec_ready")
        edec_done = sem("edec_done")
        head_staged = sem("head_staged")
        kk_ready = sem("kk_ready")
        diff_ready = sem("diff_ready")
        decay_ready = sem("decay_ready")
        head_done = sem("head_done")
        L_out = sem("L_out")
        L_in = sem("L_in")
        T_solved = sem("T_solved")
        T_out = sem("T_out")
        T_in = sem("T_in")
        h2_staged = sem("h2_staged")
        rows_ready = sem("rows_ready")
        rows_kept = sem("rows_kept")
        w_ready = sem("w_ready")
        w_kept = sem("w_kept")
        vnew_ready = sem("vnew_ready")
        vnew_kept = sem("vnew_kept")
        step_ready = sem("step_ready")
        S_ready = sem("S_ready")
        oh_kept = sem("oh_kept")
        ya_ready = sem("ya_ready")

        def dve_final0(dve):
            dve_rstd(dve, 2)
            dve_modulated(dve, xT[:], col("final_g"), None, None)
            dve.drain().then_inc(x_ready, 1)
            dve_rstd(dve, 3)
            dve_modulated(dve, hT[:], col("mix_g"), None, None).then_inc(h_ready, 1)

        def pe_beta(pe):
            for f in range(TT):
                for j in range(KD):
                    last = nc.tensor.matmul(A(3, 16 * f, 16), hT[:, j, P * f:P * f + P], w_beta[:, j, :],
                                            start=j == 0, stop=j == KD - 1)
            last.then_inc(lg_ready, 1)

        def act_beta(act):
            act.wait_ge(lg_ready, 1)
            nc.scalar.copy(small[:, 0:32], A(3, 0, 32)).then_inc(lg_kept, 1)
            act.wait_ge(lg_kept, 1)
            nc.scalar.activation(beta, lg[:, :, 0:8], ACT.Sigmoid).then_inc(beta_ready, 1)
            act.wait_ge(dec_in, 1)
            nc.scalar.activation(sp_b, sp_b, ACT.Exp, scale=-1.0)
            nc.scalar.activation(ea, gdn_rows[:, 0:8], ACT.Exp)
            act.drain()
            nc.scalar.activation(sp_b, sp_b, ACT.Ln, bias=1.0).then_inc(dec_log, 1)

        def dve_conv(dve):
            v = nc.vector
            wait_drained(dve, "gdn")
            cw = col("conv_w").rearrange("p (j k) -> p j k", k=4)
            with dve.Fori(0, COUNT["gdn"] * 2 // 4) as i:
                def tile(x, k, lo, hi):
                    return x[:, ds(4 * i + k, 1), lo:hi].rearrange("p a n -> p (a n)")

                for k in range(4):
                    v.tensor_scalar(tile(conv, k, 0, T), tile(raw, k, 0, T), tile(cw, k, 3, 4), None, ALU.mult)
                for tap in range(3):
                    back = 3 - tap
                    dve.drain()
                    for k in range(4):
                        dst = tile(conv, k, back, T)
                        v.scalar_tensor_tensor(dst, tile(raw, k, 0, T - back), tile(cw, k, tap, tap + 1), dst,
                                               ALU.mult, ALU.add)
            dve.drain().then_inc(conv_ready, 1)

        def act_conv(act):
            act.wait_ge(conv_ready, 1)
            for k in range(3):
                at = arena[:, 2 * 4096 + 2048 * k:2 * 4096 + 2048 * k + 2048]
                nc.scalar.activation(at, at, ACT.Silu)
            act.drain()
            nc.scalar.activation(B(0), B(2), ACT.Square).then_inc(hsq_ready, 1)

        def pe_head_squares(pe, k, sq, n):
            pe.wait_ge(hsq_ready, k + 1)
            for i in range(n):
                if i >= 4:
                    pe.wait_ge(hms_kept, HMS[k] + i - 3)
                nc.tensor.matmul(A(i % 4), ones[:], sq[:, 512 * i:512 * i + 512], start=True, stop=True).then_inc(hms_ready, 1)

        HMS = [0, 8, 12]

        def act_head_roots(act, k, dst, n, scale):
            for i in range(n):
                act.wait_ge(hms_ready, HMS[k] + i + 1)
                nc.scalar.activation(dst[:, 512 * i:512 * i + 512], A(i % 4), ACT.Sqrt, bias=eps[:],
                                     scale=scale).then_inc(hms_kept, 1)

        def dve_beta(dve):
            v = nc.vector
            dve.wait_ge(lg_kept, 1)
            v.tensor_tensor(sp_a, lg[:, :, 8:16], rep(gdn_rows[:, 8:16], TT), ALU.add)
            dve.drain()
            v.tensor_scalar(sp_b, sp_a, -1.0, None, ALU.mult)
            dve.drain()
            v.tensor_tensor(sp_b, sp_b, sp_a, ALU.max)
            v.tensor_scalar(sp_a, sp_a, 0.0, None, ALU.max)
            dve.drain().then_inc(dec_in, 1)
            dve.wait_ge(dec_log, 1)
            dve.wait_ge(beta_ready, 1)
            v.tensor_tensor(sp_a, sp_a, sp_b, ALU.add)
            dve.drain()
            v.scalar_tensor_tensor(gdec, sp_a, -1.0, rep(ea, TT), ALU.mult, ALU.mult)
            dve.drain()
            for k, x in ((0, gdec), (1, beta)):
                last = v.tensor_copy(wide[k].rearrange("p (a n) -> p a n", n=P),
                                     bc(x.rearrange("p t h -> p (t h)"), P))
            last.then_inc(wide_ready, 1)

        def pe_beta_sums(pe):
            pe.wait_ge(wide_ready, 1)
            pe.wait_ge(hms_kept, 8)
            for f in range(TT):
                nc.tensor.matmul(A(0, 8 * f, 8), cst("cum"), gdec[:, f, :], start=True, stop=True)
            for f in range(TT):
                last = nc.tensor.matmul(A(0, 16 + 8 * f, 8), cst("same"), gdec[:, f, :], start=True, stop=True)
            last.then_inc(cum_ready, 1)
            pe.wait_ge(cum_kept, 1)
            for k, rhs in ((0, cst("cum")), (1, ident)):
                if k:
                    pe.wait_ge(bcast_kept, 1)
                for h in range(GH):
                    for f in range(TT):
                        at = P * (GH * f + h)
                        last = nc.tensor.matmul(aux[:, T * h + P * f:T * h + P * f + P], wide[k][:, at:at + P], rhs,
                                                start=True, stop=True)
                last.then_inc(bcast_ready, 1)

        def act_beta_sums(act):
            act.wait_ge(cum_ready, 1)
            nc.scalar.copy(gcum.rearrange("p t h -> p (t h)"), A(0, 0, 16))
            nc.scalar.copy(glast.rearrange("p t h -> p (t h)"), A(0, 16, 16)).then_inc(cum_kept, 1)
            act.wait_ge(bcast_ready, 1)
            nc.scalar.copy(Gb, aux[:]).then_inc(bcast_kept, 1)
            act.wait_ge(bcast_ready, 2)
            nc.scalar.copy(betab, aux[:]).then_inc(bcast_kept, 1)
            act.wait_ge(edec_in, 1)
            nc.scalar.activation(EGb, Gb, ACT.Exp)
            nc.scalar.activation(edec.rearrange("p t h -> p (t h)"), edec.rearrange("p t h -> p (t h)"), ACT.Exp)
            nc.scalar.activation(ebeta.rearrange("p t h -> p (t h)"), gcum.rearrange("p t h -> p (t h)"), ACT.Exp).then_inc(edec_ready, 1)

        def dve_qk(dve):
            v = nc.vector
            dve.wait_ge(hms_kept, 8)
            v.reciprocal(B(4), B(4))
            dve.drain()
            v.tensor_tensor(B(2), B(2), B(4), ALU.mult).then_inc(qk_ready, 1)

        def dve_beta_sums(dve):
            v = nc.vector
            dve.wait_ge(cum_kept, 1)
            v.tensor_tensor(edec, glast, gcum, ALU.subtract)
            dve.wait_ge(bcast_kept, 2)
            dve.drain().then_inc(edec_in, 1)
            dve.wait_ge(edec_ready, 1)
            v.tensor_tensor(ebeta, ebeta, beta, ALU.mult)
            v.tensor_copy(egl.rearrange("p (h c) -> p h c", c=NCH),
                          EGb.rearrange("p (h c i) -> p h c i", c=NCH, i=CH)[:, :, :, CH - 1])
            dve.drain().then_inc(edec_done, 1)

        def act_heads(act):
            act.drain()
            act.wait_ge(qk_ready, 1)
            with act.Fori(0, GH) as h:
                loop_wait(act, head_done, h + 1)
                nc.scalar.copy(qh.rearrange("p (o n) -> p o n", o=1), conv[:, ds(h, 1), :])
                nc.scalar.copy(kh.rearrange("p (o n) -> p o n", o=1), conv[:, ds(8 + h, 1), :]).then_inc(head_staged, 1)
                act.wait_ge(diff_ready, h + 1)
                nc.scalar.activation(st[3], st[3], ACT.Exp).then_inc(decay_ready, 1)

        def pe_heads(pe):
            with pe.Fori(0, GH) as h:
                pe.wait_ge(head_staged, h + 1)
                for f in range(TT):
                    r = slice(P * f, P * f + P)
                    nc.tensor.matmul(A(0, P * f, P), kh[:, r], kh[:, r], start=True, stop=True)
                for f in range(TT):
                    r = slice(P * f, P * f + P)
                    last = nc.tensor.matmul(A(1, P * f, P), kh[:, r], qh[:, r], start=True, stop=True)
                last.then_inc(kk_ready, 1)

        def dve_heads(dve):
            v = nc.vector
            v.nop().then_inc(head_done, 1)
            Gb3, bb3 = tiles(Gb), tiles(betab)
            diff = st[3].rearrange("p (t n) -> p t n", t=TT)
            prod = st[4].rearrange("p (t n) -> p t n", t=TT)
            with dve.Fori(0, GH) as h:
                for f in range(TT):
                    v.scalar_tensor_tensor(diff[:, f, :], Gb3[:, ds(h, 1), P * f:P * f + P].rearrange("p o n -> p (o n)"),
                                           gcum[:, f, ds(h, 1)], cst("decay_neg"), ALU.subtract, ALU.add)
                dve.drain().then_inc(diff_ready, 1)
                dve.wait_ge(decay_ready, h + 1)
                dve.wait_ge(kk_ready, h + 1)
                v.scalar_tensor_tensor(at_all[:, ds(h, 1), :, :].rearrange("p o t n -> p (o t n)"), A(1, 0, T), SCALE, st[3],
                                       ALU.mult, ALU.mult)
                v.tensor_tensor(st[4], A(0, 0, T), st[3], ALU.mult)
                dve.drain()
                v.tensor_tensor(st[4], st[4], bb3[:, ds(h, 1), :].rearrange("p o n -> p (o n)"), ALU.mult)
                dve.drain()
                for c in range(2):
                    r = slice(CH * c, CH * c + CH)
                    v.tensor_tensor(LT[r, ds(h, 1), :, :].rearrange("p o t n -> p (o t) n"), prod[r, :, CH * c:CH * c + CH],
                                    rep(cst("strict")[r], TT), ALU.mult)
                dve.drain().then_inc(head_done, 1)

        def sp_solve(sp):
            Ls = t["scratch_L"]
            sp.wait_ge(head_done, GH + 1)
            for c in range(2):
                r = slice(CH * c, CH * c + CH)
                sp.dma_start(Ls.rearrange("h (t c) j i -> c j h t i", c=2)[c], LT[r]).then_inc(L_out, 16)
            sp.dma_start(Tsol, t["eye"]).then_inc(L_in, 16)
            sp.wait_ge(L_out, 32)
            src = Ls.rearrange("h c j i -> (h c) (j i)")
            for c in range(4):
                dst = arena[:, 5 * 4096:6 * 4096]
                dst = bass.AP(tensor=dst.tensor, offset=dst[c:c + 1].offset, ap=[[dst.ap[0][0] * 4, 32], [1, 4096]])
                sp.dma_start(dst, src).then_inc(L_in, 16)
            sp.wait_ge(T_solved, 1)
            sp.dma_start(t["scratch_T"].rearrange("h c (a b) i -> (h c a) b i", a=4), Tsol).then_inc(T_out, 16)
            sp.wait_ge(T_out, 16)
            for c in range(2):
                r = slice(CH * c, CH * c + CH)
                sp.dma_start(LT[r], t["scratch_T"].rearrange("h (t c) j i -> c j h t i", c=2)[c]).then_inc(T_in, 16)

        def dve_solve(dve):
            v = nc.vector
            dve.wait_ge(L_in, 16 * 5)
            for q in range(4):
                J = 16 * (q + 1)
                tmp = tmp_solve[:, 0:16 * J].rearrange("p (c j) -> p c j", c=16)
                with dve.Fori(16 * q, 16 * q + 16) as i:
                    row = Lsys[:, 0:J, ds(i, 1)].rearrange("p j o -> p o j").to_broadcast([P, 16, J])
                    v.tensor_tensor(tmp, Tsol[:, :, 0:J], row, ALU.mult)
                    dve.drain()
                    v.reduce_sum(red, tmp, AX_X)
                    dve.drain()
                    x = Tsol[:, :, ds(i, 1)]
                    v.tensor_tensor(x, x, red.rearrange("p (c o) -> p c o", o=1), ALU.subtract)
                    dve.drain()
            dve.drain().then_inc(T_solved, 1)

        TT_h, AT_h = W[:, 512:768], W[:, 1216:1472]
        kdec = W[:, 0:512]
        S_, VN = W[:, 1472:1600], W[:, 1600:1728]
        egl_h = W[:, 1728:1732]
        scal = W[:, 1732:1738]
        kbg, vbr = st[3], st[5]
        scan_clear = sem("scan_clear")
        qdec, nw = st[6], st[7]

        def act_scan(act):
            act.drain()
            act.wait_ge(T_in, 32)
            act.wait_ge(edec_done, 1)
            act.wait_ge(scan_clear, 1)
            with act.Fori(0, GH) as h:
                loop_wait(act, oh_kept, h + 1)
                nc.scalar.copy(kh.rearrange("p (o n) -> p o n", o=1), conv[:, ds(8 + h, 1), :])
                nc.scalar.copy(vh.rearrange("p (o n) -> p o n", o=1), conv[:, ds(16 + h, 1), :])
                for c in range(2):
                    r = slice(CH * c, CH * c + CH)
                    nc.scalar.copy(TT_h[r].rearrange("p (o t n) -> p o t n", o=1, t=TT)[:, :, :, CH * c:CH * c + CH],
                                   LT[r, ds(h, 1), :, :])
                nc.scalar.copy(AT_h.rearrange("p (o t n) -> p o t n", o=1, t=TT), at_all[:, ds(h, 1), :, :])
                nc.scalar.copy(egl_h, egl[:, ds(4 * h, 4)])
                for k, x in enumerate((ebeta, edec, beta)):
                    last = nc.scalar.copy(scal[:, 2 * k:2 * k + 2].rearrange("p (t o) -> p t o", o=1), x[:, :, ds(h, 1)])
                last.then_inc(h2_staged, 1)
                act.wait_ge(w_ready, h + 1)
                nc.scalar.mul(nw, A(1, 0, T), -1.0).then_inc(w_kept, 1)
                for c in range(NCH):
                    r = slice(CH * (c % 2), CH * (c % 2) + CH)
                    act.wait_ge(vnew_ready, NCH * h + c + 1)
                    nc.scalar.copy(VN[r], A(2, 0, P)[r]).then_inc(vnew_kept, 1)
                loop_wait(act, step_ready, NCH * h + NCH)
                nc.scalar.copy(o_all[:, ds(h, 1), :], bank[0][:, 0:T].rearrange("p (o n) -> p o n", o=1)).then_inc(oh_kept, 1)

        def pe_scan(pe):
            with pe.Fori(0, GH) as h:
                pe.wait_ge(h2_staged, h + 1)
                for f in range(TT):
                    r = slice(P * f, P * f + P)
                    nc.tensor.transpose(A(0, P * f, P), kh[:, r], ident)
                    last = nc.tensor.transpose(A(0, 256 + P * f, P), vh[:, r], ident)
                last.then_inc(rows_ready, 1)
                pe.wait_ge(rows_kept, h + 1)
                for f in range(TT):
                    last = nc.tensor.matmul(A(1, P * f, P), kbg[:, P * f:P * f + P], TT_h[:, P * f:P * f + P],
                                            start=True, stop=True)
                last.then_inc(w_ready, 1)
                pe.wait_ge(w_kept, h + 1)
                for c in range(NCH):
                    r = slice(CH * (c % 2), CH * (c % 2) + CH)
                    f = c // 2
                    nc_last = nc.tensor.matmul(A(2, 0, P)[r], TT_h[:, CH * c:CH * c + CH], vbr[:, P * f:P * f + P],
                                               start=True, stop=c == 0)
                    if c:
                        pe.wait_ge(S_ready, (NCH - 1) * h + c)
                        nc_last = nc.tensor.matmul(A(2, 0, P)[r], nw[:, CH * c:CH * c + CH], S_, start=False, stop=True)
                    nc_last.then_inc(vnew_ready, 1)
                    o = bank[0][:, CH * c:CH * c + CH]
                    if c:
                        nc.tensor.matmul(o, S_, qdec[:, CH * c:CH * c + CH], start=True, stop=False)
                    pe.wait_ge(vnew_kept, NCH * h + c + 1)
                    last = nc.tensor.matmul(o, VN, AT_h[:, CH * c:CH * c + CH], start=c == 0, stop=True)
                    if c < NCH - 1:
                        last = nc.tensor.matmul(A(3, 0, P), kdec[:, P * c:P * c + P], VN, start=True, stop=True)
                    last.then_inc(step_ready, 1)

        def dve_scan(dve):
            v = nc.vector
            v.nop().then_inc(oh_kept, 1)
            v.memset(W[:, 0:768], 0.0)
            v.memset(VN, 0.0)
            dve.drain().then_inc(scan_clear, 1)
            Eg3 = tiles(EGb)
            with dve.Fori(0, GH) as h:
                dve.wait_ge(h2_staged, h + 1)
                v.scalar_tensor_tensor(qdec, conv[:, ds(h, 1), :].rearrange("p o n -> p (o n)"), SCALE,
                                       Eg3[:, ds(h, 1), :].rearrange("p o n -> p (o n)"), ALU.mult, ALU.mult)
                dve.wait_ge(rows_ready, h + 1)
                for f in range(TT):
                    r = slice(P * f, P * f + P)
                    v.tensor_scalar(kbg[:, r], A(0, P * f, P), scal[:, f:f + 1], None, ALU.mult)
                    for c in range(2):
                        half = slice(CH * c, CH * c + CH)
                        at = P * (2 * f + c)
                        v.tensor_scalar(kdec[half, at:at + P], A(0, P * f, P)[half], scal[half, 2 + f:3 + f], None, ALU.mult)
                    v.tensor_scalar(vbr[:, r], A(0, 256 + P * f, P), scal[:, 4 + f:5 + f], None, ALU.mult)
                dve.drain().then_inc(rows_kept, 1)
                for c in range(NCH - 1):
                    dve.wait_ge(step_ready, NCH * h + c + 1)
                    if c == 0:
                        v.tensor_copy(S_, A(3, 0, P)).then_inc(S_ready, 1)
                    else:
                        v.scalar_tensor_tensor(S_, S_, egl_h[:, c:c + 1], A(3, 0, P), ALU.mult, ALU.add).then_inc(S_ready, 1)
                    dve.drain()

        def act_ya(act):
            act.drain()
            nc.scalar.activation(B(0, 0, 2048), B(4, 2048, 2048), ACT.Square).then_inc(hsq_ready, 1)
            act_head_roots(act, 1, B(0, 2048, 2048), 4, 1.0 / DH)

        def dve_ya(dve):
            v = nc.vector
            dve.wait_ge(hms_kept, 12)
            v.reciprocal(B(0, 2048, 2048), B(0, 2048, 2048))
            dve.drain()
            v.scalar_tensor_tensor(B(4, 2048, 2048), B(4, 2048, 2048), col("o_norm"), B(0, 2048, 2048), ALU.mult, ALU.mult)
            dve.drain()
            wait_drained(dve, "za")
            v.tensor_tensor(B(4, 2048, 2048), B(4, 2048, 2048), B(1, 2048, 2048), ALU.mult).then_inc(ya_ready, 1)

        vb_row = B(3, 2048, 2048).rearrange("p (t n) -> p t n", t=TT)
        bias = B(2, 0, 3072).rearrange("p (h n) -> p h n", h=GH)
        yb_all = tiles(B(5, 0, 2048))
        flip, causal_flip = B(2, 3072, P), B(2, 3072 + P, P)
        onehot = W[0:32, 0:512]
        rel = W[0:32, 512:520]
        by_dist = W[0:GH, 1024:1536]
        rel_in = sem("rel_in")
        rel_ready = sem("rel_ready")
        rel_kept = sem("rel_kept")
        rel_out = sem("rel_out")
        bias_in = sem("bias_in")
        bias_ready = sem("bias_ready")
        qkb_ready = sem("qkb_ready")
        yb_ready = sem("yb_ready")
        mix_ready = sem("mix_ready")
        mSS, mPP, mPT = W[:, 0:1024], W[:, 1024:2048], B(5, 2048, 1024)

        def sp_bias(sp):
            sp.wait_ge(oh_kept, GH + 1)
            sp.dma_start(onehot, t["onehot"]).then_inc(rel_in, 16)
            sp.dma_start(rel, t["rel_bias"]).then_inc(rel_in, 16)
            sp.wait_ge(rel_kept, 1)
            sp.dma_start(t["scratch_R"], by_dist).then_inc(rel_out, 16)
            sp.wait_ge(rel_out, 16)
            sp.wait_ge(hms_kept, 20)
            R = t["scratch_R"]
            sp.dma_start(B(2, 3072, 2 * P), t["flips"]).then_inc(bias_in, 16)
            for f, first, n in ((0, 0, P), (1, P, T)):
                src = bass.AP(tensor=R.tensor, offset=P - P * f, ap=[[1, P], [512, GH], [1, n]])
                sp.dma_start(bias[:, :, first:first + n], src).then_inc(bias_in, 16)

        def pe_bias(pe):
            pe.wait_ge(rel_in, 32)
            nc.tensor.matmul(bank[0][0:GH, :], rel, onehot, start=True, stop=True).then_inc(rel_ready, 1)

        def act_bias(act):
            act.wait_ge(rel_ready, 1)
            nc.scalar.copy(by_dist, bank[0][0:GH, :]).then_inc(rel_kept, 1)

        def act_qkb(act):
            act.wait_ge(ya_ready, 1)
            drain_to(act, "qkb", tiles(B(0)))

            def body(i, k):
                s = product_ready(act, "vb", i, k)
                nc.scalar.copy(vb_row[:, :, SLOT_COLS * k:SLOT_COLS * k + SLOT_COLS],
                               bank[s][:].rearrange("p (t n) -> p t n", t=TT)).then_inc(slot_free[s], 1)
            steps(act, "vb", body)
            act.drain()
            nc.scalar.activation(B(2), B(0), ACT.Square).then_inc(hsq_ready, 1)
            act_head_roots(act, 2, B(5), 8, 1.0 / DH)

        def dve_qkb(dve):
            v = nc.vector
            dve.wait_ge(hms_kept, 20)
            v.reciprocal(B(5), B(5))
            dve.drain()
            for k, name in ((0, "q_norm"), (1, "k_norm")):
                r = B(0, 2048 * k, 2048)
                v.scalar_tensor_tensor(r, r, col(name), B(5, 2048 * k, 2048), ALU.mult, ALU.mult)
            dve.drain()
            v.tensor_scalar(B(0, 0, 2048), B(0, 0, 2048), SCALE, None, ALU.mult)
            dve.wait_ge(bias_in, 48)
            v.tensor_tensor(bias[:, :, 0:P], bias[:, :, 0:P], rep(causal_flip, GH), ALU.add)
            v.tensor_tensor(bias[:, :, 2 * P:3 * P], bias[:, :, 2 * P:3 * P], rep(causal_flip, GH), ALU.add)
            dve.drain().then_inc(qkb_ready, 1)

        MB = [(g, f) for g in range(2) for f in range(TT)]
        MB0 = ATT * KV

        def act_moba(act):
            for u, (g, f) in enumerate(MB):
                nk = P * (f + 1)
                act.wait_ge(s_shifted, MB0 + u + 1)
                nc.scalar.activation(mPP[:, 0:4 * nk], mSS[:, 0:4 * nk], ACT.Exp).then_inc(e_ready, 1)
                act.wait_ge(pT_ready, MB0 + u + 1)
                nc.scalar.copy(mPT[:, 0:512], A(2)) if f == 0 else None
                if f == 0:
                    act.drain().then_inc(pT_kept, 1)
                else:
                    nc.scalar.copy(mPT2[:, 0:1024], aux[:, 1024:2048]).then_inc(pT_kept, 1)

        mPT2 = B(5, 2048, 1024)

        def pe_moba(pe):
            pe.wait_ge(qkb_ready, 1)
            q3, k3 = tiles(B(0, 0, 2048)), tiles(B(0, 2048, 2048))
            for u, (g, f) in enumerate(MB):
                nk = P * (f + 1)
                for h in range(4):
                    nc.tensor.matmul(aux[:, nk * h:nk * h + nk], q3[:, 4 * g + h, P * f:P * f + P],
                                     k3[:, 4 * g + h, 0:nk], start=True, stop=False)
                    last = nc.tensor.matmul(aux[:, nk * h:nk * h + nk], flip,
                                            bias[:, 4 * g + h, P * f:P * f + nk], start=False, stop=True)
                last.then_inc(s_ready, 1)
                pe.wait_ge(p_ready, MB0 + u + 1)
                pe.wait_ge(o_used, MB0 + u + 1)
                for kt in range(f + 1):
                    for h in range(4):
                        at = nk * h + P * kt
                        last = nc.tensor.transpose(A(2 + kt, P * h, P), mPP[:, at:at + P], ident)
                last.then_inc(pT_ready, 1)
                pe.wait_ge(pT_kept, MB0 + u + 1)
                for h in range(4):
                    hh = 4 * g + h
                    for kt in range(f + 1):
                        last = nc.tensor.matmul(A(2, P * h, P), vb_row[:, kt, P * hh:P * hh + P],
                                                mPT[:, 512 * kt + P * h:512 * kt + P * h + P], start=kt == 0, stop=kt == f)
                last.then_inc(o_ready, 1)

        def dve_moba(dve):
            v = nc.vector
            for u, (g, f) in enumerate(MB):
                nk = P * (f + 1)
                s3 = mSS[:, 0:4 * nk].rearrange("p (h n) -> p h n", h=4)
                p3 = mPP[:, 0:4 * nk].rearrange("p (h n) -> p h n", h=4)
                dve.wait_ge(s_ready, MB0 + u + 1)
                scores = aux[:, 0:4 * nk].rearrange("p (h n) -> p h n", h=4)
                v.reduce_max(mx, scores, AX_X)
                dve.drain()
                v.tensor_tensor(s3, scores, bc(mx, nk), ALU.subtract).then_inc(s_shifted, 1)
                dve.wait_ge(e_ready, MB0 + u + 1)
                v.reduce_sum(rc, p3, AX_X)
                dve.drain()
                v.reciprocal(rc, rc)
                dve.drain()
                v.tensor_tensor(p3, p3, bc(rc, nk), ALU.mult).then_inc(p_ready, 1)
                dve.wait_ge(o_ready, MB0 + u + 1)
                v.tensor_copy(yb_all[:, 4 * g:4 * g + 4, P * f:P * f + P],
                              A(2).rearrange("p (h n) -> p h n", h=4)).then_inc(o_used, 1)

        def dve_mix(dve):
            v = nc.vector
            wait_drained(dve, "ga")
            v.tensor_tensor(B(0), B(0), B(2), ALU.mult)
            wait_drained(dve, "gb")
            v.tensor_tensor(B(1), B(1), B(4), ALU.mult)
            dve.drain()
            v.tensor_tensor(B(0), B(0), B(1), ALU.add).then_inc(mix_ready, 1)

        gate_all = arena[:, 0:FF * 2].rearrange("p (j n) -> p j n", n=T)
        up_all = arena[:, FF * 2:FF * 4].rearrange("p (j n) -> p j n", n=T)
        ffn_ready = sem("ffn_ready")

        def halves(w):
            view = w.rearrange("(a j p) n -> a p j n", a=2, p=P)

            def src(i, k):
                at = P * (k // 2)
                at = ds(2 * P * i + at, P)
                return (lambda slot: slot[:, 0:KF // 2 * P].rearrange("p (j n) -> p j n", n=P)), view[k % 2][:, :, at]
            return src

        def pe_down(pe):
            pe.wait_ge(ffn_ready, 1)
            with pe.Fori(0, COUNT["down"] // 4) as i:
                for f in range(2):
                    own = BASE["down"] + 2 * f + 1
                    wait_free(pe, own, i)
                    for a in range(2):
                        n = BASE["down"] + 2 * f + a
                        wait_landed(pe, n, i)
                        w = ring[:, n % RING, 0:KF // 2 * P].rearrange("p (j n) -> p j n", n=P)
                        for j in range(KF // 2):
                            last = nc.tensor.matmul(bank[own % RING][:, 0:T], w[:, j, :],
                                                    gate_all[:, KF // 2 * a + j, :],
                                                    start=a == 0 and j == 0, stop=a == 1 and j == KF // 2 - 1)
                        last.then_inc(products if a else slot_free[n % RING], 1)

        def act_down(act):
            with act.Fori(0, COUNT["down"] // 4) as i:
                for f in range(2):
                    own = (BASE["down"] + 2 * f + 1) % RING
                    loop_wait(act, products, 2 * i + PBASE["down"] + f + 1)
                    nc.scalar.copy(hT[:, ds(2 * i + f, 1), :],
                                   bank[own][:, 0:T].rearrange("p (o n) -> p o n", o=1)).then_inc(slot_free[own], 1)

        def dve_ffn(dve):
            wait_drained(dve, "up")
            for k in range(4):
                n = FF * 2 // 4
                last = nc.vector.tensor_tensor(arena[:, n * k:n * k + n], arena[:, n * k:n * k + n],
                                               arena[:, FF * 2 + n * k:FF * 2 + n * k + n], ALU.mult)
            last.then_inc(ffn_ready, 1)

        locals_of = dict(arena=arena, E=E, W=W, hT=hT, xT=xT, mod=mod, small=small, rstd=rstd)

        block = ctx.enter_context(nc.Block())

        @block.sync
        def _(sp):
            sp_params(sp)
            sp_ssm_loads(sp)
            if stages >= 1:
                mod_cols = cols_of(t["mod_w"])
                stream_mod0(sp, mod_cols)
                stream_mixed(sp, "u", cols_of(t["ssm_w_in"]), mod_cols)
                stream_mixed(sp, "z", cols_of(t["ssm_w_in"], D), mod_cols)
                stream_mixed(sp, "glu", cols_of(t["ssm_w_glu"]), mod_cols)
                stream(sp, "out", cols_of(t["ssm_w_out"]))
            if stages >= 2:
                stream(sp, "kv", cols_of(t["w_kv"]))
                stream(sp, "kvrow", cols_of(t["w_kv"], 2048))
                w1 = t["cmp_w1"].rearrange("k (l d) h -> k d l h", d=P)
                stream(sp, "cmp", lambda i, k: ((lambda slot: slot.rearrange("p (l h) -> p l h", h=P)), w1[k]))
                stream(sp, "q", cols_of(t["w_qg"]))
                stream(sp, "zn", cols_of(t["w_qg"], D + 48))
                stream(sp, "o", cols_of(t["w_o"]))
            if stages >= 3:
                stream(sp, "gdn", cols_of(t["w_in_2"]))
                stream(sp, "za", cols_of(t["w_in_2"], 3072))
                sp_solve(sp)
            if stages >= 4:
                stream(sp, "qkb", cols_of(t["w_in_2"], 4112))
                stream(sp, "vb", cols_of(t["w_in_2"], 6160))
                sp_bias(sp)
                stream(sp, "bra", cols_of(t["w_branch_gdn"], 0, 8))
                stream(sp, "brb", cols_of(t["w_branch_moba"], 0, 8))
                stream(sp, "ga", cols_of(t["w_in_2"], 7184))
                stream(sp, "gb", cols_of(t["w_in_2"], 9232))
                stream(sp, "out2", cols_of(t["w_out_2"]))
            if stages >= 5:
                stream(sp, "gate", cols_of(t["w_ffn_gate"]))
                stream(sp, "up", cols_of(t["w_ffn_up"]))
                stream(sp, "down", halves(t["w_ffn_down"]))
            last_x = {1: 2, 2: 3, 3: 4, 4: 5, 5: 6}[min(stages, 5)]
            sp.wait_ge(x_ready, last_x)
            if stages == 3:
                sp.wait_ge(ya_ready, 1)
            if dump:
                for name, ap in dump(locals_of).items():
                    sp.dma_start(t[name], ap).then_inc(stored, 16)
                sp.wait_ge(stored, 16 * len(dump(locals_of)))
            sp.dma_start(t["out"], xT[:]).then_inc(stored, 16)
            sp.wait_ge(stored, 16 * (1 + (len(dump(locals_of)) if dump else 0)))


        @block.tensor
        def _(pe):
            if stages >= 1:
                pe_ssm_params(pe)
                pe_mod0(pe)
                pe_mean_square(pe, 0, B(1))
                pe.wait_ge(h_ready, 1)
                dense(pe, "u", hT)
                dense(pe, "z", hT)
                pe_ssm(pe)
                pe.wait_ge(y_kept, SBLOCKS + 1)
                dense(pe, "glu", u_all)
                pe.wait_ge(glu_ready, 1)
                dense(pe, "out", tiles(B(2)))
            if stages >= 2:
                pe_mean_square(pe, 1, B(1))
                pe.wait_ge(h_ready, 2)
                dense(pe, "kv", tiles(B(0)))
                dense_rows(pe, "kvrow", tiles(B(0)))
                pe_cmp(pe)
                pe.wait_ge(h_ready, 3)
                dense(pe, "q", hT)
                pe_gates(pe)
                dense(pe, "zn", hT)
                pe_attend(pe)
                pe.wait_ge(att_ready, 1)
                dense(pe, "o", tiles(B(1)))
            if stages >= 3:
                pe_mean_square(pe, 2, B(0))
                pe_mean_square(pe, 3, B(0))
                pe.wait_ge(h_ready, 4)
                dense(pe, "gdn", hT)
                dense(pe, "za", hT)
                pe_beta(pe)
                pe_head_squares(pe, 0, B(0), 8)
                pe_beta_sums(pe)
                pe_heads(pe)
                pe_scan(pe)
                pe_head_squares(pe, 1, B(0, 0, 2048), 4)
            if stages >= 4:
                dense(pe, "qkb", hT)
                dense_rows(pe, "vb", hT)
                pe_head_squares(pe, 2, B(2), 8)
                pe_bias(pe)
                pe_moba(pe)
                pe.wait_ge(ya_ready, 1)
                dense(pe, "bra", o_all, 8)
                pe.wait_ge(o_used, MB0 + len(MB) + 1)
                dense(pe, "brb", yb_all, 8)
                dense(pe, "ga", hT)
                dense(pe, "gb", hT)
                pe.wait_ge(mix_ready, 1)
                dense(pe, "out2", tiles(B(0)))
            if stages >= 5:
                pe_mean_square(pe, 4, B(0))
                pe.wait_ge(h_ready, 5)
                dense(pe, "gate", hT)
                dense(pe, "up", hT)
                pe_down(pe)

        @block.scalar
        def _(act):
            act_start(act)
            if stages >= 1:
                act_ssm_params(act)
                act_ssm_transposed(act)
                act_mean_square(act, 0, B(1))
                drain_to(act, "u", u_all)
                drain_to(act, "z", z_all, ACT.Silu)
                act.nop().then_inc(y_kept, 1)
                act_ssm(act)
                act_glu(act)
                drain_to(act, "out", tiles(B(3)))
            if stages >= 2:
                act_mean_square(act, 1, B(1))
                act_kv(act)
                act_cmp(act)
                drain_to(act, "q", q_all, ACT.Copy, SCALE)
                act_gates(act)
                drain_to(act, "zn", zn, ACT.Silu)
                act_attend(act)
                drain_to(act, "o", tiles(B(2)))
            if stages >= 3:
                act_mean_square(act, 2, B(0))
                act_mean_square(act, 3, B(0))
                drain_to(act, "gdn", raw)
                drain_to(act, "za", za, ACT.Silu)
                act_beta(act)
                act_conv(act)
                act_head_roots(act, 0, B(4), 8, 1.0)
                act_beta_sums(act)
                act_heads(act)
                act_scan(act)
                act_ya(act)
            if stages >= 4:
                act_qkb(act)
                act_bias(act)
                act_moba(act)
                drain_to(act, "bra", tiles(B(0)))
                drain_to(act, "brb", tiles(B(1)))
                drain_to(act, "ga", tiles(B(2)), ACT.Sigmoid)
                drain_to(act, "gb", tiles(B(4)), ACT.Sigmoid)
                drain_to(act, "out2", tiles(B(2)))
            if stages >= 5:
                act_mean_square(act, 4, B(0))
                drain_to(act, "gate", gate_all, ACT.Silu)
                drain_to(act, "up", up_all)
                act_down(act)

        @block.vector
        def _(dve):
            dve_start(dve)
            if stages >= 1:
                dve_ssm_params(dve)
                dve.wait_ge(c_ready, 1)
                dve_mods(dve, "mod0")
                dve_norm0(dve)
                dve_mods(dve, "u")
                dve_mods(dve, "z")
                dve_ssm(dve)
                dve_mods(dve, "glu")
                dve_glu(dve)
                dve_residual(dve, "out", tiles(B(3)), GT0)
            if stages >= 2:
                dve_norm1(dve)
                dve_cmp_in(dve)
                dve_cmp(dve)
                dve_attend(dve)
                dve_residual(dve, "o", tiles(B(2)), GT1)
            if stages >= 3:
                dve_final0(dve)
                dve_conv(dve)
                dve_beta(dve)
                dve_qk(dve)
                dve_beta_sums(dve)
                dve_heads(dve)
                dve_solve(dve)
                dve_scan(dve)
                dve_ya(dve)
            if stages >= 4:
                dve_qkb(dve)
                dve_moba(dve)
                dve_mix(dve)
                dve_residual(dve, "out2", tiles(B(2)), None)
            if stages >= 5:
                dve_rstd(dve, 4)
                dve_modulated(dve, hT[:], col("ffn_g"), None, None).then_inc(h_ready, 1)
                dve_ffn(dve)
                dve_residual(dve, "down", hT, None)


def constants():
    i = np.arange(P)
    con = {
        "ident": np.eye(P),
        "causal": np.concatenate([np.zeros((P, P)), np.where(i[None, :] <= i[:, None], 0, NEG)], 1),
        "cum": (i[:, None] // CH == i[None, :] // CH) & (i[:, None] <= i[None, :]),
        "same": i[:, None] // CH == i[None, :] // CH,
        "decay_neg": np.where((i[:, None] // CH == i[None, :] // CH) & (i[:, None] <= i[None, :]), 0, NEG),
        "strict": i[:, None] % CH < np.arange(CH)[None, :],
    }
    tok = np.arange(TT)[None, :, None] * P + i[:, None, None]
    seen = (np.arange(NCMP) * CMP_STRIDE + CMP_LEN - 1)[None, None, :] <= tok
    con["cmp_neg"] = np.where(seen, 0, NEG).reshape(P, -1)
    con["cmp_one"] = seen.reshape(P, -1)
    flips = np.concatenate([con["ident"][::-1], con["causal"][::-1, P:]], 1).astype(np.float32)
    con["iota"] = np.broadcast_to(np.arange(T), (P, T))
    con = np.concatenate([np.asarray(con[n], np.float32) for n, _ in CONSTS], 1)
    eye = np.zeros((P, 16, CH), np.float32)
    for p in range(P):
        for c in range(16):
            eye[p, c, 16 * (p % 4) + c] = 1
    dist = np.maximum(T - 1 - np.arange(512), 0)
    d = dist.astype(np.float32)
    ratio = np.log(np.maximum(d, np.float32(16)) / np.float32(16)) / np.float32(math.log(2048 / 16))
    large = np.minimum(16 + (ratio * np.float32(16)).astype(np.int32), 31)
    bucket = np.where(dist < 16, dist, large)
    onehot = (np.arange(32)[:, None] == bucket[None, :]).astype(np.float32)
    return np.ascontiguousarray(con), eye, onehot, flips


def lay_out(x):
    x = {k: np.asarray(v) for k, v in x.items()}

    def feat(v):
        return v.reshape(-1, P).T

    def states(v):
        return v[0].reshape(STILES, P, *v.shape[3:]).swapaxes(0, 1)

    packed = {
        "c": feat(x["c"]), "norm_g": feat(x["norm_g"]),
        "mod_b": feat(np.concatenate([x["mod_b"][0], x["kv_mod_b"], x["mod_b"][1]])),
        "kv_norm_g": feat(x["kv_norm_g"]), "ssm_d": feat(x["ssm_d"]), "b_glu": feat(x["ssm_b_glu"]),
        "final_g": feat(x["final_norm_g"]), "mix_g": feat(x["norm_mix_w_2"]), "ffn_g": feat(x["norm_ffn_w_2"]),
        "conv_w": x["conv_w_2"][0].reshape(4, 24, P).transpose(2, 1, 0).reshape(P, 96),
        "q_norm": feat(x["q_norm_w_2"]), "k_norm": feat(x["k_norm_w_2"]), "o_norm": feat(x["gdn_o_norm_w_2"]),
        "cmp_b1": x["cmp_b1"].T, "cmp_b2": x["cmp_b2"].T,
        "pe": x["cmp_pe"].transpose(2, 0, 1).reshape(P, 64),
        "lam_re": states(x["ssm_lam_re"]), "lam_im": states(x["ssm_lam_im"]),
    }
    con, eye, onehot, flips = constants()
    w_qg, w_in = x["nsa_w_qg"][0], x["w_in_2"][0]
    kv = x["w_kv"].reshape(D, 6, 512)[:, [0, 1, 2, 4, 3, 5]].reshape(D, 3072)

    def c_states(v):
        return v[0].swapaxes(1, 2).reshape(STILES, P, CG).swapaxes(0, 1).reshape(P, 1024)

    out = {
        "cols": np.concatenate([packed[n] for n, _ in COLS], 1), "con": con, "eye": eye, "onehot": onehot, "flips": flips,
        "xT": x["x"][0].T.reshape(KD, P, T).swapaxes(0, 1),
        "w_gate": w_qg[:, D:D + 48], "w_beta": w_in[:, 4096:4112],
        "cmp_w2": x["cmp_w2"], "cmp_b2v": x["cmp_b2"][1:2],
        "gdn_rows": np.concatenate([x["a_log_2"], x["dt_bias_2"]], 1),
        "log_step": x["ssm_log_step"][0].reshape(STILES, 2).T,
        "mod_w": np.concatenate([x["mod_w"][0], x["kv_mod_w"], x["mod_w"][1]], 1),
        "ssm_w_in": x["ssm_w_in"][0], "ssm_w_glu": x["ssm_w_glu"][0], "ssm_w_out": x["ssm_w_out"][0],
        "b_re": states(x["ssm_b_re"]).reshape(P, 1024), "b_im": states(x["ssm_b_im"]).reshape(P, 1024),
        "ssm_c_re": c_states(x["ssm_c_re"]), "ssm_c_im": c_states(x["ssm_c_im"]),
        "w_kv": kv, "cmp_w1": x["cmp_w1"], "w_qg": w_qg, "w_o": x["nsa_w_o"][0], "w_in_2": w_in,
        "rel_bias": x["rel_bias_2"], "w_branch_gdn": x["w_branch_gdn_2"][0], "w_branch_moba": x["w_branch_moba_2"][0],
        "w_out_2": x["w_out_2"][0], "w_ffn_gate": x["w_ffn_gate_2"][0], "w_ffn_up": x["w_ffn_up_2"][0],
        "w_ffn_down": x["w_ffn_down_2"][0],
    }
    return {k: np.ascontiguousarray(v) for k, v in out.items()}


SCRATCH = {"scratch_L": (GH, NCH, CH, CH), "scratch_T": (GH, NCH, CH, CH), "scratch_R": (GH, 512)}


def program(nc, arrays, stages=99, dump=None, extra=()):
    t = {n: nc.dram_tensor("in_" + n, a.shape, F32, kind="ExternalInput").ap() for n, a in arrays.items()}
    t |= {n: nc.dram_tensor(n, s, F32, kind="Internal").ap() for n, s in SCRATCH.items()}
    t["out"] = nc.dram_tensor("out_0", (P, KD, T), F32, kind="ExternalOutput").ap()
    for n, s in extra:
        t[n] = nc.dram_tensor(n, s, F32, kind="ExternalOutput").ap()
    build(nc, t, stages, dump)


def kernel(**inputs):
    import concourse.bacc as bacc
    from concourse.bass_utils import run_bass_kernel_spmd

    nc = bacc.Bacc("TRN2", target_bir_lowering=False, num_devices=1, dynamic_dma_scratch_size=DMA_SCRATCH)
    arrays = lay_out(inputs)
    program(nc, arrays)
    got = run_bass_kernel_spmd(nc, [{"in_" + n: a for n, a in arrays.items()}], core_ids=[0])
    out = got.results[0]["out_0"]
    return np.ascontiguousarray(out.transpose(2, 1, 0).reshape(1, T, D))
```

```python
import math
from contextlib import ExitStack

import numpy as np

import concourse.bass as bass
import concourse.mybir as mybir

F32 = mybir.dt.float32
ALU = mybir.AluOpType
ACT = mybir.ActivationFunctionType
AX_X = mybir.AxisListType.X
ds = bass.ds

P = 128
T = 256
TT = T // P
D = 2048
KD = D // P
QUARTER = KD // 4
RING = 4
SLOT_COLS = 256
SLOT = KD * SLOT_COLS
G, N, CG = 128, 64, 16
STILES = G * N // P
SBLOCKS = STILES // 4
HEADS, KV, HPG, DH = 16, 4, 4, 128
NCMP, CMP_LEN, CMP_STRIDE = 15, 32, 16
GH, CH = 8, 64
NCH = T // CH
FF = 5632
KF = FF // P
DMA_SCRATCH = 64
EPS = 1e-6
NEG = -1e30
SCALE = DH ** -0.5
ROUND = 1.5 * 2.0 ** 23
TWO_PI = 2.0 * math.pi
TURN = float(np.nextafter(np.float32(TWO_PI), np.float32(0)))
TWO_PI_HI = 6.28125
TWO_PI_LO = TWO_PI - TWO_PI_HI

COLS = [("c", 16), ("norm_g", 32), ("mod_b", 128), ("kv_norm_g", 16), ("ssm_d", 16), ("b_glu", 16),
        ("final_g", 16), ("mix_g", 16), ("ffn_g", 16), ("conv_w", 96), ("q_norm", 1), ("k_norm", 1),
        ("o_norm", 1), ("cmp_b1", 2), ("cmp_b2", 2), ("pe", 64), ("lam_re", 64), ("lam_im", 64)]
COL = {}
for _name, _n in COLS:
    COL[_name] = (sum(n for _, n in COLS[:len(COL)]), _n)
NCOLS = sum(n for _, n in COLS)

CONSTS = [("ident", 128), ("causal", 256), ("cum", 128), ("same", 128), ("decay_neg", 128),
          ("strict", 64), ("cmp_neg", 30), ("cmp_one", 30), ("iota", 256)]
CON = {}
for _name, _n in CONSTS:
    CON[_name] = (sum(n for _, n in CONSTS[:len(CON)]), _n)
NCON = sum(n for _, n in CONSTS)

ORDER = [("mod0", 16), ("u", 24), ("z", 24), ("glu", 24), ("out", 8), ("kv", 8), ("kvrow", 4),
         ("cmp", 2), ("q", 8), ("zc", 8), ("zs", 16), ("o", 8), ("gdn", 12), ("za", 4), ("qkb", 8), ("vb", 4),
         ("ga", 8), ("gb", 4), ("gb2", 4), ("bra", 8), ("brb", 8), ("out2", 8), ("gate", 22), ("up", 22), ("down", 32)]
BASE = {}
for _name, _n in ORDER:
    BASE[_name] = sum(n for _, n in ORDER[:len(BASE)])
COUNT = dict(ORDER)
MIXED = ("u", "z", "glu")
DENSE = {n: 0 if n == "mod0" else c // 3 if n in MIXED else c // 2 if n == "down" else c for n, c in ORDER}
PBASE = {n: sum(DENSE[m] for m, _ in ORDER[:k]) for k, (n, _) in enumerate(ORDER)}
PAIRS = {"mod0": 0, "u": 8, "z": 16, "glu": 24}


def build(nc, t, stages=99, dump=None):
    ctx = ExitStack()
    with ctx:
        def sb(name, shape):
            return ctx.enter_context(nc.sbuf_tensor(name, shape, F32))

        def sem(name):
            return ctx.enter_context(nc.semaphore(name))

        ring = sb("ring", [P, RING, SLOT])
        xT = sb("xT", [P, KD, T])
        hT = sb("hT", [P, KD, T])
        arena = sb("arena", [P, 6 * 4096])
        E = sb("E", [P, 2048])
        W = sb("W", [P, 2048])
        cols = sb("cols", [P, NCOLS])
        con = sb("con", [P, NCON])
        ones = sb("ones", [P, P])
        eps = sb("eps", [P, 1])
        w_gate = sb("w_gate", [P, KD, 48])
        w_beta = sb("w_beta", [P, KD, 16])
        cmp_w2 = sb("cmp_w2", [P, 2, P])
        cmp_b2r = sb("cmp_b2r", [NCMP, P])
        gdn_rows = sb("gdn_rows", [P, 16])
        c_act = sb("c_act", [P, KD])
        mod = sb("mod", [P, 128])
        gain = sb("gain", [P, KD])
        rstd = sb("rstd", [P, T])
        small = sb("small", [P, 320])

        bank = [ctx.enter_context(nc.psum_tensor(f"bank{k}", [P, 512], F32)) for k in range(RING)]
        aux = ctx.enter_context(nc.psum_tensor("aux", [P, 2048], F32))

        def B(k, lo=0, n=4096):
            return arena[:, 4096 * k + lo:4096 * k + lo + n]

        def tiles(ap):
            return ap.rearrange("p (j n) -> p j n", n=T)

        def col(name, lo=0, n=None):
            o, m = COL[name]
            return cols[:, o + lo:o + lo + (m - lo if n is None else n)]

        def cst(name, lo=0, n=None):
            o, m = CON[name]
            return con[:, o + lo:o + lo + (m - lo if n is None else n)]

        ident = cst("ident")

        def A(k, lo=0, n=512):
            return aux[:, 512 * k + lo:512 * k + lo + n]

        def bc(ap, n):
            return ap.rearrange("p (a o) -> p a o", o=1).to_broadcast([ap.shape[0], ap.shape[1], n])

        def rep(ap, n):
            return ap.rearrange("p (o a) -> p o a", o=1).to_broadcast([ap.shape[0], n, ap.shape[1]])

        SH0, SC0, GT0, KSH, KSC, SH1, SC1, GT1 = (mod[:, 16 * k:16 * k + 16] for k in range(8))

        params_in = sem("params_in")
        weights_in = [sem(f"weights_in{k}") for k in range(RING)]
        products = sem("products")
        slot_free = [sem(f"slot_free{k}") for k in range(RING)]
        acc_ready = sem("acc_ready")
        acc_used = sem("acc_used")
        c_ready = sem("c_ready")
        ones_ready = sem("ones_ready")
        mod_ready = sem("mod_ready")
        sq_ready = sem("sq_ready")
        ms_ready = sem("ms_ready")
        std_ready = sem("std_ready")
        h_ready = sem("h_ready")
        x_ready = sem("x_ready")
        stored = sem("stored")


        def wait_free(eng, n, r):
            eng.wait_ge(slot_free[n % RING], r + n // RING + 1)

        def wait_landed(eng, n, r):
            eng.wait_ge(weights_in[n % RING], 16 * r + 16 * (n // RING + 1))

        def load(sp, n, r, src):
            dst, from_ = src
            wait_free(sp, n, r)
            sp.dma_start(dst(ring[:, n % RING, :]), from_).then_inc(weights_in[n % RING], 16)

        def stream(sp, name, src):
            steps(sp, name, lambda i, k: load(sp, BASE[name] + k, i, src(i, k)), COUNT[name])

        def stream_mod0(sp, src):
            with sp.Fori(0, COUNT["mod0"] // 8) as i:
                for k in range(8):
                    load(sp, BASE["mod0"] + k, 2 * i, src(2 * i, k))

        def stream_mixed(sp, name, src, mod_src):
            with sp.Fori(0, COUNT[name] // 12) as i:
                for k in range(4):
                    load(sp, BASE[name] + 3 * k, 3 * i, src(i, k))
                    for x in range(2):
                        load(sp, BASE[name] + 3 * k + 1 + x, 3 * i, mod_src(2 * i, 2 * PAIRS[name] + 2 * k + x))

        def cols_of(w, first=0, kd=KD):
            view = w.rearrange("(j p) n -> p j n", p=P)

            def src(i, k):
                at = first + SLOT_COLS * k
                if not isinstance(i, int):
                    at = ds(SLOT_COLS * 4 * i + at, SLOT_COLS)
                else:
                    at = slice(at, at + SLOT_COLS)
                return (lambda slot: slot[:, 0:kd * SLOT_COLS].rearrange("p (j n) -> p j n", j=kd)), view[:, :, at]
            return src

        def steps(eng, name, body, count=None):
            count = DENSE[name] if count is None else count
            if count // 4 > 1:
                with eng.Fori(0, count // 4) as i:
                    for k in range(4):
                        body(i, k)
            else:
                for k in range(count - count % 4):
                    body(0, k)
            for k in range(count - count % 4, count):
                body(0, k)

        def place(name, i, k):
            return (BASE[name] + 3 * k, 3 * i) if name in MIXED else (BASE[name] + k, i)

        def slot_ready(pe, name, i, k):
            n, r = place(name, i, k)
            wait_landed(pe, n, r)
            wait_free(pe, n, r)
            return n % RING

        def dense(pe, name, act, kd=KD, ready=None):
            def body(i, k):
                s = slot_ready(pe, name, i, k)
                w = ring[:, s, :].rearrange("p (j n) -> p j n", n=SLOT_COLS)
                for f in range(2):
                    for j in range(kd):
                        if ready and k == 0 and f == 0 and j % QUARTER == 0:
                            pe.wait_ge(ready[0], ready[1] + j // QUARTER + 1)
                        last = nc.tensor.matmul(bank[s][:, T * f:T * f + T], w[:, j, P * f:P * f + P], act[:, j, :],
                                                start=j == 0, stop=j == kd - 1)
                last.then_inc(products, 1)
                if name in SQUARES:
                    for m in ([] if k == 0 else [k - 1] if k < 3 else [2, 3]):
                        residual_squares(pe, name, i, m)
                if name in MIXED:
                    mod_columns(pe, name, i, k)
            steps(pe, name, body)

        def dense_piece(s, act, first, count):
            w = ring[:, s, :].rearrange("p (j n) -> p j n", n=SLOT_COLS)
            for m in range(first, first + count):
                f, j = m // KD, m % KD
                last = nc.tensor.matmul(bank[s][:, T * f:T * f + T], w[:, j, P * f:P * f + P], act[:, j, :],
                                        start=j == 0, stop=j == KD - 1)
            if first + count == 2 * KD:
                last.then_inc(products, 1)

        def dense_rows(pe, name, act):
            def body(i, k):
                s = slot_ready(pe, name, i, k)
                w = ring[:, s, :].rearrange("p (j n) -> p j n", n=SLOT_COLS)
                for f in range(TT):
                    for j in range(KD):
                        last = nc.tensor.matmul(bank[s][:, T * f:T * f + T], act[:, j, P * f:P * f + P], w[:, j, :],
                                                start=j == 0, stop=j == KD - 1)
                last.then_inc(products, 1)
            steps(pe, name, body)

        acc = E[:, 1024:2048].rearrange("p (b x n) -> p b x n", b=2, x=2)
        DIRECT = {"mod0": 4, "u": 0, "z": 0, "glu": 0}
        MOD_BANK = {"mod0": 2, "u": 3, "z": 2, "glu": 3}

        def mod_pair(dve, name, i, k, slots):
            dve.wait_ge(acc_used, 4 * i + PAIRS[name] + k + 1)
            for n, r in slots:
                wait_landed(dve, n, r)
            s0, s1 = (n % RING for n, _ in slots)
            rows = KD - DIRECT[name]
            for j in range(rows):
                at = slice(SLOT_COLS * j, SLOT_COLS * j + SLOT_COLS)
                for x in ([slice(0, 2)] if s1 == s0 + 1 else [slice(0, 1), slice(1, 2)]):
                    s = (s0, s1)[x.start]
                    w, a = ring[:, s:s + x.stop - x.start, at], acc[:, k % 2, x, :]
                    if j == 0:
                        nc.vector.tensor_scalar(a, w, c_act[:, j:j + 1], None, ALU.mult)
                    else:
                        nc.vector.scalar_tensor_tensor(a, w, c_act[:, j:j + 1], a, ALU.mult, ALU.add)
                if j < rows - 1:
                    dve.drain()
            dve.drain().then_inc(acc_ready, 1)
            if not DIRECT[name]:
                for s in (s0, s1):
                    nc.vector.nop().then_inc(slot_free[s], 1)

        def mod_columns(pe, name, i, k):
            def column(x, f, off):
                at = 512 * MOD_BANK[name] + off + 4 * k + 2 * x + f
                return aux[:, slice(at, at + 1) if isinstance(i, int) else ds(16 * i + at, 1)]

            slots = [(BASE[name] + 2 * k + x, 2 * i) for x in range(2)]
            if DIRECT[name]:
                for x, (n, r) in enumerate(slots):
                    wait_landed(pe, n, r)
                    w = ring[:, n % RING, :].rearrange("p (j n) -> p j n", n=SLOT_COLS)
                    for f in range(2):
                        for j in range(KD - DIRECT[name], KD):
                            nc.tensor.matmul(column(x, f, 32), w[:, j, P * f:P * f + P], c_act[:, j:j + 1],
                                             start=j == KD - DIRECT[name], stop=j == KD - 1)
            pe.wait_ge(acc_ready, 4 * i + PAIRS[name] + k + 1)
            for x in range(2):
                for f in range(2):
                    last = nc.tensor.matmul(column(x, f, 0), acc[:, k % 2, x, P * f:P * f + P], ones[:, 0:1],
                                            start=True, stop=True)
                if DIRECT[name]:
                    last.then_inc(slot_free[slots[x][0] % RING], 1)
                    last = None
            if last is None:
                pe.drain().then_inc(acc_used, 1)
            else:
                last.then_inc(acc_used, 1)

        def dve_mods(dve, name):
            with dve.Fori(0, 2) as i:
                for k in range(4):
                    if name == "mod0":
                        slots = [(BASE[name] + 2 * k + x, 2 * i) for x in range(2)]
                    else:
                        slots = [(BASE[name] + 3 * k + 1 + x, 3 * i) for x in range(2)]
                    mod_pair(dve, name, i, k, slots)
            dve.wait_ge(acc_used, PAIRS[name] + 8 + 2)
            at = 4 * PAIRS[name]
            nc.vector.tensor_tensor(mod[:, at:at + 32], A(MOD_BANK[name], 0, 32), col("mod_b", at, 32), ALU.add)
            dve.drain()
            if DIRECT[name]:
                nc.vector.tensor_tensor(mod[:, at:at + 32], mod[:, at:at + 32], A(MOD_BANK[name], 32, 32), ALU.add)
                dve.drain()

        def product_ready(act, name, i, k):
            act.wait_ge(products, 4 * i + PBASE[name] + k + 1)
            act.wait_ge(params_in, 16 * N_PARAMS)
            n, r = place(name, i, k)
            return n % RING

        def loop_wait(act, sem, value):
            act.wait_ge(sem, value)
            act.wait_ge(params_in, 16 * N_PARAMS)

        def drain_to(act, name, dst, func=ACT.Copy, scale=1.0):
            def body(i, k):
                s = product_ready(act, name, i, k)
                at = slice(2 * k, 2 * k + 2) if isinstance(i, int) else ds(8 * i + 2 * k, 2)
                nc.scalar.activation(dst[:, at, :], bank[s][:].rearrange("p (f n) -> p f n", f=2), func,
                                     scale=scale).then_inc(slot_free[s], 1)
            steps(act, name, body)

        def wait_drained(eng, name):
            n = BASE[name] + COUNT[name] - (3 if name in MIXED else 1)
            eng.wait_ge(slot_free[n % RING], n // RING + 2)


        SQUARES = {"out": (1, B(1), None), "o": (9, B(0), B(3)), "out2": (17, B(1), None)}

        def act_mean_square(act, sq):
            act.wait_ge(x_ready, 1)
            nc.scalar.activation(sq, xT[:].rearrange("p j n -> p (j n)"), ACT.Square).then_inc(sq_ready, 1)
            act_root(act, 0)

        def act_root(act, k):
            act.wait_ge(ms_ready, k + 1)
            nc.scalar.activation(rstd[:], A(0, 0, T), ACT.Sqrt, scale=1.0 / D, bias=eps[:]).then_inc(std_ready, 1)

        def pe_mean_square(pe, sq):
            pe.wait_ge(sq_ready, 1)
            for j in range(KD):
                last = nc.tensor.matmul(A(0, 0, T), ones[:], sq[:, T * j:T * j + T], start=j == 0, stop=j == KD - 1)
            last.then_inc(ms_ready, 1)

        def pe_zero(name, start):
            for n in range(1 if SQUARES[name][2] is None else 2):
                last = nc.tensor.matmul(A(n, 0, T), cst("causal", 0, P), con[:, 0:T], start=start, stop=not start)
            return last

        def residual_squares(pe, name, i, k):
            first, *rooms = SQUARES[name]
            pe.wait_ge(sq_ready, 4 * i + first + k + 1)
            for n, room in enumerate(rooms):
                if room is not None:
                    for f in range(2):
                        sq = tiles(room)[:, ds(8 * i + 2 * k + f, 1), :].rearrange("p o n -> p (o n)")
                        nc.tensor.matmul(A(n, 0, T), ones[:], sq, start=False, stop=False)

        def pe_residual(pe, name, act):
            pe_zero(name, True)
            dense(pe, name, act)
            pe_zero(name, False).then_inc(ms_ready, 1)

        def act_residual(act, name, dst, k):
            first, sq, sq_gain = SQUARES[name]
            o = COL["final_g"][0]

            def body(i, k):
                s = product_ready(act, name, i, k)
                at = ds(8 * i + 2 * k, 2)
                nc.scalar.activation(dst[:, at, :], bank[s][:].rearrange("p (f n) -> p f n", f=2),
                                     ACT.Copy).then_inc(slot_free[s], 1)
                loop_wait(act, x_ready, 4 * i + first + k + 1)
                last = nc.scalar.activation(tiles(sq)[:, at, :], xT[:, at, :], ACT.Square)
                if sq_gain is not None:
                    for f in range(2):
                        at = 2 * k + f
                        last = nc.scalar.activation(tiles(sq_gain)[:, ds(8 * i + at, 1), :].rearrange("p o n -> p (o n)"),
                                                    xT[:, ds(8 * i + at, 1), :].rearrange("p o n -> p (o n)"), ACT.Square,
                                                    scale=cols[:, ds(8 * i + o + at, 1)])
                last.then_inc(sq_ready, 1)
            steps(act, name, body)
            act_root(act, k)

        def dve_rstd(dve, k):
            dve.wait_ge(std_ready, k + 1)
            nc.vector.reciprocal(rstd[:], rstd[:])
            dve.drain()

        def dve_modulated(dve, dst, g, scale, shift, r=None, signal=True):
            r = rstd[:] if r is None else r
            if scale is not None:
                nc.vector.scalar_tensor_tensor(gain[:], scale, 1.0, g, ALU.add, ALU.mult)
            for q in range(4):
                at = slice(QUARTER * q, QUARTER * q + QUARTER)
                nc.vector.tensor_tensor(dst[:, at, :], xT[:, at, :], rep(r, QUARTER), ALU.mult)
                dve.drain()
                for j in range(QUARTER * q, QUARTER * q + QUARTER):
                    if scale is not None:
                        last = nc.vector.tensor_scalar(dst[:, j, :], dst[:, j, :], gain[:, j:j + 1], shift[:, j:j + 1],
                                                       ALU.mult, ALU.add)
                    else:
                        last = nc.vector.tensor_scalar(dst[:, j, :], dst[:, j, :], g[:, j:j + 1], None, ALU.mult)
                if signal:
                    last.then_inc(h_ready, 1)
            dve.drain()

        def dve_residual(dve, name, out, gate):
            def body(i, k):
                n, r = place(name, i, k)
                dve.wait_ge(slot_free[n % RING], r + n // RING + 2)
                at = ds(8 * i + 2 * k, 2)
                if gate is None:
                    nc.vector.tensor_tensor(xT[:, at, :], xT[:, at, :], out[:, at, :], ALU.add)
                else:
                    for f in range(2):
                        at = ds(8 * i + 2 * k + f, 1)
                        x = xT[:, at, :].rearrange("p o n -> p (o n)")
                        nc.vector.scalar_tensor_tensor(x, out[:, at, :].rearrange("p o n -> p (o n)"), gate[:, at], x,
                                                       ALU.mult, ALU.add)
                dve.drain().then_inc(x_ready, 1)
            steps(dve, name, body)

        N_PARAMS = 10

        def sp_params(sp):
            for dst, src in ((cols[:], t["cols"]), (con[:], t["con"]), (xT[:], t["xT"]),
                             (w_gate[:], t["w_gate"].rearrange("(j p) n -> p j n", p=P)),
                             (w_beta[:], t["w_beta"].rearrange("(j p) n -> p j n", p=P)),
                             (cmp_w2[:], t["cmp_w2"].rearrange("k a b -> a k b")),
                             (cmp_b2r[:], t["cmp_b2v"].to_broadcast([NCMP, P])),
                             (gdn_rows[:], t["gdn_rows"].to_broadcast([P, 16])),
                             (small[0:64, 0:64], t["log_step"][0:1, :].to_broadcast([64, 64])),
                             (small[64:128, 0:64], t["log_step"][1:2, :].to_broadcast([64, 64]))):
                sp.dma_start(dst, src).then_inc(params_in, 16)

        def act_start(act):
            for k in range(RING):
                act.nop().then_inc(slot_free[k], 1)
            act.wait_ge(params_in, 16 * N_PARAMS)
            nc.scalar.activation(c_act[:], col("c"), ACT.Silu).then_inc(c_ready, 1)

        def pe_mod0(pe):
            pe.wait_ge(c_ready, 1)
            pe.nop().then_inc(acc_used, 2)
            with pe.Fori(0, 2) as i:
                for k in range(4):
                    for b in range(2):
                        pe_transposed(pe, SBLOCKS // 2 * i + 2 * k + b)
                    mod_columns(pe, "mod0", i, k)

        def dve_start(dve):
            nc.vector.memset(ones[:], 1.0)
            nc.vector.memset(eps[:], EPS)
            dve.wait_ge(params_in, 16 * N_PARAMS)
            dve.drain().then_inc(x_ready, 1)

        def dve_norm0(dve):
            dve_modulated(dve, hT[:], col("norm_g", 0, 16), SC0, SH0)

        B_RE, B_IM, C_RE, C_IM = (B(3, 1024 * k, 1024) for k in range(4))
        BB_RE, BB_IM, NC_RE, NC_IM = (B(4, 1024 * k, 1024) for k in range(4))
        BT = B(2).rearrange("p (b n) -> p b n", n=256)
        u_all, z_all = tiles(B(0)), tiles(B(1))
        hflat = hT[:].rearrange("p j n -> p (j n)")
        SIN = [hflat[:, 1024 * k:1024 * k + 1024] for k in range(2)]
        COS = [hflat[:, 2048 + 1024 * k:3072 + 1024 * k] for k in range(2)]
        PH, ROUNDED = [B(4, 0, 1024), B(3, 3072, 1024)], B(4, 1024, 1024)
        ZC = B(3, 0, 2048)
        MC, MS = B(5, 0, 2048), B(5, 2048, 2048)
        V = E[:]
        dt, mag, turns, c_re, c_im = (small[:, 64 * k:64 * k + 64] for k in range(5))
        t0, t1, t2, t3, t4 = (E[:, 64 * k:64 * k + 64] for k in range(5))
        ub = W[:, 0:256]
        bT = W[:, 256:512]
        cpad = W[:, 512:2048].rearrange("p (r k n) -> p r k n", r=3, k=4)
        bst = W[:, 0:256]
        ysum = rstd[:]

        ssm_in = sem("ssm_in")
        dt_ready = sem("dt_ready")
        arg_ready = sem("arg_ready")
        mag_ready = sem("mag_ready")
        angle_ready = sem("angle_ready")
        root_ready = sem("root_ready")
        neg_ready = sem("neg_ready")
        bb_ready = sem("bb_ready")
        spread_ready = sem("spread_ready")
        bT_ready = sem("bT_ready")
        bT_kept = sem("bT_kept")
        staged = sem("staged")
        c_staged = sem("c_staged")
        frac_ready = sem("frac_ready")
        trig_ready = sem("trig_ready")
        bu_ready = sem("bu_ready")
        bu_used = sem("bu_used")
        turned = sem("turned")
        z_scanned = sem("z_scanned")
        z_sined = sem("z_sined")
        turns_ready = sem("turns_ready")
        rounded = sem("rounded")
        y_ready = sem("y_ready")
        ysum_ready = sem("ysum_ready")
        y_kept = sem("y_kept")
        glu_ready = sem("glu_ready")
        yz_ready = sem("yz_ready")

        def sp_ssm_loads(sp):
            for dst, name in ((B_RE, "b_re"), (B_IM, "b_im"), (C_RE, "ssm_c_re"), (C_IM, "ssm_c_im")):
                sp.dma_start(dst, t[name]).then_inc(ssm_in, 16)

        def act_ssm_params(act):
            nc.scalar.activation(dt, dt, ACT.Exp).then_inc(dt_ready, 1)
            act.wait_ge(arg_ready, 1)
            nc.scalar.activation(mag, t0, ACT.Exp).then_inc(mag_ready, 1)
            act.wait_ge(angle_ready, 1)
            nc.scalar.activation(t2, t1, ACT.Sin)
            nc.scalar.activation(t3, t1, ACT.Sin, scale=0.5).then_inc(root_ready, 1)
            act.wait_ge(ssm_in, 64)
            nc.scalar.mul(NC_RE, C_RE, -1.0)
            nc.scalar.mul(NC_IM, C_IM, -1.0).then_inc(neg_ready, 1)

        def dve_ssm_params(dve):
            lr, li = col("lam_re"), col("lam_im")
            v = nc.vector
            dve.wait_ge(dt_ready, 1)
            v.tensor_tensor(t0, lr, dt, ALU.mult).then_inc(arg_ready, 1)
            v.tensor_tensor(t1, li, dt, ALU.mult)
            dve.drain()
            v.tensor_scalar(t2, t1, 1.0 / TWO_PI, ROUND, ALU.mult, ALU.add)
            dve.drain()
            v.tensor_scalar(t2, t2, ROUND, None, ALU.subtract)
            dve.drain()
            v.scalar_tensor_tensor(t1, t2, -TWO_PI_HI, t1, ALU.mult, ALU.add)
            dve.drain()
            v.scalar_tensor_tensor(t1, t2, -TWO_PI_LO, t1, ALU.mult, ALU.add)
            dve.drain()
            v.tensor_scalar(t1, t1, 3.1415925, -3.1415925, ALU.min, ALU.max)
            dve.drain()
            v.tensor_scalar(turns, t1, 1.0 / TWO_PI, None, ALU.mult).then_inc(angle_ready, 1)
            dve.wait_ge(root_ready, 1)
            dve.wait_ge(mag_ready, 1)
            v.tensor_tensor(t3, t3, t3, ALU.mult)
            v.tensor_tensor(t2, t2, mag, ALU.mult)
            dve.drain()
            v.tensor_scalar(t3, t3, -2.0, 1.0, ALU.mult, ALU.add)
            dve.drain()
            v.tensor_tensor(t3, t3, mag, ALU.mult)
            dve.drain()
            v.tensor_scalar(t3, t3, 1.0, None, ALU.subtract)
            v.tensor_tensor(t0, lr, lr, ALU.mult)
            v.tensor_tensor(t1, li, li, ALU.mult)
            dve.drain()
            v.tensor_tensor(t0, t0, t1, ALU.add)
            dve.drain()
            v.reciprocal(t0, t0)
            v.tensor_tensor(t1, t3, lr, ALU.mult)
            v.tensor_tensor(t4, t2, li, ALU.mult)
            v.tensor_tensor(c_im, t2, lr, ALU.mult)
            dve.drain()
            v.tensor_tensor(t1, t1, t4, ALU.add)
            dve.drain()
            v.tensor_tensor(c_re, t1, t0, ALU.mult)
            v.tensor_tensor(t4, t3, li, ALU.mult)
            dve.drain()
            v.tensor_tensor(c_im, c_im, t4, ALU.subtract)
            dve.drain()
            v.tensor_tensor(c_im, c_im, t0, ALU.mult)
            dve.drain()
            dve.wait_ge(ssm_in, 64)

            def g(x):
                return x.rearrange("p (a n) -> p a n", n=CG)

            tmp = MC[:, 0:1024]
            v.tensor_tensor(g(BB_RE), g(B_RE), bc(c_re, CG), ALU.mult)
            v.tensor_tensor(g(tmp), g(B_IM), bc(c_im, CG), ALU.mult)
            v.tensor_tensor(g(BB_IM), g(B_IM), bc(c_re, CG), ALU.mult)
            dve.drain()
            v.tensor_tensor(BB_RE, BB_RE, tmp, ALU.subtract)
            dve.drain()
            v.tensor_tensor(g(tmp), g(B_RE), bc(c_im, CG), ALU.mult)
            dve.drain()
            v.tensor_tensor(BB_IM, BB_IM, tmp, ALU.add)
            dve.drain().then_inc(bb_ready, 1)

        def pool_spread(pool):
            g = nc.gpsimd
            g.memset(bst, 0.0)
            g.memset(cpad.rearrange("p r k n -> p (r k n)"), 0.0)
            pool.drain()
            pool.wait_ge(bb_ready, 1)
            with pool.Fori(0, SBLOCKS) as b:
                pool.wait_ge(bT_kept, b + 1)
                for r, bb in ((0, BB_RE), (1, BB_IM)):
                    src = bb.rearrange("p (k c) -> p k c", c=CG)
                    dst = bst[:, P * r:P * r + P].rearrange("p (k h c) -> p k h c", h=2, c=CG)
                    g.tensor_copy(dst[0:64, :, 0, :], src[0:64, ds(4 * b, 4), :])
                    last = g.tensor_copy(dst[64:128, :, 1, :], src[64:128, ds(4 * b, 4), :])
                last.then_inc(spread_ready, 1)

        def pe_transposed(pe, b):
            pe.wait_ge(spread_ready, b + 1)
            nc.tensor.transpose(A(1, 0, P), bst[:, 0:P], ident)
            nc.tensor.transpose(A(1, P, P), bst[:, P:2 * P], ident).then_inc(bT_ready, 1)

        def act_ssm_transposed(act):
            act.nop().then_inc(bT_kept, 1)
            with act.Fori(0, SBLOCKS) as b:
                loop_wait(act, bT_ready, b + 1)
                nc.scalar.copy(BT[:, ds(b, 1), :], A(1, 0, 256).rearrange("p (o n) -> p o n", o=1)).then_inc(bT_kept, 1)

        def blocks(eng, body):
            body(0, 0, False, True, True)
            with eng.Fori(0, SBLOCKS // 2 - 2) as i:
                for k in range(2):
                    body(2 * i + 1 + k, 1 - k, True, True, True)
            for b in range(SBLOCKS - 3, SBLOCKS):
                body(b, b % 2, True, b + 1 < SBLOCKS, b + 2 < SBLOCKS)

        def at_block(x, b):
            return x[:, b:b + 1, :] if isinstance(b, int) else x[:, ds(b, 1), :]

        def act_ssm(act):
            def stage_inputs(b):
                nc.scalar.copy(ub.rearrange("p (o n) -> p o n", o=1), at_block(u_all, b))
                nc.scalar.copy(bT.rearrange("p (o n) -> p o n", o=1), at_block(BT, b)).then_inc(staged, 1)

            def trig(b, parity):
                act.wait_ge(frac_ready, b + 1)
                nc.scalar.activation(SIN[parity], PH[parity], ACT.Sin, scale=TURN)
                nc.scalar.activation(COS[parity], PH[parity], ACT.Sin, scale=TURN / 2)
                act.drain()
                nc.scalar.activation(COS[parity], COS[parity], ACT.Square)
                act.drain()
                nc.scalar.activation(COS[parity], COS[parity], ACT.Copy, scale=-2.0, bias=1.0).then_inc(trig_ready, 1)

            def finish(b):
                act.wait_ge(ysum_ready, b + 2)
                nc.scalar.activation(ysum, ysum, ACT.Gelu_apprx_tanh)
                act.drain()
                nc.scalar.copy(at_block(u_all, b), ysum.rearrange("p (o n) -> p o n", o=1)).then_inc(y_kept, 1)

            def body(b, parity, prev, following, ahead):
                if following:
                    if prev:
                        loop_wait(act, turned, b)
                        loop_wait(act, z_sined, b)
                    trig(b + 1, 1 - parity)
                loop_wait(act, y_ready, b + 1)
                for r, src in ((0, C_RE), (1, NC_RE), (2, NC_IM)):
                    x = src.rearrange("p (k c) -> p k c", c=CG)
                    flat = W[:, 512 + 512 * r:1024 + 512 * r]
                    for h in range(2):
                        rows = slice(64 * h, 64 * h + 64)
                        diag = bass.AP(tensor=flat.tensor, offset=flat[rows, 16 * h:16 * h + 1].offset,
                                       ap=[list(flat[rows].ap[0]), [P + 32, 4], [1, CG]])
                        mine = x[rows, 4 * b:4 * b + 4, :] if isinstance(b, int) else x[rows, ds(4 * b, 4), :]
                        last = nc.scalar.copy(diag, mine)
                last.then_inc(c_staged, 1)
                if following:
                    loop_wait(act, bu_ready, b + 1)
                    stage_inputs(b + 1)
                if prev:
                    finish(b - 1)

            act.drain()
            stage_inputs(0)
            trig(0, 0)
            blocks(act, body)
            finish(SBLOCKS - 1)

        def pe_ssm(pe):
            def inputs(b):
                pe.wait_ge(staged, b + 1)
                pe.wait_ge(bu_used, b + 1)
                for k in range(4):
                    rows = slice(32 * k, 32 * k + 32)
                    for r in range(2):
                        last = nc.tensor.matmul(A(k, T * r, T), bT[rows, P * r:P * r + P], ub[rows, :],
                                                start=True, stop=True)
                last.then_inc(bu_ready, 1)

            def outputs(b):
                pe.wait_ge(c_staged, b + 1)
                pe.wait_ge(ysum_ready, b + 1)
                pe.wait_ge(turned, b + 1)
                pe.wait_ge(z_sined, b + 1)
                zc = ZC.rearrange("p (k r n) -> p k r n", k=4, r=2)
                zs = V.rearrange("p (k r n) -> p k r n", k=4, r=2)
                n = 0
                for k in range(4):
                    for sign, x in ((0, zc[:, k, 0]), (1, zs[:, k, 1]), (2, zs[:, k, 0]), (2, zc[:, k, 1])):
                        last = nc.tensor.matmul(bank[0][:, T:2 * T], cpad[:, sign, k, :], x, start=n == 0, stop=n == 15)
                        n += 1
                last.then_inc(y_ready, 1)

            def body(b, parity, prev, following, ahead):
                if following:
                    inputs(b + 1)
                outputs(b)

            pe.nop().then_inc(y_ready, 1)
            inputs(0)
            blocks(pe, body)

        def dve_ssm(dve):
            v = nc.vector
            mag_k = mag.rearrange("p (a o) -> p a o", o=1)
            d_k = col("ssm_d").rearrange("p (a o) -> p a o", o=1)

            def round_turns(b, parity):
                dve.wait_ge(turns_ready, b + 1)
                v.tensor_scalar(ROUNDED, PH[parity], ROUND, ROUND, ALU.add, ALU.subtract).then_inc(rounded, 1)

            def finish(b):
                dve.wait_ge(y_kept, b + 1)
                v.scalar_tensor_tensor(ysum, at_block(u_all, b).rearrange("p o n -> p (o n)"),
                                       at_block(d_k, b).rearrange("p a o -> p (a o)"), bank[0][:, T:2 * T],
                                       ALU.mult, ALU.add).then_inc(ysum_ready, 1)

            def body(b, parity, prev, following, ahead):
                bu = aux[:].rearrange("p (k r n) -> p k r n", k=4, r=2)
                z = MC.rearrange("p (k r n) -> p k r n", k=4, r=2)
                ms = MS.rearrange("p (k r n) -> p k r n", k=4, r=2)
                zc = ZC.rearrange("p (k r n) -> p k r n", k=4, r=2)
                co = COS[parity].rearrange("p (k n) -> p k n", k=4)
                si = SIN[parity].rearrange("p (k n) -> p k n", k=4)
                dve.wait_ge(trig_ready, b + 1)
                dve.wait_ge(bu_ready, b + 1)
                for r in range(2):
                    v.tensor_tensor(ms[:, :, r, :], bu[:, :, r, :], si, ALU.mult)
                if prev:
                    dve.wait_ge(z_sined, b)
                for r in range(2):
                    last = v.tensor_tensor(z[:, :, r, :], bu[:, :, r, :], co, ALU.mult)
                last.then_inc(bu_used, 1)
                dve.drain()
                v.tensor_tensor(z[:, :, 0, :], z[:, :, 0, :], ms[:, :, 1, :], ALU.add)
                v.tensor_tensor(z[:, :, 1, :], z[:, :, 1, :], ms[:, :, 0, :], ALU.subtract)
                if ahead:
                    round_turns(b + 2, parity)
                dve.drain()
                for k in range(4):
                    m = mag_k[:, 4 * b + k:4 * b + k + 1, :] if isinstance(b, int) else mag_k[:, ds(4 * b + k, 1), :]
                    m = m.rearrange("p a o -> p (a o)").to_broadcast([P, T])
                    for r in range(2):
                        v.tensor_tensor_scan(z[:, k, r, :], m, z[:, k, r, :], 0.0, ALU.mult, ALU.add)
                dve.drain().then_inc(z_scanned, 1)
                dve.wait_ge(y_ready, b + 1)
                if prev:
                    finish(b - 1)
                for r in range(2):
                    last = v.tensor_tensor(zc[:, :, r, :], z[:, :, r, :], co, ALU.mult)
                last.then_inc(turned, 1)
                dve.drain()

            v.nop().then_inc(bu_used, 1)
            v.nop().then_inc(ysum_ready, 1)
            wait_drained(dve, "z")
            for b in range(2):
                round_turns(b, b)
            blocks(dve, body)
            dve.wait_ge(y_ready, SBLOCKS + 1)
            finish(SBLOCKS - 1)

        def pool_ssm(pool):
            g = nc.gpsimd

            def turns_of(b, parity):
                ph = PH[parity].rearrange("p (k n) -> p k n", k=4)
                f = turns.rearrange("p (a o) -> p a o", o=1)
                f = f[:, 4 * b:4 * b + 4, :] if isinstance(b, int) else f[:, ds(4 * b, 4), :]
                g.tensor_tensor(ph, f.to_broadcast([P, 4, T]), rep(cst("iota"), 4), ALU.mult)
                pool.drain().then_inc(turns_ready, 1)
                pool.wait_ge(rounded, b + 1)
                g.tensor_tensor(PH[parity], PH[parity], ROUNDED, ALU.subtract).then_inc(frac_ready, 1)

            def body(b, parity, prev, following, ahead):
                z = MC.rearrange("p (k r n) -> p k r n", k=4, r=2)
                zs = V.rearrange("p (k r n) -> p k r n", k=4, r=2)
                si = SIN[parity].rearrange("p (k n) -> p k n", k=4)
                pool.wait_ge(trig_ready, b + 1)
                if ahead:
                    turns_of(b + 2, parity)
                pool.wait_ge(z_scanned, b + 1)
                pool.wait_ge(y_ready, b + 1)
                for r in range(2):
                    g.tensor_tensor(zs[:, :, r, :], z[:, :, r, :], si, ALU.mult)
                pool.drain().then_inc(z_sined, 1)

            pool.wait_ge(angle_ready, 1)
            pool.wait_ge(params_in, 16 * N_PARAMS)
            pool.wait_ge(bT_kept, SBLOCKS + 1)
            pool.wait_ge(neg_ready, 1)
            for b in range(2):
                turns_of(b, b)
            blocks(pool, body)

        def act_glu(act):
            s_all = tiles(B(2))

            def body(i, k):
                s = product_ready(act, "glu", i, k)
                for f in range(2):
                    at = 2 * k + f
                    o = COL["b_glu"][0] + at
                    last = nc.scalar.activation(s_all[:, ds(8 * i + at, 1), :].rearrange("p a n -> p (a n)"),
                                                bank[s][:, T * f:T * f + T], ACT.Sigmoid,
                                                bias=cols[:, ds(8 * i + o, 1)])
                last.then_inc(slot_free[s], 1)
            steps(act, "glu", body)

        def dve_glu(dve):
            wait_drained(dve, "glu")
            dve.wait_ge(yz_ready, 1)
            for q in range(4):
                nc.vector.tensor_tensor(B(2, 1024 * q, 1024), B(2, 1024 * q, 1024), B(1, 1024 * q, 1024),
                                        ALU.mult).then_inc(glu_ready, 1)

        def pool_glu(pool):
            pool.wait_ge(y_kept, SBLOCKS + 1)
            nc.gpsimd.tensor_tensor(B(1), B(1), B(0), ALU.mult).then_inc(yz_ready, 1)

        KC, VC, KS, KW = (B(4, 1024 * k, 1024) for k in range(4))
        v_row = E[:].rearrange("p (b t n) -> p b t n", b=2, t=TT)
        cmp_in = [[B(5, 2048 * k + 1024 * h, 1024) for h in range(2)] for k in range(2)]
        q_all = tiles(B(0))
        zn = arena[:, 4096:4 * 4096].rearrange("p (j n) -> p j n", n=T)
        hid = W[:, 0:120].rearrange("p (k n) -> p k n", k=2)
        kcT = W[:, 128:188]
        vcr = W[0:NCMP, 256:768]
        gates = small[:, 0:96].rearrange("p (t n) -> p t n", t=TT)
        qg = B(5, 0, 1024).rearrange("p (h n) -> p h n", h=4)
        vg = W[:, 1024:1536].rearrange("p (b t n) -> p b t n", b=2, t=TT)
        vcg = W[0:NCMP, 1536:1664]
        SS, PP, PT = B(5, 1024, 1024), B(5, 2048, 1024), B(5, 3072, 1024)
        mx, rc = small[:, 96:100], small[:, 100:104]
        cmp_ready = sem("cmp_ready")
        hid_ready = sem("hid_ready")
        hid_act = sem("hid_act")
        cmp_out = sem("cmp_out")
        kc_kept = sem("kc_kept")
        vc_kept = sem("vc_kept")
        gates_ready = sem("gates_ready")
        gates_kept = sem("gates_kept")
        group_staged = sem("group_staged")
        s_ready = sem("s_ready")
        s_shifted = sem("s_shifted")
        e_ready = sem("e_ready")
        p_ready = sem("p_ready")
        pT_ready = sem("pT_ready")
        pT_kept = sem("pT_kept")
        o_ready = sem("o_ready")
        o_used = sem("o_used")
        att_ready = sem("att_ready")

        def dve_norm1(dve):
            dve_rstd(dve, 1)
            dve_modulated(dve, tiles(B(0)), col("kv_norm_g"), KSC, KSH)
            dve_modulated(dve, hT[:], col("norm_g", 16, 16), SC1, SH1)

        def act_kv(act):
            drain_to(act, "kv", tiles(B(4)))

            def body(i, k):
                s = product_ready(act, "kvrow", i, k)
                nc.scalar.copy(v_row[:, k // 2, :, SLOT_COLS * (k % 2):SLOT_COLS * (k % 2) + SLOT_COLS],
                               bank[s][:].rearrange("p (t n) -> p t n", t=TT)).then_inc(slot_free[s], 1)
            steps(act, "kvrow", body)

        def dve_cmp_in(dve):
            wait_drained(dve, "kv")
            for k, src in ((0, KC), (1, VC)):
                for h in range(2):
                    pe_ = col("pe", 32 * k + 16 * h, 16)
                    last = nc.vector.tensor_tensor(cmp_in[k][h].rearrange("p (a l) -> p a l", l=16),
                                                   src.rearrange("p (a l) -> p a l", l=16), rep(pe_, 64), ALU.add)
            last.then_inc(cmp_ready, 1)

        def pe_cmp(pe):
            pe.wait_ge(cmp_ready, 1)
            for k in range(2):
                s = slot_ready(pe, "cmp", 0, k)
                for l in range(CMP_LEN):
                    x = cmp_in[k][l // 16].rearrange("p (h a l) -> p h a l", h=KV, l=16)
                    x = x[:, :, l // 16:l // 16 + NCMP, l % 16]
                    last = nc.tensor.matmul(bank[s][:, 0:60].rearrange("p (h a) -> p h a", h=KV),
                                            ring[:, s, P * l:P * l + P], x, start=l == 0, stop=l == CMP_LEN - 1)
                last.then_inc(products, 1)
            pe.wait_ge(hid_act, 2)
            nc.tensor.matmul(A(1, 0, 60), cmp_w2[:, 0, :], hid[:, 0, :], start=True, stop=True)
            for h in range(KV):
                last = nc.tensor.matmul(A(2)[0:NCMP, P * h:P * h + P], hid[:, 1, NCMP * h:NCMP * h + NCMP],
                                        cmp_w2[:, 1, :], start=True, stop=True)
            last.then_inc(cmp_out, 1)

        def act_cmp(act):
            for k in range(2):
                s = product_ready(act, "cmp", 0, k)
                nc.scalar.activation(hid[:, k, :], bank[s][:, 0:60], ACT.Gelu_apprx_tanh,
                                     bias=col("cmp_b1", k, 1)).then_inc(hid_act, 1)
                act.wait_ge(hid_act, k + 1)
                act.nop().then_inc(slot_free[s], 1)
            act.wait_ge(cmp_out, 1)
            nc.scalar.activation(kcT, A(1, 0, 60), ACT.Identity, bias=col("cmp_b2", 0, 1)).then_inc(kc_kept, 1)

        def dve_cmp(dve):
            dve.wait_ge(cmp_out, 1)
            nc.vector.tensor_tensor(vcr.rearrange("p (h d) -> p h d", h=KV),
                                    A(2)[0:NCMP].rearrange("p (h d) -> p h d", h=KV),
                                    rep(cmp_b2r[:], KV), ALU.add).then_inc(vc_kept, 1)

        def pe_gates(pe):
            for f in range(TT):
                for j in range(KD):
                    last = nc.tensor.matmul(A(3, 48 * f, 48), hT[:, j, P * f:P * f + P], w_gate[:, j, :],
                                            start=j == 0, stop=j == KD - 1)
            last.then_inc(gates_ready, 1)

        def act_gates(act):
            act.wait_ge(gates_ready, 1)
            nc.scalar.activation(small[:, 0:96], A(3, 0, 96), ACT.Sigmoid).then_inc(gates_kept, 1)

        UNITS = [("cmp", 0), ("cmp", 1), (0, 0), (0, 1), (1, 0), (1, 1)]
        ATT = len(UNITS)

        FILL0, FILL = 10, [(12, 4), (12, 4), (18, 4), (22, 4), (16, 4), (18, 0)]
        ENDS = {}
        _done = FILL0
        for _u, _pieces in enumerate(FILL):
            for _place, _count in enumerate(_pieces):
                for _slot in range(_done // (2 * KD), (_done + _count) // (2 * KD)):
                    ENDS[_slot] = (_u, _place)
                _done += _count

        def zs_cols(w):
            view = w.rearrange("(j p) n -> p j n", p=P)

            def src(i, k):
                at = D + 48 + D * (1 + k // 2) + SLOT_COLS * (k % 2)
                return (lambda slot: slot.rearrange("p (j n) -> p j n", j=KD)), view[:, :, ds(2 * SLOT_COLS * i + at, SLOT_COLS)]
            return src

        def act_attend(act):
            def gate_drain(g, u, place):
                for k in range(4):
                    if ENDS[k] == (u, place):
                        s = product_ready(act, "zs", g, k)
                        at = HEADS * (1 + k // 2) + 2 * (k % 2)
                        nc.scalar.activation(zn[:, ds(4 * g + at, 2), :], bank[s][:].rearrange("p (f n) -> p f n", f=2),
                                             ACT.Silu).then_inc(slot_free[s], 1)

            act.drain()
            act.wait_ge(vc_kept, 1)
            with act.Fori(0, KV) as g:
                loop_wait(act, o_used, ATT * g + 1)
                nc.scalar.copy(qg, q_all[:, ds(4 * g, 4), :])
                for b in range(2):
                    nc.scalar.copy(vg[:, b], v_row[:, b, :, ds(P * g, P)])
                nc.scalar.copy(vcg, vcr[:, ds(P * g, P)]).then_inc(group_staged, 1)
                for u, (b, f) in enumerate(UNITS):
                    nk = NCMP if b == "cmp" else P * (f + 1)
                    act.wait_ge(s_shifted, ATT * g + u + 1)
                    nc.scalar.activation(PP[:, 0:4 * nk], SS[:, 0:4 * nk], ACT.Exp).then_inc(e_ready, 1)
                    gate_drain(g, u, 0)
                    act.wait_ge(pT_ready, ATT * g + u + 1)
                    if b == "cmp":
                        last = nc.scalar.copy(PT[0:NCMP, 0:512], A(2)[0:NCMP])
                    else:
                        last = nc.scalar.copy(PT[:, 0:512 * (f + 1)], aux[:, 1024:1024 + 512 * (f + 1)])
                    last.then_inc(pT_kept, 1)
                    gate_drain(g, u, 1)

        def pe_attend(pe):
            pe.wait_ge(kc_kept, 1)
            with pe.Fori(0, KV) as g:
                def scores(u):
                    b, f = UNITS[u]
                    if b == "cmp":
                        nk, keys = NCMP, kcT[:, ds(NCMP * g, NCMP)]
                    else:
                        nk, keys = P * (f + 1), (KS, KW)[b][:, ds(T * g, P * (f + 1))]
                    for h in range(HPG):
                        last = nc.tensor.matmul(aux[:, nk * h:nk * h + nk], qg[:, h, P * f:P * f + P], keys,
                                                start=True, stop=True)
                    last.then_inc(s_ready, 1)

                def fill(done, count):
                    while count:
                        k, first = done // (2 * KD), done % (2 * KD)
                        n = min(count, 2 * KD - first)
                        if first == 0:
                            slot_ready(pe, "zs", g, k)
                        dense_piece((BASE["zs"] + k) % RING, hT, first, n)
                        done, count = done + n, count - n

                fill(0, FILL0)
                done = FILL0
                pe.wait_ge(group_staged, g + 1)
                scores(0)
                for u, (b, f) in enumerate(UNITS):
                    nk = NCMP if b == "cmp" else P * (f + 1)
                    fill(done, FILL[u][0])
                    done += FILL[u][0]
                    pe.wait_ge(p_ready, ATT * g + u + 1)
                    pe.wait_ge(o_used, ATT * g + u + 1)
                    if b == "cmp":
                        for h in range(HPG):
                            last = nc.tensor.transpose(A(2)[0:NCMP, P * h:P * h + P], PP[:, nk * h:nk * h + nk], ident)
                    else:
                        for kt in range(f + 1):
                            for h in range(HPG):
                                at = nk * h + P * kt
                                last = nc.tensor.transpose(A(2 + kt, P * h, P), PP[:, at:at + P], ident)
                    last.then_inc(pT_ready, 1)
                    if u + 1 < ATT:
                        scores(u + 1)
                    fill(done, FILL[u][1])
                    done += FILL[u][1]
                    pe.wait_ge(pT_kept, ATT * g + u + 1)
                    if b == "cmp":
                        last = nc.tensor.matmul(A(2), vcg, PT[0:NCMP, 0:512], start=True, stop=True)
                    else:
                        for kt in range(f + 1):
                            last = nc.tensor.matmul(A(2), vg[:, b, kt, :], PT[:, 512 * kt:512 * kt + 512],
                                                    start=kt == 0, stop=kt == f)
                    last.then_inc(o_ready, 1)

        def dve_attend(dve):
            v = nc.vector
            dve.wait_ge(gates_kept, 1)
            wait_drained(dve, "zc")
            v.nop().then_inc(o_used, 1)
            with dve.Fori(0, KV) as g:
                def heads(x, u):
                    n = 4 * (NCMP if UNITS[u][0] == "cmp" else P * (UNITS[u][1] + 1))
                    return x[:, 0:n].rearrange("p (h n) -> p h n", h=4)

                def shifted(u):
                    b, f = UNITS[u]
                    mask = cst("cmp_neg", NCMP * f, NCMP) if b == "cmp" else cst("causal", P - P * f, P * (f + 1))
                    s3 = heads(SS, u)
                    dve.wait_ge(s_ready, ATT * g + u + 1)
                    v.tensor_tensor(s3, heads(aux, u), rep(mask, 4), ALU.add)
                    dve.drain()
                    v.reduce_max(mx, s3, AX_X)
                    dve.drain()
                    v.tensor_tensor(s3, s3, bc(mx, s3.shape[2]), ALU.subtract).then_inc(s_shifted, 1)

                def weights(u):
                    b, f = UNITS[u]
                    br = 0 if b == "cmp" else b + 1
                    p3 = heads(PP, u)
                    dve.wait_ge(e_ready, ATT * g + u + 1)
                    v.reduce_sum(rc, p3, AX_X)
                    dve.drain()
                    v.reciprocal(rc, rc)
                    dve.drain()
                    v.tensor_tensor(rc, rc, gates[:, f, ds(4 * g + HEADS * br, 4)], ALU.mult)
                    dve.drain()
                    last = v.tensor_tensor(p3, p3, bc(rc, p3.shape[2]), ALU.mult)
                    if b == "cmp":
                        dve.drain()
                        last = v.tensor_tensor(p3, p3, rep(cst("cmp_one", NCMP * f, NCMP), 4), ALU.mult)
                    last.then_inc(p_ready, 1)

                shifted(0)
                for u, (b, f) in enumerate(UNITS):
                    weights(u)
                    if u + 1 < ATT:
                        shifted(u + 1)
                    br = 0 if b == "cmp" else b + 1
                    if br and f == 0:
                        n = BASE["zs"] + 2 * br - 1
                        dve.wait_ge(slot_free[n % RING], g + n // RING + 2)
                    dve.wait_ge(o_ready, ATT * g + u + 1)
                    z = zn[:, ds(4 * g + HEADS * br, 4), P * f:P * f + P]
                    v.tensor_tensor(z, z, A(2).rearrange("p (h n) -> p h n", h=4), ALU.mult).then_inc(o_used, 1)
                for br in (1, 2):
                    dve.drain()
                    z = zn[:, ds(4 * g, 4), :]
                    v.tensor_tensor(z, z, zn[:, ds(4 * g + HEADS * br, 4), :], ALU.add)
            dve.drain().then_inc(att_ready, 1)

        raw = arena[:, 0:6144].rearrange("p (j n) -> p j n", n=T)
        conv = arena[:, 2 * 4096:2 * 4096 + 6144].rearrange("p (j n) -> p j n", n=T)
        za = tiles(B(1, 2048, 2048))
        qk = conv[:, 0:16, :]
        lg = small[:, 0:32].rearrange("p (t n) -> p t n", t=TT)
        beta, gdec, gcum, glast, ebeta, edec = (small[:, 32 + 16 * k:48 + 16 * k].rearrange("p (t h) -> p t h", t=TT)
                                                for k in range(6))
        sp_a, sp_b = (small[:, 128 + 16 * k:144 + 16 * k].rearrange("p (t h) -> p t h", t=TT) for k in range(2))
        ea = small[:, 160:168]
        egl = small[:, 168:200]
        Gb, betab = B(0, 0, 2048), B(0, 2048, 2048)
        wide = [B(5, 0, 2048), B(5, 2048, 2048)]
        EGb = B(1, 0, 2048)
        at_all = B(4, 0, 2048).rearrange("p (h t n) -> p h t n", h=GH, t=TT)
        o_all = tiles(B(4, 2048, 2048))
        st = [B(3, 2048 + 256 * k, 256) for k in range(8)]
        qh, kh, vh = st[0], st[1], st[2]
        LT = E[:, 0:1024].rearrange("p (h t n) -> p h t n", h=GH, t=TT)
        Tsol = E[:, 1024:2048].rearrange("p (c n) -> p c n", c=16)
        Lsys = B(5).rearrange("p (j i) -> p j i", i=CH)
        tmp_solve = W[:, 0:1024]
        red = W[:, 1024:1040]

        conv_ready = sem("conv_ready")
        silu_ready = sem("silu_ready")
        hsq_ready = sem("hsq_ready")
        hms_ready = sem("hms_ready")
        hms_kept = sem("hms_kept")
        qk_ready = sem("qk_ready")
        lg_ready = sem("lg_ready")
        lg_kept = sem("lg_kept")
        beta_ready = sem("beta_ready")
        dec_in = sem("dec_in")
        dec_log = sem("dec_log")
        wide_ready = sem("wide_ready")
        cum_ready = sem("cum_ready")
        cum_kept = sem("cum_kept")
        bcast_ready = sem("bcast_ready")
        bcast_kept = sem("bcast_kept")
        edec_in = sem("edec_in")
        edec_ready = sem("edec_ready")
        edec_done = sem("edec_done")
        head_staged = sem("head_staged")
        kk_ready = sem("kk_ready")
        diff_ready = sem("diff_ready")
        decay_ready = sem("decay_ready")
        head_done = sem("head_done")
        L_out = sem("L_out")
        L_in = sem("L_in")
        T_solved = sem("T_solved")
        T_out = sem("T_out")
        T_in = sem("T_in")
        h2_staged = sem("h2_staged")
        rows_ready = sem("rows_ready")
        rows_kept = sem("rows_kept")
        w_ready = sem("w_ready")
        w_kept = sem("w_kept")
        vnew_ready = sem("vnew_ready")
        vnew_kept = sem("vnew_kept")
        step_ready = sem("step_ready")
        S_ready = sem("S_ready")
        oh_kept = sem("oh_kept")
        ya_ready = sem("ya_ready")

        rstd2 = W[:, 0:T]
        ms2_ready = sem("ms2_ready")

        def dve_final0(dve):
            v = nc.vector
            dve_rstd(dve, 2)
            v.tensor_tensor(rstd2, rstd[:], rstd[:], ALU.mult)
            v.tensor_tensor(gain[:], col("final_g"), col("mix_g"), ALU.mult)
            dve.drain()
            v.tensor_tensor(rstd2, rstd2, A(1, 0, T), ALU.mult)
            dve.drain().then_inc(ms2_ready, 1)
            dve.wait_ge(std_ready, 4)
            v.reciprocal(rstd2, rstd2)
            dve.drain()
            v.tensor_tensor(rstd2, rstd2, rstd[:], ALU.mult)
            dve.drain()
            dve_modulated(dve, hT[:], gain[:], None, None, rstd2)
            dve_modulated(dve, xT[:], col("final_g"), None, None, signal=False)

        def act_final0(act):
            act.wait_ge(ms2_ready, 1)
            nc.scalar.activation(rstd2, rstd2, ACT.Sqrt, scale=1.0 / D, bias=eps[:]).then_inc(std_ready, 1)

        def pe_beta(pe):
            for f in range(TT):
                for j in range(KD):
                    last = nc.tensor.matmul(A(3, 16 * f, 16), hT[:, j, P * f:P * f + P], w_beta[:, j, :],
                                            start=j == 0, stop=j == KD - 1)
            last.then_inc(lg_ready, 1)

        def act_beta(act):
            act.wait_ge(lg_ready, 1)
            nc.scalar.copy(small[:, 0:32], A(3, 0, 32)).then_inc(lg_kept, 1)
            act.wait_ge(lg_kept, 1)
            nc.scalar.activation(beta, lg[:, :, 0:8], ACT.Sigmoid).then_inc(beta_ready, 1)
            act.wait_ge(dec_in, 1)
            nc.scalar.activation(sp_b, sp_b, ACT.Exp, scale=-1.0)
            nc.scalar.activation(ea, gdn_rows[:, 0:8], ACT.Exp)
            act.drain()
            nc.scalar.activation(sp_b, sp_b, ACT.Ln, bias=1.0).then_inc(dec_log, 1)

        def dve_conv(dve):
            v = nc.vector
            wait_drained(dve, "gdn")
            cw = col("conv_w").rearrange("p (j k) -> p j k", k=4)
            with dve.Fori(0, COUNT["gdn"] * 2 // 4) as i:
                def tile(x, k, lo, hi):
                    return x[:, ds(4 * i + k, 1), lo:hi].rearrange("p a n -> p (a n)")

                for k in range(4):
                    v.tensor_scalar(tile(conv, k, 0, T), tile(raw, k, 0, T), tile(cw, k, 3, 4), None, ALU.mult)
                for tap in range(3):
                    back = 3 - tap
                    dve.drain()
                    for k in range(4):
                        dst = tile(conv, k, back, T)
                        v.scalar_tensor_tensor(dst, tile(raw, k, 0, T - back), tile(cw, k, tap, tap + 1), dst,
                                               ALU.mult, ALU.add)
            dve.drain().then_inc(conv_ready, 1)

        def act_conv(act):
            act.wait_ge(conv_ready, 1)
            for k in range(3):
                at = arena[:, 2 * 4096 + 2048 * k:2 * 4096 + 2048 * k + 2048]
                nc.scalar.activation(at, at, ACT.Silu)
            act.drain()
            nc.scalar.activation(B(0), B(2), ACT.Square).then_inc(hsq_ready, 1)

        def pe_head_squares(pe, k, sq, n):
            pe.wait_ge(hsq_ready, k + 1)
            for i in range(n):
                if i >= 4 or k == 2:
                    pe.wait_ge(hms_kept, HMS[k] + i - 3)
                nc.tensor.matmul(A(i % 4), ones[:], sq[:, 512 * i:512 * i + 512], start=True, stop=True).then_inc(hms_ready, 1)

        HMS = [0, 8, 12]

        def act_head_roots(act, k, dst, n, scale):
            for i in range(n):
                act.wait_ge(hms_ready, HMS[k] + i + 1)
                nc.scalar.activation(dst[:, 512 * i:512 * i + 512], A(i % 4), ACT.Sqrt, bias=eps[:],
                                     scale=scale).then_inc(hms_kept, 1)

        def dve_beta(dve):
            v = nc.vector
            dve.wait_ge(lg_kept, 1)
            v.tensor_tensor(sp_a, lg[:, :, 8:16], rep(gdn_rows[:, 8:16], TT), ALU.add)
            dve.drain()
            v.tensor_scalar(sp_b, sp_a, -1.0, None, ALU.mult)
            dve.drain()
            v.tensor_tensor(sp_b, sp_b, sp_a, ALU.max)
            v.tensor_scalar(sp_a, sp_a, 0.0, None, ALU.max)
            dve.drain().then_inc(dec_in, 1)
            dve.wait_ge(dec_log, 1)
            dve.wait_ge(beta_ready, 1)
            v.tensor_tensor(sp_a, sp_a, sp_b, ALU.add)
            dve.drain()
            v.scalar_tensor_tensor(gdec, sp_a, -1.0, rep(ea, TT), ALU.mult, ALU.mult)
            dve.drain()
            for k, x in ((0, gdec), (1, beta)):
                last = v.tensor_copy(wide[k].rearrange("p (a n) -> p a n", n=P),
                                     bc(x.rearrange("p t h -> p (t h)"), P))
            last.then_inc(wide_ready, 1)

        def pe_beta_sums(pe):
            pe.wait_ge(wide_ready, 1)
            pe.wait_ge(hms_kept, 8)
            for f in range(TT):
                nc.tensor.matmul(A(0, 8 * f, 8), cst("cum"), gdec[:, f, :], start=True, stop=True)
            for f in range(TT):
                last = nc.tensor.matmul(A(0, 16 + 8 * f, 8), cst("same"), gdec[:, f, :], start=True, stop=True)
            last.then_inc(cum_ready, 1)
            pe.wait_ge(cum_kept, 1)
            for k, rhs in ((0, cst("cum")), (1, ident)):
                if k:
                    pe.wait_ge(bcast_kept, 1)
                for h in range(GH):
                    for f in range(TT):
                        at = P * (GH * f + h)
                        last = nc.tensor.matmul(aux[:, T * h + P * f:T * h + P * f + P], wide[k][:, at:at + P], rhs,
                                                start=True, stop=True)
                last.then_inc(bcast_ready, 1)

        def act_beta_sums(act):
            act.wait_ge(cum_ready, 1)
            nc.scalar.copy(gcum.rearrange("p t h -> p (t h)"), A(0, 0, 16))
            nc.scalar.copy(glast.rearrange("p t h -> p (t h)"), A(0, 16, 16)).then_inc(cum_kept, 1)
            act.wait_ge(bcast_ready, 1)
            nc.scalar.copy(Gb, aux[:]).then_inc(bcast_kept, 1)
            act.wait_ge(bcast_ready, 2)
            nc.scalar.copy(betab, aux[:]).then_inc(bcast_kept, 1)
            act.wait_ge(edec_in, 1)
            nc.scalar.activation(EGb, Gb, ACT.Exp)
            nc.scalar.activation(edec.rearrange("p t h -> p (t h)"), edec.rearrange("p t h -> p (t h)"), ACT.Exp)
            nc.scalar.activation(ebeta.rearrange("p t h -> p (t h)"), gcum.rearrange("p t h -> p (t h)"), ACT.Exp).then_inc(edec_ready, 1)

        def dve_qk(dve):
            v = nc.vector
            dve.wait_ge(hms_kept, 8)
            v.reciprocal(B(4), B(4))
            dve.drain()
            v.tensor_tensor(B(2), B(2), B(4), ALU.mult).then_inc(qk_ready, 1)

        def dve_beta_sums(dve):
            v = nc.vector
            dve.wait_ge(cum_kept, 1)
            v.tensor_tensor(edec, glast, gcum, ALU.subtract)
            dve.wait_ge(bcast_kept, 2)
            dve.drain().then_inc(edec_in, 1)
            dve.wait_ge(edec_ready, 1)
            v.tensor_tensor(ebeta, ebeta, beta, ALU.mult)
            v.tensor_copy(egl.rearrange("p (h c) -> p h c", c=NCH),
                          EGb.rearrange("p (h c i) -> p h c i", c=NCH, i=CH)[:, :, :, CH - 1])
            dve.drain().then_inc(edec_done, 1)

        def act_heads(act):
            act.drain()
            act.wait_ge(qk_ready, 1)
            with act.Fori(0, GH) as h:
                loop_wait(act, head_done, h + 1)
                nc.scalar.copy(qh.rearrange("p (o n) -> p o n", o=1), conv[:, ds(h, 1), :])
                nc.scalar.copy(kh.rearrange("p (o n) -> p o n", o=1), conv[:, ds(8 + h, 1), :]).then_inc(head_staged, 1)
                act.wait_ge(diff_ready, h + 1)
                nc.scalar.activation(st[3], st[3], ACT.Exp).then_inc(decay_ready, 1)

        def pe_heads(pe):
            with pe.Fori(0, GH) as h:
                pe.wait_ge(head_staged, h + 1)
                for f in range(TT):
                    r = slice(P * f, P * f + P)
                    nc.tensor.matmul(A(0, P * f, P), kh[:, r], kh[:, r], start=True, stop=True)
                for f in range(TT):
                    r = slice(P * f, P * f + P)
                    last = nc.tensor.matmul(A(1, P * f, P), kh[:, r], qh[:, r], start=True, stop=True)
                last.then_inc(kk_ready, 1)

        def dve_heads(dve):
            v = nc.vector
            v.nop().then_inc(head_done, 1)
            Gb3, bb3, Eg3 = tiles(Gb), tiles(betab), tiles(EGb)
            diff = st[3].rearrange("p (t n) -> p t n", t=TT)
            prod = st[4].rearrange("p (t n) -> p t n", t=TT)
            with dve.Fori(0, GH) as h:
                for f in range(TT):
                    v.scalar_tensor_tensor(diff[:, f, :], Gb3[:, ds(h, 1), P * f:P * f + P].rearrange("p o n -> p (o n)"),
                                           gcum[:, f, ds(h, 1)], cst("decay_neg"), ALU.subtract, ALU.add)
                dve.drain().then_inc(diff_ready, 1)
                dve.wait_ge(decay_ready, h + 1)
                dve.wait_ge(kk_ready, h + 1)
                v.scalar_tensor_tensor(at_all[:, ds(h, 1), :, :].rearrange("p o t n -> p (o t n)"), A(1, 0, T), SCALE, st[3],
                                       ALU.mult, ALU.mult)
                q = conv[:, ds(h, 1), :].rearrange("p o n -> p (o n)")
                v.scalar_tensor_tensor(q, q, SCALE, Eg3[:, ds(h, 1), :].rearrange("p o n -> p (o n)"), ALU.mult, ALU.mult)
                v.tensor_tensor(st[4], A(0, 0, T), st[3], ALU.mult)
                dve.drain()
                v.tensor_tensor(st[4], st[4], bb3[:, ds(h, 1), :].rearrange("p o n -> p (o n)"), ALU.mult)
                dve.drain()
                for c in range(2):
                    r = slice(CH * c, CH * c + CH)
                    v.tensor_tensor(LT[r, ds(h, 1), :, :].rearrange("p o t n -> p (o t) n"), prod[r, :, CH * c:CH * c + CH],
                                    rep(cst("strict")[r], TT), ALU.mult)
                dve.drain().then_inc(head_done, 1)

        def sp_solve(sp):
            Ls = t["scratch_L"]
            sp.wait_ge(head_done, GH + 1)
            for c in range(2):
                r = slice(CH * c, CH * c + CH)
                sp.dma_start(Ls.rearrange("h (t c) j i -> c j h t i", c=2)[c], LT[r]).then_inc(L_out, 16)
            sp.dma_start(Tsol, t["eye"]).then_inc(L_in, 16)
            sp.wait_ge(L_out, 32)
            src = Ls.rearrange("h c j i -> (h c) (j i)")
            for c in range(4):
                dst = arena[:, 5 * 4096:6 * 4096]
                dst = bass.AP(tensor=dst.tensor, offset=dst[c:c + 1].offset, ap=[[dst.ap[0][0] * 4, 32], [1, 4096]])
                sp.dma_start(dst, src).then_inc(L_in, 16)

        def sp_solved(sp):
            sp.wait_ge(T_solved, 1)
            sp.dma_start(t["scratch_T"].rearrange("h c (a b) i -> (h c a) b i", a=4), Tsol).then_inc(T_out, 16)
            sp.wait_ge(T_out, 16)
            for c in range(2):
                r = slice(CH * c, CH * c + CH)
                sp.dma_start(LT[r], t["scratch_T"].rearrange("h (t c) j i -> c j h t i", c=2)[c]).then_inc(T_in, 16)

        def dve_solve(dve):
            v = nc.vector
            dve.wait_ge(L_in, 16 * 5)
            for q in range(4):
                J = 16 * (q + 1)
                tmp = tmp_solve[:, 0:16 * J].rearrange("p (c j) -> p c j", c=16)
                with dve.Fori(16 * q, 16 * q + 16) as i:
                    row = Lsys[:, 0:J, ds(i, 1)].rearrange("p j o -> p o j").to_broadcast([P, 16, J])
                    v.tensor_tensor(tmp, Tsol[:, :, 0:J], row, ALU.mult)
                    dve.drain()
                    v.reduce_sum(red, tmp, AX_X)
                    dve.drain()
                    x = Tsol[:, :, ds(i, 1)]
                    v.tensor_tensor(x, x, red.rearrange("p (c o) -> p c o", o=1), ALU.subtract)
                    dve.drain()
            dve.drain().then_inc(T_solved, 1)

        TT_h, AT_h = W[:, 512:768], W[:, 1216:1472]
        kdec = W[:, 0:512]
        S_, VN = W[:, 1472:1600], W[:, 1600:1728]
        egl_h = W[:, 1728:1732]
        scal = W[:, 1732:1738]
        kbg, vbr = st[3], st[5]
        scan_clear = sem("scan_clear")
        nw = st[7]
        ga_all = tiles(B(5))

        o_bank = A(1, 256, T)

        def scan_heads(eng, body):
            with eng.Fori(0, GH // 4) as i:
                for k in range(4):
                    body(i, k, 4 * i + k)

        def act_scan(act):
            def body(i, k, h):
                loop_wait(act, oh_kept, h + 1)
                nc.scalar.copy(kh.rearrange("p (o n) -> p o n", o=1), conv[:, ds(8 + h, 1), :])
                nc.scalar.copy(vh.rearrange("p (o n) -> p o n", o=1), conv[:, ds(16 + h, 1), :])
                for c in range(2):
                    r = slice(CH * c, CH * c + CH)
                    nc.scalar.copy(TT_h[r].rearrange("p (o t n) -> p o t n", o=1, t=TT)[:, :, :, CH * c:CH * c + CH],
                                   LT[r, ds(h, 1), :, :])
                nc.scalar.copy(AT_h.rearrange("p (o t n) -> p o t n", o=1, t=TT), at_all[:, ds(h, 1), :, :])
                nc.scalar.copy(egl_h, egl[:, ds(4 * h, 4)])
                for m, x in enumerate((ebeta, edec, beta)):
                    last = nc.scalar.copy(scal[:, 2 * m:2 * m + 2].rearrange("p (t o) -> p t o", o=1), x[:, :, ds(h, 1)])
                last.then_inc(h2_staged, 1)
                act.wait_ge(w_ready, h + 1)
                nc.scalar.mul(nw, A(1, 0, T), -1.0).then_inc(w_kept, 1)
                for c in range(NCH):
                    r = slice(CH * (c % 2), CH * (c % 2) + CH)
                    act.wait_ge(vnew_ready, NCH * h + c + 1)
                    nc.scalar.copy(VN[r], A(2, 0, P)[r]).then_inc(vnew_kept, 1)
                s = product_ready(act, "ga", i, k)
                nc.scalar.activation(ga_all[:, ds(8 * i + 2 * k, 2), :], bank[s][:].rearrange("p (f n) -> p f n", f=2),
                                     ACT.Sigmoid).then_inc(slot_free[s], 1)
                loop_wait(act, step_ready, NCH * h + NCH)
                nc.scalar.copy(o_all[:, ds(h, 1), :], o_bank.rearrange("p (o n) -> p o n", o=1)).then_inc(oh_kept, 1)

            act.drain()
            act.wait_ge(T_in, 32)
            act.wait_ge(edec_done, 1)
            act.wait_ge(scan_clear, 1)
            scan_heads(act, body)

        def pe_scan(pe):
            def body(i, k, h):
                g = slot_ready(pe, "ga", i, k)
                dense_piece(g, hT, 0, 7)
                pe.wait_ge(h2_staged, h + 1)
                for f in range(TT):
                    r = slice(P * f, P * f + P)
                    nc.tensor.transpose(A(0, P * f, P), kh[:, r], ident)
                    last = nc.tensor.transpose(A(0, 256 + P * f, P), vh[:, r], ident)
                last.then_inc(rows_ready, 1)
                dense_piece(g, hT, 7, 5)
                pe.wait_ge(rows_kept, h + 1)
                for f in range(TT):
                    last = nc.tensor.matmul(A(1, P * f, P), kbg[:, P * f:P * f + P], TT_h[:, P * f:P * f + P],
                                            start=True, stop=True)
                last.then_inc(w_ready, 1)
                dense_piece(g, hT, 12, 2)
                pe.wait_ge(w_kept, h + 1)
                done = 14
                for c in range(NCH):
                    r = slice(CH * (c % 2), CH * (c % 2) + CH)
                    f = c // 2
                    added = nc.tensor.matmul(A(2, 0, P)[r], TT_h[:, CH * c:CH * c + CH], vbr[:, P * f:P * f + P],
                                             start=True, stop=c == 0)
                    if c:
                        dense_piece(g, hT, done, 2)
                        done += 2
                        pe.wait_ge(S_ready, (NCH - 1) * h + c)
                        added = nc.tensor.matmul(A(2, 0, P)[r], nw[:, CH * c:CH * c + CH], S_, start=False, stop=True)
                    added.then_inc(vnew_ready, 1)
                    o = o_bank[:, CH * c:CH * c + CH]
                    if c:
                        q = conv[:, ds(h, 1), CH * c:CH * c + CH].rearrange("p o n -> p (o n)")
                        nc.tensor.matmul(o, S_, q, start=True, stop=False)
                    dense_piece(g, hT, done, 3)
                    done += 3
                    pe.wait_ge(vnew_kept, NCH * h + c + 1)
                    last = nc.tensor.matmul(o, VN, AT_h[:, CH * c:CH * c + CH], start=c == 0, stop=True)
                    if c < NCH - 1:
                        last = nc.tensor.matmul(A(3, 0, P), kdec[:, P * c:P * c + P], VN, start=True, stop=True)
                    last.then_inc(step_ready, 1)

            scan_heads(pe, body)

        def dve_scan(dve):
            v = nc.vector
            v.nop().then_inc(oh_kept, 1)
            v.memset(W[:, 0:768], 0.0)
            v.memset(VN, 0.0)
            dve.drain().then_inc(scan_clear, 1)
            with dve.Fori(0, GH) as h:
                dve.wait_ge(h2_staged, h + 1)
                dve.wait_ge(rows_ready, h + 1)
                for f in range(TT):
                    r = slice(P * f, P * f + P)
                    v.tensor_scalar(kbg[:, r], A(0, P * f, P), scal[:, f:f + 1], None, ALU.mult)
                    for c in range(2):
                        half = slice(CH * c, CH * c + CH)
                        at = P * (2 * f + c)
                        v.tensor_scalar(kdec[half, at:at + P], A(0, P * f, P)[half], scal[half, 2 + f:3 + f], None, ALU.mult)
                    v.tensor_scalar(vbr[:, r], A(0, 256 + P * f, P), scal[:, 4 + f:5 + f], None, ALU.mult)
                dve.drain().then_inc(rows_kept, 1)
                for c in range(NCH - 1):
                    dve.wait_ge(step_ready, NCH * h + c + 1)
                    if c == 0:
                        v.tensor_copy(S_, A(3, 0, P)).then_inc(S_ready, 1)
                    else:
                        v.scalar_tensor_tensor(S_, S_, egl_h[:, c:c + 1], A(3, 0, P), ALU.mult, ALU.add).then_inc(S_ready, 1)
                    dve.drain()

        o_sq, o_root = W[:], E[:]

        def act_ya(act):
            act.drain()
            nc.scalar.activation(o_sq, B(4, 2048, 2048), ACT.Square).then_inc(hsq_ready, 1)
            nc.scalar.activation(B(2), B(0), ACT.Square).then_inc(hsq_ready, 1)
            act_head_roots(act, 1, o_root, 4, 1.0 / DH)

        def dve_ya(dve):
            v = nc.vector
            dve.wait_ge(hms_kept, 12)
            v.reciprocal(o_root, o_root)
            dve.drain()
            v.scalar_tensor_tensor(B(4, 2048, 2048), B(4, 2048, 2048), col("o_norm"), o_root, ALU.mult, ALU.mult)
            dve.drain()
            wait_drained(dve, "za")
            v.tensor_tensor(B(4, 2048, 2048), B(4, 2048, 2048), B(1, 2048, 2048), ALU.mult).then_inc(ya_ready, 1)

        vb_row = B(1, 0, 2048).rearrange("p (t n) -> p t n", t=TT)
        bias = B(2, 0, 3072).rearrange("p (h n) -> p h n", h=GH)
        yb_all = tiles(B(4, 0, 2048))
        gb_all = tiles(B(3))
        flip, causal_flip = B(2, 3072, P), B(2, 3072 + P, P)
        onehot = B(4, 0, 512)[0:32]
        rel = B(4, 512, 8)[0:32]
        by_dist = B(4, 1024, 512)[0:GH]
        rel_in = sem("rel_in")
        rel_ready = sem("rel_ready")
        rel_kept = sem("rel_kept")
        rel_out = sem("rel_out")
        bias_in = sem("bias_in")
        bias_ready = sem("bias_ready")
        qkb_ready = sem("qkb_ready")
        yb_ready = sem("yb_ready")
        mix_ready = sem("mix_ready")
        mSS, mPP, mPT = W[:, 0:1024], W[:, 1024:2048], E[:, 0:1024]
        qk_normed = sem("qk_normed")

        def sp_bias(sp):
            sp.wait_ge(oh_kept, GH + 1)
            sp.dma_start(onehot, t["onehot"]).then_inc(rel_in, 16)
            sp.dma_start(rel, t["rel_bias"]).then_inc(rel_in, 16)
            sp.wait_ge(rel_kept, 1)
            sp.dma_start(t["scratch_R"], by_dist).then_inc(rel_out, 16)
            sp.wait_ge(rel_out, 16)
            sp.wait_ge(qk_normed, 1)
            R = t["scratch_R"]
            sp.dma_start(B(2, 3072, 2 * P), t["flips"]).then_inc(bias_in, 16)
            for f, first, n in ((0, 0, P), (1, P, T)):
                src = bass.AP(tensor=R.tensor, offset=P - P * f, ap=[[1, P], [512, GH], [1, n]])
                sp.dma_start(bias[:, :, first:first + n], src).then_inc(bias_in, 16)

        def pe_bias(pe):
            pe.wait_ge(rel_in, 32)
            pe.wait_ge(hms_kept, 20)
            nc.tensor.matmul(A(0)[0:GH], rel, onehot, start=True, stop=True).then_inc(rel_ready, 1)

        def act_bias(act):
            act.wait_ge(rel_ready, 1)
            nc.scalar.copy(by_dist, A(0)[0:GH]).then_inc(rel_kept, 1)

        def act_qkb(act):
            act.wait_ge(head_done, GH + 1)
            drain_to(act, "qkb", tiles(B(0)))

            def body(i, k):
                s = product_ready(act, "vb", i, k)
                nc.scalar.copy(vb_row[:, :, SLOT_COLS * k:SLOT_COLS * k + SLOT_COLS],
                               bank[s][:].rearrange("p (t n) -> p t n", t=TT)).then_inc(slot_free[s], 1)
            steps(act, "vb", body)

        def dve_qkb(dve):
            v = nc.vector
            dve.wait_ge(hms_kept, 20)
            v.reciprocal(B(2), B(2))
            dve.drain()
            for k, name in ((0, "q_norm"), (1, "k_norm")):
                r = B(0, 2048 * k, 2048)
                v.scalar_tensor_tensor(r, r, col(name), B(2, 2048 * k, 2048), ALU.mult, ALU.mult)
            dve.drain().then_inc(qk_normed, 1)
            v.tensor_scalar(B(0, 0, 2048), B(0, 0, 2048), SCALE, None, ALU.mult)
            dve.wait_ge(bias_in, 48)
            v.tensor_tensor(bias[:, :, 0:P], bias[:, :, 0:P], rep(causal_flip, GH), ALU.add)
            v.tensor_tensor(bias[:, :, 2 * P:3 * P], bias[:, :, 2 * P:3 * P], rep(causal_flip, GH), ALU.add)
            dve.drain().then_inc(qkb_ready, 1)

        MB = [(g, f) for g in range(2) for f in range(TT)]
        MB0 = ATT * KV

        def act_moba(act):
            for u, (g, f) in enumerate(MB):
                nk = P * (f + 1)
                act.wait_ge(s_shifted, MB0 + u + 1)
                nc.scalar.activation(mPP[:, 0:4 * nk], mSS[:, 0:4 * nk], ACT.Exp).then_inc(e_ready, 1)
                act.wait_ge(pT_ready, MB0 + u + 1)
                nc.scalar.copy(mPT[:, 0:512 * (f + 1)], aux[:, 1024:1024 + 512 * (f + 1)]).then_inc(pT_kept, 1)
                s = product_ready(act, "gb2", 0, u)
                nc.scalar.activation(gb_all[:, 8 + 2 * u:10 + 2 * u, :], bank[s][:].rearrange("p (f n) -> p f n", f=2),
                                     ACT.Sigmoid).then_inc(slot_free[s], 1)

        def pe_moba(pe):
            pe.wait_ge(qkb_ready, 1)
            q3, k3 = tiles(B(0, 0, 2048)), tiles(B(0, 2048, 2048))
            for u, (g, f) in enumerate(MB):
                nk = P * (f + 1)
                for h in range(4):
                    nc.tensor.matmul(aux[:, nk * h:nk * h + nk], q3[:, 4 * g + h, P * f:P * f + P],
                                     k3[:, 4 * g + h, 0:nk], start=True, stop=False)
                    last = nc.tensor.matmul(aux[:, nk * h:nk * h + nk], flip,
                                            bias[:, 4 * g + h, P * f:P * f + nk], start=False, stop=True)
                last.then_inc(s_ready, 1)
                gate = slot_ready(pe, "gb2", 0, u)
                dense_piece(gate, hT, 0, 20)
                pe.wait_ge(p_ready, MB0 + u + 1)
                pe.wait_ge(o_used, MB0 + u + 1)
                for kt in range(f + 1):
                    for h in range(4):
                        at = nk * h + P * kt
                        last = nc.tensor.transpose(A(2 + kt, P * h, P), mPP[:, at:at + P], ident)
                last.then_inc(pT_ready, 1)
                dense_piece(gate, hT, 20, 12)
                pe.wait_ge(pT_kept, MB0 + u + 1)
                for h in range(4):
                    hh = 4 * g + h
                    for kt in range(f + 1):
                        last = nc.tensor.matmul(A(2, P * h, P), vb_row[:, kt, P * hh:P * hh + P],
                                                mPT[:, 512 * kt + P * h:512 * kt + P * h + P], start=kt == 0, stop=kt == f)
                last.then_inc(o_ready, 1)

        def dve_moba(dve):
            v = nc.vector
            for u, (g, f) in enumerate(MB):
                nk = P * (f + 1)
                s3 = mSS[:, 0:4 * nk].rearrange("p (h n) -> p h n", h=4)
                p3 = mPP[:, 0:4 * nk].rearrange("p (h n) -> p h n", h=4)
                dve.wait_ge(s_ready, MB0 + u + 1)
                scores = aux[:, 0:4 * nk].rearrange("p (h n) -> p h n", h=4)
                v.reduce_max(mx, scores, AX_X)
                dve.drain()
                v.tensor_tensor(s3, scores, bc(mx, nk), ALU.subtract).then_inc(s_shifted, 1)
                dve.wait_ge(e_ready, MB0 + u + 1)
                v.reduce_sum(rc, p3, AX_X)
                dve.drain()
                v.reciprocal(rc, rc)
                dve.drain()
                v.tensor_tensor(p3, p3, bc(rc, nk), ALU.mult).then_inc(p_ready, 1)
                dve.wait_ge(o_ready, MB0 + u + 1)
                v.tensor_copy(yb_all[:, 4 * g:4 * g + 4, P * f:P * f + P],
                              A(2).rearrange("p (h n) -> p h n", h=4)).then_inc(o_used, 1)

        def dve_mix(dve):
            v = nc.vector
            wait_drained(dve, "bra")
            v.tensor_tensor(B(0), B(0), B(5), ALU.mult)
            wait_drained(dve, "brb")
            v.tensor_tensor(B(2), B(2), B(3), ALU.mult)
            dve.drain()
            v.tensor_tensor(B(0), B(0), B(2), ALU.add).then_inc(mix_ready, 1)

        gate_all = arena[:, 0:FF * 2].rearrange("p (j n) -> p j n", n=T)
        up_all = arena[:, FF * 2:FF * 4].rearrange("p (j n) -> p j n", n=T)
        ffn_ready = sem("ffn_ready")

        def halves(w):
            view = w.rearrange("(a j p) n -> a p j n", a=2, p=P)

            def src(i, k):
                at = P * (k // 2)
                at = ds(2 * P * i + at, P)
                return (lambda slot: slot[:, 0:KF // 2 * P].rearrange("p (j n) -> p j n", n=P)), view[k % 2][:, :, at]
            return src

        def pe_down(pe):
            pe.wait_ge(ffn_ready, 1)
            with pe.Fori(0, COUNT["down"] // 4) as i:
                for f in range(2):
                    own = BASE["down"] + 2 * f + 1
                    wait_free(pe, own, i)
                    for a in range(2):
                        n = BASE["down"] + 2 * f + a
                        wait_landed(pe, n, i)
                        w = ring[:, n % RING, 0:KF // 2 * P].rearrange("p (j n) -> p j n", n=P)
                        for j in range(KF // 2):
                            last = nc.tensor.matmul(bank[own % RING][:, 0:T], w[:, j, :],
                                                    gate_all[:, KF // 2 * a + j, :],
                                                    start=a == 0 and j == 0, stop=a == 1 and j == KF // 2 - 1)
                        last.then_inc(products if a else slot_free[n % RING], 1)

        def act_down(act):
            with act.Fori(0, COUNT["down"] // 4) as i:
                for f in range(2):
                    own = (BASE["down"] + 2 * f + 1) % RING
                    loop_wait(act, products, 2 * i + PBASE["down"] + f + 1)
                    nc.scalar.copy(hT[:, ds(2 * i + f, 1), :],
                                   bank[own][:, 0:T].rearrange("p (o n) -> p o n", o=1)).then_inc(slot_free[own], 1)

        def dve_down(dve):
            with dve.Fori(0, COUNT["down"] // 4) as i:
                for f in range(2):
                    n = BASE["down"] + 2 * f + 1
                    dve.wait_ge(slot_free[n % RING], i + n // RING + 2)
                    at = ds(2 * i + f, 1)
                    nc.vector.tensor_tensor(xT[:, at, :], xT[:, at, :], hT[:, at, :], ALU.add)
                    dve.drain().then_inc(x_ready, 1)

        def dve_ffn(dve):
            wait_drained(dve, "up")
            for k in range(4):
                n = FF * 2 // 4
                last = nc.vector.tensor_tensor(arena[:, n * k:n * k + n], arena[:, n * k:n * k + n],
                                               arena[:, FF * 2 + n * k:FF * 2 + n * k + n], ALU.mult)
            last.then_inc(ffn_ready, 1)

        locals_of = dict(arena=arena, E=E, W=W, hT=hT, xT=xT, mod=mod, small=small, rstd=rstd)

        block = ctx.enter_context(nc.Block())

        @block.sync
        def _(sp):
            sp_params(sp)
            sp_ssm_loads(sp)
            if stages >= 1:
                mod_cols = cols_of(t["mod_w"])
                stream_mod0(sp, mod_cols)
                stream_mixed(sp, "u", cols_of(t["ssm_w_in"]), mod_cols)
                stream_mixed(sp, "z", cols_of(t["ssm_w_in"], D), mod_cols)
                stream_mixed(sp, "glu", cols_of(t["ssm_w_glu"]), mod_cols)
                stream(sp, "out", cols_of(t["ssm_w_out"]))
            if stages >= 2:
                stream(sp, "kv", cols_of(t["w_kv"]))
                stream(sp, "kvrow", cols_of(t["w_kv"], 2048))
                w1 = t["cmp_w1"].rearrange("k (l d) h -> k d l h", d=P)
                stream(sp, "cmp", lambda i, k: ((lambda slot: slot.rearrange("p (l h) -> p l h", h=P)), w1[k]))
                stream(sp, "q", cols_of(t["w_qg"]))
                stream(sp, "zc", cols_of(t["w_qg"], D + 48))
                stream(sp, "zs", zs_cols(t["w_qg"]))
                stream(sp, "o", cols_of(t["w_o"]))
            if stages >= 3:
                stream(sp, "gdn", cols_of(t["w_in_2"]))
                stream(sp, "za", cols_of(t["w_in_2"], 3072))
                sp_solve(sp)
                stream(sp, "qkb", cols_of(t["w_in_2"], 4112))
                stream(sp, "vb", cols_of(t["w_in_2"], 6160))
                sp_solved(sp)
                stream(sp, "ga", cols_of(t["w_in_2"], 7184))
                stream(sp, "gb", cols_of(t["w_in_2"], 9232))
                sp_bias(sp)
                stream(sp, "gb2", cols_of(t["w_in_2"], 9232 + D // 2))
                stream(sp, "bra", cols_of(t["w_branch_gdn"], 0, 8))
                stream(sp, "brb", cols_of(t["w_branch_moba"], 0, 8))
                stream(sp, "out2", cols_of(t["w_out_2"]))
            if stages >= 5:
                stream(sp, "gate", cols_of(t["w_ffn_gate"]))
                stream(sp, "up", cols_of(t["w_ffn_up"]))
                stream(sp, "down", halves(t["w_ffn_down"]))
            for q in range(4):
                at = slice(QUARTER * q, QUARTER * q + QUARTER)
                sp.wait_ge(x_ready, 1 + 3 * 8 + QUARTER * (q + 1) if stages >= 5 else 9 if stages < 2 else 17)
                sp.dma_start(t["out"][:, at, :], xT[:, at, :]).then_inc(stored, 16)
            if dump:
                for name, ap in dump(locals_of).items():
                    sp.dma_start(t[name], ap).then_inc(stored, 16)
            sp.wait_ge(stored, 16 * (4 + (len(dump(locals_of)) if dump else 0)))

        @block.tensor
        def _(pe):
            if stages >= 1:
                pe_mean_square(pe, B(1))
                pe_mod0(pe)
                dense(pe, "u", hT, ready=(h_ready, 0))
                dense(pe, "z", hT)
                pe_ssm(pe)
                pe.wait_ge(y_kept, SBLOCKS + 1)
                dense(pe, "glu", u_all)
                pe.wait_ge(glu_ready, 4)
                pe_residual(pe, "out", tiles(B(2)))
            if stages >= 2:
                dense(pe, "kv", tiles(B(0)), ready=(h_ready, 4))
                dense_rows(pe, "kvrow", tiles(B(0)))
                pe_cmp(pe)
                dense(pe, "q", hT, ready=(h_ready, 8))
                pe_gates(pe)
                dense(pe, "zc", hT)
                pe_attend(pe)
                pe.wait_ge(att_ready, 1)
                pe_residual(pe, "o", tiles(B(1)))
            if stages >= 3:
                dense(pe, "gdn", hT, ready=(h_ready, 12))
                dense(pe, "za", hT)
                pe_beta(pe)
                pe_head_squares(pe, 0, B(0), 8)
                pe_beta_sums(pe)
                pe_heads(pe)
                dense(pe, "qkb", hT)
                dense_rows(pe, "vb", hT)
                pe_scan(pe)
                pe_head_squares(pe, 1, o_sq, 4)
                pe_head_squares(pe, 2, B(2), 8)
                pe_bias(pe)
                dense(pe, "gb", hT)
                pe_moba(pe)
                pe.wait_ge(ya_ready, 1)
                dense(pe, "bra", o_all, 8)
                pe.wait_ge(o_used, MB0 + len(MB) + 1)
                dense(pe, "brb", yb_all, 8)
                pe.wait_ge(mix_ready, 1)
                pe_residual(pe, "out2", tiles(B(0)))
            if stages >= 5:
                dense(pe, "gate", hT, ready=(h_ready, 16))
                dense(pe, "up", hT)
                pe_down(pe)

        @block.scalar
        def _(act):
            act_start(act)
            if stages >= 1:
                act_ssm_params(act)
                act_mean_square(act, B(1))
                act_ssm_transposed(act)
                drain_to(act, "u", u_all)
                drain_to(act, "z", z_all, ACT.Silu)
                act.nop().then_inc(y_kept, 1)
                act_ssm(act)
                act_glu(act)
                act_residual(act, "out", tiles(B(3)), 1)
            if stages >= 2:
                act_kv(act)
                act_cmp(act)
                drain_to(act, "q", q_all, ACT.Copy, SCALE)
                act_gates(act)
                drain_to(act, "zc", zn, ACT.Silu)
                act_attend(act)
                act_residual(act, "o", tiles(B(2)), 2)
            if stages >= 3:
                act_final0(act)
                drain_to(act, "gdn", raw)
                drain_to(act, "za", za, ACT.Silu)
                act_beta(act)
                act_conv(act)
                act_head_roots(act, 0, B(4), 8, 1.0)
                act_beta_sums(act)
                act_heads(act)
                act_qkb(act)
                act_scan(act)
                act_ya(act)
                act_head_roots(act, 2, B(2), 8, 1.0 / DH)
                act_bias(act)
                drain_to(act, "gb", gb_all, ACT.Sigmoid)
                act_moba(act)
                drain_to(act, "bra", tiles(B(0)))
                drain_to(act, "brb", tiles(B(2)))
                act_residual(act, "out2", tiles(B(2)), 3)
            if stages >= 5:
                drain_to(act, "gate", gate_all, ACT.Silu)
                drain_to(act, "up", up_all)
                act_down(act)

        @block.gpsimd
        def _(pool):
            if stages >= 1:
                pool_spread(pool)
                pool_ssm(pool)
                pool_glu(pool)

        @block.vector
        def _(dve):
            dve_start(dve)
            if stages >= 1:
                dve_ssm_params(dve)
                dve.wait_ge(c_ready, 1)
                dve_rstd(dve, 0)
                dve_mods(dve, "mod0")
                dve_norm0(dve)
                dve_mods(dve, "u")
                dve_mods(dve, "z")
                dve_ssm(dve)
                dve_mods(dve, "glu")
                dve_glu(dve)
                dve_residual(dve, "out", tiles(B(3)), GT0)
            if stages >= 2:
                dve_norm1(dve)
                dve_cmp_in(dve)
                dve_cmp(dve)
                dve_attend(dve)
                dve_residual(dve, "o", tiles(B(2)), GT1)
            if stages >= 3:
                dve_final0(dve)
                dve_conv(dve)
                dve_beta(dve)
                dve_qk(dve)
                dve_beta_sums(dve)
                dve_heads(dve)
                dve_solve(dve)
                dve_scan(dve)
                dve_ya(dve)
                dve_qkb(dve)
                dve_moba(dve)
                dve_mix(dve)
                dve_residual(dve, "out2", tiles(B(2)), None)
            if stages >= 5:
                dve_rstd(dve, 4)
                dve_modulated(dve, hT[:], col("ffn_g"), None, None)
                dve_ffn(dve)
                dve_down(dve)


def constants():
    i = np.arange(P)
    con = {
        "ident": np.eye(P),
        "causal": np.concatenate([np.zeros((P, P)), np.where(i[None, :] <= i[:, None], 0, NEG)], 1),
        "cum": (i[:, None] // CH == i[None, :] // CH) & (i[:, None] <= i[None, :]),
        "same": i[:, None] // CH == i[None, :] // CH,
        "decay_neg": np.where((i[:, None] // CH == i[None, :] // CH) & (i[:, None] <= i[None, :]), 0, NEG),
        "strict": i[:, None] % CH < np.arange(CH)[None, :],
    }
    tok = np.arange(TT)[None, :, None] * P + i[:, None, None]
    seen = (np.arange(NCMP) * CMP_STRIDE + CMP_LEN - 1)[None, None, :] <= tok
    con["cmp_neg"] = np.where(seen, 0, NEG).reshape(P, -1)
    con["cmp_one"] = seen.reshape(P, -1)
    flips = np.concatenate([con["ident"][::-1], con["causal"][::-1, P:]], 1).astype(np.float32)
    con["iota"] = np.broadcast_to(np.arange(T), (P, T))
    con = np.concatenate([np.asarray(con[n], np.float32) for n, _ in CONSTS], 1)
    eye = np.zeros((P, 16, CH), np.float32)
    for p in range(P):
        for c in range(16):
            eye[p, c, 16 * (p % 4) + c] = 1
    dist = np.maximum(T - 1 - np.arange(512), 0)
    d = dist.astype(np.float32)
    ratio = np.log(np.maximum(d, np.float32(16)) / np.float32(16)) / np.float32(math.log(2048 / 16))
    large = np.minimum(16 + (ratio * np.float32(16)).astype(np.int32), 31)
    bucket = np.where(dist < 16, dist, large)
    onehot = (np.arange(32)[:, None] == bucket[None, :]).astype(np.float32)
    return np.ascontiguousarray(con), eye, onehot, flips


def lay_out(x):
    x = {k: np.asarray(v) for k, v in x.items()}

    def feat(v):
        return v.reshape(-1, P).T

    def states(v):
        return v[0].reshape(STILES, P, *v.shape[3:]).swapaxes(0, 1)

    packed = {
        "c": feat(x["c"]), "norm_g": feat(x["norm_g"]),
        "mod_b": feat(np.concatenate([x["mod_b"][0], x["kv_mod_b"], x["mod_b"][1]])),
        "kv_norm_g": feat(x["kv_norm_g"]), "ssm_d": feat(x["ssm_d"]), "b_glu": feat(x["ssm_b_glu"]),
        "final_g": feat(x["final_norm_g"]), "mix_g": feat(x["norm_mix_w_2"]), "ffn_g": feat(x["norm_ffn_w_2"]),
        "conv_w": x["conv_w_2"][0].reshape(4, 24, P).transpose(2, 1, 0).reshape(P, 96),
        "q_norm": feat(x["q_norm_w_2"]), "k_norm": feat(x["k_norm_w_2"]), "o_norm": feat(x["gdn_o_norm_w_2"]),
        "cmp_b1": x["cmp_b1"].T, "cmp_b2": x["cmp_b2"].T,
        "pe": x["cmp_pe"].transpose(2, 0, 1).reshape(P, 64),
        "lam_re": states(x["ssm_lam_re"]), "lam_im": states(x["ssm_lam_im"]),
    }
    con, eye, onehot, flips = constants()
    w_qg, w_in = x["nsa_w_qg"][0], x["w_in_2"][0]
    kv = x["w_kv"].reshape(D, 6, 512)[:, [0, 1, 2, 4, 3, 5]].reshape(D, 3072)

    def c_states(v):
        return v[0].swapaxes(1, 2).reshape(STILES, P, CG).swapaxes(0, 1).reshape(P, 1024)

    out = {
        "cols": np.concatenate([packed[n] for n, _ in COLS], 1), "con": con, "eye": eye, "onehot": onehot, "flips": flips,
        "xT": x["x"][0].T.reshape(KD, P, T).swapaxes(0, 1),
        "w_gate": w_qg[:, D:D + 48], "w_beta": w_in[:, 4096:4112],
        "cmp_w2": x["cmp_w2"], "cmp_b2v": x["cmp_b2"][1:2],
        "gdn_rows": np.concatenate([x["a_log_2"], x["dt_bias_2"]], 1),
        "log_step": x["ssm_log_step"][0].reshape(STILES, 2).T,
        "mod_w": np.concatenate([x["mod_w"][0], x["kv_mod_w"], x["mod_w"][1]], 1),
        "ssm_w_in": x["ssm_w_in"][0], "ssm_w_glu": x["ssm_w_glu"][0], "ssm_w_out": x["ssm_w_out"][0],
        "b_re": states(x["ssm_b_re"]).reshape(P, 1024), "b_im": states(x["ssm_b_im"]).reshape(P, 1024),
        "ssm_c_re": c_states(x["ssm_c_re"]), "ssm_c_im": c_states(x["ssm_c_im"]),
        "w_kv": kv, "cmp_w1": x["cmp_w1"], "w_qg": w_qg, "w_o": x["nsa_w_o"][0], "w_in_2": w_in,
        "rel_bias": x["rel_bias_2"], "w_branch_gdn": x["w_branch_gdn_2"][0], "w_branch_moba": x["w_branch_moba_2"][0],
        "w_out_2": x["w_out_2"][0], "w_ffn_gate": x["w_ffn_gate_2"][0], "w_ffn_up": x["w_ffn_up_2"][0],
        "w_ffn_down": x["w_ffn_down_2"][0],
    }
    return {k: np.ascontiguousarray(v) for k, v in out.items()}


SCRATCH = {"scratch_L": (GH, NCH, CH, CH), "scratch_T": (GH, NCH, CH, CH), "scratch_R": (GH, 512)}


def program(nc, arrays, stages=99, dump=None, extra=()):
    t = {n: nc.dram_tensor("in_" + n, a.shape, F32, kind="ExternalInput").ap() for n, a in arrays.items()}
    t |= {n: nc.dram_tensor(n, s, F32, kind="Internal").ap() for n, s in SCRATCH.items()}
    t["out"] = nc.dram_tensor("out_0", (P, KD, T), F32, kind="ExternalOutput").ap()
    for n, s in extra:
        t[n] = nc.dram_tensor(n, s, F32, kind="ExternalOutput").ap()
    build(nc, t, stages, dump)


def kernel(**inputs):
    import concourse.bacc as bacc
    from concourse.bass_utils import run_bass_kernel_spmd

    nc = bacc.Bacc("TRN2", target_bir_lowering=False, num_devices=1, dynamic_dma_scratch_size=DMA_SCRATCH)
    arrays = lay_out(inputs)
    program(nc, arrays)
    got = run_bass_kernel_spmd(nc, [{"in_" + n: a for n, a in arrays.items()}], core_ids=[0])
    out = got.results[0]["out_0"]
    return np.ascontiguousarray(out.transpose(2, 1, 0).reshape(1, T, D))
```
